# Optimizing a Trainium2 kernel written in Bass

```python
import jax
import jax.numpy as jnp
from jax import lax
import numpy as np

D_MODEL = 1024
BATCH = 1
SEQ = 1024
DEPTH = 1
DEC_BATCH = 8
DEC_SEQ = 1
PAST_LEN = 2048
PAGE_SIZE = 128

HEAD_DIM = 64
GLA_HEADS = 4
GLA_LOWRANK = 16
GLA_TAU = 16.0
GLA_CHUNK = 64
NSA_HEADS = 8
NSA_KV_HEADS = 2
NSA_GROUP = NSA_HEADS // NSA_KV_HEADS
CMP_BLOCK = 32
CMP_STRIDE = 16
CMP_HIDDEN = 64
SEL_BLOCK = 64
SEL_RATIO = SEL_BLOCK // CMP_STRIDE
SEL_TOPK = 16
WINDOW = 512
NSA_QBLOCK = 128
FORCE_SCORE = 1.0e4
MLSTM_HEADS = 4
MLSTM_CHUNK = 64
CONV_WIDTH = 4
D_FF = 4 * D_MODEL
EPS = 1e-6

GLA_W = GLA_HEADS * HEAD_DIM
NSA_W = NSA_HEADS * HEAD_DIM
KV_W = NSA_KV_HEADS * HEAD_DIM
MLSTM_W = MLSTM_HEADS * HEAD_DIM
MIX_W = GLA_W + NSA_W + MLSTM_W
IN_SPLITS = (GLA_W, GLA_W, GLA_W, GLA_W, GLA_LOWRANK,
             NSA_W, KV_W, KV_W, KV_W, KV_W, KV_W, KV_W, 3 * NSA_HEADS,
             MLSTM_W, MLSTM_W, MLSTM_HEADS, MLSTM_HEADS, MLSTM_W)
IN_W = sum(IN_SPLITS)

kernel_name = 'hybrid_gla_nsa_mlstm_step'

def split_points():
    return tuple(int(p) for p in np.cumsum(np.array(IN_SPLITS))[:-1])

def rmsnorm(x, g):
    xf = x.astype(jnp.float32)
    y = xf * lax.rsqrt(jnp.mean(xf * xf, axis=-1, keepdims=True) + EPS)
    return (y * g.astype(jnp.float32)).astype(x.dtype)

def masked_softmax(s, mask):
    s = jnp.where(mask, s, -jnp.inf)
    m = jnp.max(s, axis=-1, keepdims=True)
    m = jnp.where(jnp.isfinite(m), m, 0.0)
    e = jnp.exp(s - m)
    return e / jnp.maximum(jnp.sum(e, axis=-1, keepdims=True), 1e-30)

def to_chunks(a, c, pad_value=0.0):
    b, t = a.shape[0], a.shape[1]
    n = -(-t // c)
    widths = [(0, 0), (0, n * c - t)] + [(0, 0)] * (a.ndim - 2)
    a = jnp.pad(a, widths, constant_values=pad_value)
    a = a.reshape((b, n, c) + a.shape[2:])
    return jnp.swapaxes(jnp.moveaxis(a, 1, 0), 2, 3)

def from_chunks(o, t):
    n, b, h, c = o.shape[:4]
    o = jnp.moveaxis(jnp.swapaxes(o, 2, 3), 0, 1)
    return o.reshape((b, n * c, h) + o.shape[4:])[:, :t]

def gla_scan(q, k, v, log_a, s0):
    f32 = jnp.float32
    t = q.shape[1]
    c = min(GLA_CHUNK, t)
    causal = jnp.tril(jnp.ones((c, c), dtype=bool))
    xs = (to_chunks(q.astype(f32), c), to_chunks(k.astype(f32), c),
          to_chunks(v.astype(f32), c), to_chunks(log_a.astype(f32), c))

    def step(s, inp):
        qc, kc, vc, gc = inp
        bcum = jnp.cumsum(gc, axis=2)
        rel = jnp.where(causal[None, None, :, :, None],
                        bcum[:, :, :, None, :] - bcum[:, :, None, :, :], -jnp.inf)
        scores = jnp.einsum('bhtd,bhsd,bhtsd->bhts', qc, kc, jnp.exp(rel))
        o = (jnp.einsum('bhts,bhse->bhte', scores, vc)
             + jnp.einsum('bhtd,bhde->bhte', qc * jnp.exp(bcum), s))
        b_end = bcum[:, :, -1:, :]
        s_new = (jnp.exp(b_end[:, :, 0, :, None]) * s
                 + jnp.einsum('bhsd,bhse->bhde', kc * jnp.exp(b_end - bcum), vc))
        return s_new, o

    s_fin, o = lax.scan(step, s0.astype(f32), xs)
    return from_chunks(o, t), s_fin

def mlstm_scan(q, k, v, i_pre, log_f, c0, n0, m0):
    f32 = jnp.float32
    t = q.shape[1]
    c = min(MLSTM_CHUNK, t)
    causal = jnp.tril(jnp.ones((c, c), dtype=bool))
    xs = (to_chunks(q, c), to_chunks(k, c), to_chunks(v, c),
          to_chunks(i_pre, c, -jnp.inf), to_chunks(log_f, c))

    def step(carry, inp):
        cm, nv, m = carry
        qc, kc, vc, ic, fc = inp
        fcum = jnp.cumsum(fc, axis=-1)
        a = fcum + m[..., None]
        dmat = jnp.where(causal, fcum[..., :, None] - fcum[..., None, :] + ic[..., None, :], -jnp.inf)
        m_t = jnp.maximum(a, jnp.max(dmat, axis=-1))
        w_state = jnp.exp(a - m_t)
        qk = jnp.einsum('bhtd,bhsd->bhts', qc, kc) * jnp.exp(dmat - m_t[..., None])
        num = (jnp.einsum('bhts,bhse->bhte', qk, vc)
               + w_state[..., None] * jnp.einsum('bhtd,bhde->bhte', qc, cm))
        den = jnp.sum(qk, axis=-1) + w_state * jnp.einsum('bhtd,bhd->bht', qc, nv)
        h = num / jnp.maximum(jnp.abs(den), jnp.exp(-m_t))[..., None]
        m_new = m_t[..., -1]
        w_last = jnp.exp(dmat[..., -1, :] - m_new[..., None])
        w_carry = jnp.exp(a[..., -1] - m_new)
        c_new = w_carry[..., None, None] * cm + jnp.einsum('bhs,bhsd,bhse->bhde', w_last, kc, vc)
        n_new = w_carry[..., None] * nv + jnp.einsum('bhs,bhsd->bhd', w_last, kc)
        return (c_new, n_new, m_new), h

    (c_f, n_f, m_f), h = lax.scan(step, (c0.astype(f32), n0.astype(f32), m0.astype(f32)), xs)
    return from_chunks(h, t), c_f, n_f, m_f

def causal_conv(u, buf, w, bias):
    t = u.shape[1]
    up = jnp.concatenate([buf.astype(u.dtype), u], axis=1)
    y = bias
    for j in range(CONV_WIDTH):
        y = y + up[:, j:j + t] * w[j]
    return y, up[:, t:]

def compress_rows(rows, pe, w1, b1, w2, b2):
    f32 = jnp.float32
    b, length, hk, d = rows.shape
    n16 = length // CMP_STRIDE
    r = rows[:, :n16 * CMP_STRIDE].reshape(b, n16, CMP_STRIDE, hk, d).astype(f32)
    pe, w1 = pe.astype(f32), w1.astype(f32)
    hid = (jnp.einsum('bnrhd,rde->bnhe', r[:, :-1] + pe[None, None, :CMP_STRIDE, None, :], w1[:CMP_STRIDE])
           + jnp.einsum('bnrhd,rde->bnhe', r[:, 1:] + pe[None, None, CMP_STRIDE:, None, :], w1[CMP_STRIDE:])
           + b1)
    return jnp.einsum('bnhe,ed->bnhd', jax.nn.silu(hid), w2.astype(f32)) + b2

def nsa_query_block(q, gates, q_pos, k_cmp, v_cmp, k_blk, v_blk, k_win, v_win, w_pos):
    f32 = jnp.float32
    b, tq, hk, g, d = q.shape
    qf = q.astype(f32) * (HEAD_DIM ** -0.5)
    n_c = k_cmp.shape[1]
    c_end = jnp.arange(n_c) * CMP_STRIDE + (CMP_BLOCK - 1)
    p_c = masked_softmax(jnp.einsum('bthgd,bnhd->bhgtn', qf, k_cmp.astype(f32)),
                         c_end[None, :] <= q_pos[:, None])
    o_c = jnp.einsum('bhgtn,bnhd->bthgd', p_c, v_cmp.astype(f32))
    n_s = k_blk.shape[2]
    p_grp = jnp.sum(p_c, axis=2)
    pp = jnp.pad(p_grp, ((0, 0), (0, 0), (0, 0), (1, SEL_RATIO * n_s - n_c)))
    p_sel = (pp[..., 1:] + pp[..., :-1]).reshape(b, hk, tq, n_s, SEL_RATIO).sum(-1)
    blk = jnp.arange(n_s)[None, :]
    cur = (q_pos // SEL_BLOCK)[:, None]
    forced = (blk == 0) | (blk == cur) | (blk == cur - 1)
    score = jnp.where(blk > cur, -1.0, jnp.where(forced, FORCE_SCORE, p_sel))
    n_top = min(SEL_TOPK, n_s)
    _, idx = lax.top_k(score, n_top)
    take = jax.vmap(jax.vmap(lambda blocks, ix: blocks[ix]))
    k_sel = take(k_blk, idx).astype(f32)
    v_sel = take(v_blk, idx).astype(f32)
    s_pos = idx[..., None] * SEL_BLOCK + jnp.arange(SEL_BLOCK)
    s_mask = (s_pos <= q_pos[None, None, :, None, None]).reshape(b, hk, 1, tq, n_top * SEL_BLOCK)
    s_sc = jnp.einsum('bthgd,bhtnsd->bhgtns', qf, k_sel).reshape(b, hk, g, tq, n_top * SEL_BLOCK)
    p_s = masked_softmax(s_sc, s_mask).reshape(b, hk, g, tq, n_top, SEL_BLOCK)
    o_s = jnp.einsum('bhgtns,bhtnsd->bthgd', p_s, v_sel)
    w_mask = ((w_pos[None, :] <= q_pos[:, None]) & (w_pos[None, :] > q_pos[:, None] - WINDOW)
              & (w_pos[None, :] >= 0))
    p_w = masked_softmax(jnp.einsum('bthgd,blhd->bhgtl', qf, k_win.astype(f32)), w_mask)
    o_w = jnp.einsum('bhgtl,blhd->bthgd', p_w, v_win.astype(f32))
    gf = gates.astype(f32)
    return gf[..., 0:1] * o_c + gf[..., 1:2] * o_s + gf[..., 2:3] * o_w

def nsa_attend(q, gates, rows_full, win_all, q0, k_cmp, v_cmp):
    b, t = q.shape[0], q.shape[1]
    length = rows_full.shape[1]
    n_sel = -(-length // SEL_BLOCK)
    sel = jnp.pad(rows_full[:, :, 2:4], ((0, 0), (0, n_sel * SEL_BLOCK - length), (0, 0), (0, 0), (0, 0)))
    sel = sel.reshape((b, n_sel, SEL_BLOCK) + sel.shape[2:]).transpose(3, 0, 4, 1, 2, 5)
    k_blk, v_blk = sel[0], sel[1]
    qb = min(NSA_QBLOCK, t)
    n_qb = -(-t // qb)
    extra = n_qb * qb - t
    pad5 = ((0, 0), (0, extra), (0, 0), (0, 0), (0, 0))
    q_pad = jnp.pad(q, pad5)
    g_pad = jnp.pad(gates, pad5)
    w_pad = jnp.pad(win_all, pad5)

    def one_block(bi):
        start = bi * qb
        q_b = lax.dynamic_slice_in_dim(q_pad, start, qb, axis=1)
        g_b = lax.dynamic_slice_in_dim(g_pad, start, qb, axis=1)
        w_b = lax.dynamic_slice_in_dim(w_pad, start, WINDOW + qb, axis=1)
        q_pos = q0 + start + jnp.arange(qb)
        w_pos = q0 + start - WINDOW + jnp.arange(WINDOW + qb)
        return nsa_query_block(q_b, g_b, q_pos, k_cmp, v_cmp, k_blk, v_blk,
                               w_b[:, :, 0], w_b[:, :, 1], w_pos)

    out = jnp.moveaxis(lax.map(one_block, jnp.arange(n_qb)), 0, 1)
    return out.reshape((b, n_qb * qb) + out.shape[3:])[:, :t]

def token_mixers(h, q0, nsa_past, win_buf, gla_s0, ml_c0, ml_n0, ml_m0, ml_conv0, lp):
    b, t, _ = h.shape
    d = HEAD_DIM
    f32 = jnp.float32
    z = h @ lp['w_in']
    (gq, gk, gv, gr, ga, nq, nkc, nvc, nks, nvs, nkw, nvw, ng,
     mu, mv, mi, mf, mo) = jnp.split(z, split_points(), axis=-1)

    gshape = (b, t, GLA_HEADS, d)
    log_a = jax.nn.log_sigmoid((ga @ lp['gla_a_w'] + lp['gla_a_b']).astype(f32)) / GLA_TAU
    o_g, s_gla = gla_scan(gq.reshape(gshape) * (d ** -0.5), gk.reshape(gshape), gv.reshape(gshape),
                          log_a.reshape(gshape), gla_s0)
    o_g = (rmsnorm(o_g, lp['gla_norm_g']) * jax.nn.silu(gr.reshape(gshape).astype(f32))).reshape(b, t, GLA_W)

    g_qk = lp['nsa_qk_g']
    kv_shape = (b, t, NSA_KV_HEADS, d)
    q = rmsnorm(nq.reshape(b, t, NSA_KV_HEADS, NSA_GROUP, d), g_qk[0])
    new_rows = jnp.stack([nkc.reshape(kv_shape), nvc.reshape(kv_shape),
                          rmsnorm(nks.reshape(kv_shape), g_qk[2]), nvs.reshape(kv_shape)], axis=2)
    new_win = jnp.stack([rmsnorm(nkw.reshape(kv_shape), g_qk[3]), nvw.reshape(kv_shape)], axis=2)
    gates = jax.nn.sigmoid((ng + lp['nsa_gate_b']).astype(f32)).reshape(b, t, NSA_KV_HEADS, NSA_GROUP, 3)
    rows_full = jnp.concatenate([nsa_past.astype(new_rows.dtype), new_rows], axis=1)
    pe, w1, b1, w2, b2 = lp['cmp_pe'], lp['cmp_w1'], lp['cmp_b1'], lp['cmp_w2'], lp['cmp_b2']
    k_cmp = rmsnorm(compress_rows(rows_full[:, :, 0], pe[0], w1[0], b1[0], w2[0], b2[0]), g_qk[1])
    v_cmp = compress_rows(rows_full[:, :, 1], pe[1], w1[1], b1[1], w2[1], b2[1])
    win_cat = jnp.concatenate([win_buf.astype(new_win.dtype), new_win], axis=1)
    win_all = jnp.pad(win_cat, ((0, 0), (WINDOW - win_buf.shape[1], 0), (0, 0), (0, 0), (0, 0)))
    o_n = nsa_attend(q, gates, rows_full, win_all, q0, k_cmp, v_cmp).reshape(b, t, NSA_W)
    win_state = win_cat[:, win_cat.shape[1] - min(WINDOW, q0 + t):]

    u_conv, conv_state = causal_conv(mu, ml_conv0, lp['ml_conv_w'], lp['ml_conv_b'])
    u_act = jax.nn.silu(u_conv.astype(f32))
    u_h = u_act.reshape(b, t, MLSTM_HEADS, d)
    mq = jnp.einsum('bthd,hde->bthe', u_h, lp['ml_wq'].astype(f32))
    mk = jnp.einsum('bthd,hde->bthe', u_h, lp['ml_wk'].astype(f32)) * (d ** -0.5)
    i_pre = (mi + lp['ml_gate_b'][0]).astype(f32)
    log_f = jax.nn.log_sigmoid((mf + lp['ml_gate_b'][1]).astype(f32))
    h_m, c_m, n_m, m_m = mlstm_scan(mq, mk, mv.reshape(b, t, MLSTM_HEADS, d).astype(f32),
                                    i_pre, log_f, ml_c0, ml_n0, ml_m0)
    o_m = jax.nn.sigmoid(mo.astype(f32)) * (rmsnorm(h_m, lp['ml_norm_g']).reshape(b, t, MLSTM_W)
                                            + lp['ml_skip'] * u_act)

    mix = jnp.concatenate([o_g, o_n, o_m], axis=-1).astype(h.dtype)
    return mix, (new_rows, win_state, s_gla, c_m, n_m, m_m, conv_state)

def trunk_layer(x, q0, nsa_past, win_buf, gla_s0, ml_c0, ml_n0, ml_m0, ml_conv0, lp):
    mix, state = token_mixers(rmsnorm(x, lp['norm1_g']), q0, nsa_past, win_buf,
                              gla_s0, ml_c0, ml_n0, ml_m0, ml_conv0, lp)
    x = x + mix @ lp['w_out']
    hid = jax.nn.relu(rmsnorm(x, lp['norm2_g']) @ lp['w_up'])
    x = x + (hid * hid) @ lp['w_down']
    return x, state

def setup_inputs(seed: int = 0) -> dict:
    key = jax.random.key(seed)
    ks = jax.random.split(key, 40)
    f32 = jnp.float32

    def nrm(k, shape, s):
        return jax.random.normal(k, shape, f32) * s

    n_pages = PAST_LEN // PAGE_SIZE
    n_used = DEC_BATCH * n_pages
    n_pool = n_used + n_used // 4
    wb = min(WINDOW, PAST_LEN)
    page_table = jax.random.permutation(ks[0], n_pool)[:n_used].reshape(DEC_BATCH, n_pages).astype(jnp.int32)
    d = HEAD_DIM
    return {
        'x_prompt': nrm(ks[1], (BATCH, SEQ, D_MODEL), 1.0),
        'x_sample': nrm(ks[2], (DEC_BATCH, DEC_SEQ, D_MODEL), 1.0),
        'cache_nsa_kv': nrm(ks[3], (DEPTH, n_pool, PAGE_SIZE, 4, NSA_KV_HEADS, d), 1.0),
        'cache_nsa_win': nrm(ks[4], (DEPTH, DEC_BATCH, wb, 2, NSA_KV_HEADS, d), 1.0),
        'state_gla': nrm(ks[5], (DEPTH, DEC_BATCH, GLA_HEADS, d, d), 0.5),
        'state_mlstm_c': nrm(ks[6], (DEPTH, DEC_BATCH, MLSTM_HEADS, d, d), 0.5),
        'state_mlstm_n': nrm(ks[7], (DEPTH, DEC_BATCH, MLSTM_HEADS, d), 1.0),
        'state_mlstm_m': nrm(ks[8], (DEPTH, DEC_BATCH, MLSTM_HEADS), 1.0),
        'state_mlstm_conv': nrm(ks[9], (DEPTH, DEC_BATCH, CONV_WIDTH - 1, MLSTM_W), 1.0),
        'page_table': page_table,
        'norm1_g': 1.0 + nrm(ks[10], (DEPTH, D_MODEL), 0.1),
        'w_in': nrm(ks[11], (DEPTH, D_MODEL, IN_W), D_MODEL ** -0.5),
        'gla_a_w': nrm(ks[12], (DEPTH, GLA_LOWRANK, GLA_W), GLA_LOWRANK ** -0.5),
        'gla_a_b': nrm(ks[13], (DEPTH, GLA_W), 0.5),
        'gla_norm_g': 1.0 + nrm(ks[14], (DEPTH, d), 0.1),
        'nsa_qk_g': 1.0 + nrm(ks[15], (DEPTH, 4, d), 0.1),
        'nsa_gate_b': nrm(ks[16], (DEPTH, 3 * NSA_HEADS), 0.1),
        'cmp_pe': nrm(ks[17], (DEPTH, 2, CMP_BLOCK, d), 0.1),
        'cmp_w1': nrm(ks[18], (DEPTH, 2, CMP_BLOCK, d, CMP_HIDDEN), (CMP_BLOCK * d) ** -0.5),
        'cmp_b1': nrm(ks[19], (DEPTH, 2, CMP_HIDDEN), 0.01),
        'cmp_w2': nrm(ks[20], (DEPTH, 2, CMP_HIDDEN, d), CMP_HIDDEN ** -0.5),
        'cmp_b2': nrm(ks[21], (DEPTH, 2, d), 0.01),
        'ml_conv_w': nrm(ks[22], (DEPTH, CONV_WIDTH, MLSTM_W), CONV_WIDTH ** -0.5),
        'ml_conv_b': nrm(ks[23], (DEPTH, MLSTM_W), 0.01),
        'ml_wq': nrm(ks[24], (DEPTH, MLSTM_HEADS, d, d), d ** -0.5),
        'ml_wk': nrm(ks[25], (DEPTH, MLSTM_HEADS, d, d), d ** -0.5),
        'ml_gate_b': jnp.stack([nrm(ks[26], (DEPTH, MLSTM_HEADS), 0.1),
                                3.0 + nrm(ks[27], (DEPTH, MLSTM_HEADS), 0.5)], axis=1),
        'ml_norm_g': 1.0 + nrm(ks[28], (DEPTH, d), 0.1),
        'ml_skip': 1.0 + nrm(ks[29], (DEPTH, MLSTM_W), 0.1),
        'w_out': nrm(ks[30], (DEPTH, MIX_W, D_MODEL), MIX_W ** -0.5),
        'norm2_g': 1.0 + nrm(ks[31], (DEPTH, D_MODEL), 0.1),
        'w_up': nrm(ks[32], (DEPTH, D_MODEL, D_FF), D_MODEL ** -0.5),
        'w_down': nrm(ks[33], (DEPTH, D_FF, D_MODEL), D_FF ** -0.5),
    }

def reference(x_prompt, x_sample, cache_nsa_kv, cache_nsa_win, state_gla, state_mlstm_c, state_mlstm_n,
              state_mlstm_m, state_mlstm_conv, page_table, norm1_g, w_in, gla_a_w, gla_a_b, gla_norm_g,
              nsa_qk_g, nsa_gate_b, cmp_pe, cmp_w1, cmp_b1, cmp_w2, cmp_b2, ml_conv_w, ml_conv_b, ml_wq, ml_wk,
              ml_gate_b, ml_norm_g, ml_skip, w_out, norm2_g, w_up, w_down):
    f32 = jnp.float32
    d = HEAD_DIM
    bp = x_prompt.shape[0]
    n_dec = x_sample.shape[0]
    past = page_table.shape[1] * PAGE_SIZE
    dt = x_prompt.dtype
    empty_rows = jnp.zeros((bp, 0, 4, NSA_KV_HEADS, d), dt)
    empty_win = jnp.zeros((bp, 0, 2, NSA_KV_HEADS, d), dt)
    gla0 = jnp.zeros((bp, GLA_HEADS, d, d), f32)
    c0 = jnp.zeros((bp, MLSTM_HEADS, d, d), f32)
    n0 = jnp.zeros((bp, MLSTM_HEADS, d), f32)
    m0 = jnp.zeros((bp, MLSTM_HEADS), f32)
    conv0 = jnp.zeros((bp, CONV_WIDTH - 1, MLSTM_W), dt)
    x_p, x_s = x_prompt, x_sample
    states_p, states_s = [], []
    for l in range(DEPTH):
        lp = {'norm1_g': norm1_g[l], 'w_in': w_in[l], 'gla_a_w': gla_a_w[l], 'gla_a_b': gla_a_b[l],
              'gla_norm_g': gla_norm_g[l], 'nsa_qk_g': nsa_qk_g[l], 'nsa_gate_b': nsa_gate_b[l],
              'cmp_pe': cmp_pe[l], 'cmp_w1': cmp_w1[l], 'cmp_b1': cmp_b1[l], 'cmp_w2': cmp_w2[l],
              'cmp_b2': cmp_b2[l], 'ml_conv_w': ml_conv_w[l], 'ml_conv_b': ml_conv_b[l], 'ml_wq': ml_wq[l],
              'ml_wk': ml_wk[l], 'ml_gate_b': ml_gate_b[l], 'ml_norm_g': ml_norm_g[l], 'ml_skip': ml_skip[l],
              'w_out': w_out[l], 'norm2_g': norm2_g[l], 'w_up': w_up[l], 'w_down': w_down[l]}
        nsa_past = cache_nsa_kv[l][page_table].reshape((n_dec, past) + cache_nsa_kv.shape[3:])
        x_p, st_p = trunk_layer(x_p, 0, empty_rows, empty_win, gla0, c0, n0, m0, conv0, lp)
        x_s, st_s = trunk_layer(x_s, past, nsa_past, cache_nsa_win[l], state_gla[l], state_mlstm_c[l],
                                state_mlstm_n[l], state_mlstm_m[l], state_mlstm_conv[l], lp)
        states_p.append(st_p)
        states_s.append(st_s)
    nsa_rows_p = jnp.stack([s[0] for s in states_p])
    nsa_rows_s = jnp.stack([s[0] for s in states_s])
    win_p = jnp.stack([s[1] for s in states_p])
    win_s = jnp.stack([s[1] for s in states_s])
    gla_p = jnp.stack([s[2] for s in states_p])
    gla_s = jnp.stack([s[2] for s in states_s])
    mc_p = jnp.stack([s[3] for s in states_p])
    mc_s = jnp.stack([s[3] for s in states_s])
    mn_p = jnp.stack([s[4] for s in states_p])
    mn_s = jnp.stack([s[4] for s in states_s])
    mm_p = jnp.stack([s[5] for s in states_p])
    mm_s = jnp.stack([s[5] for s in states_s])
    conv_p = jnp.stack([s[6] for s in states_p])
    conv_s = jnp.stack([s[6] for s in states_s])
    return (x_p, x_s, nsa_rows_p, nsa_rows_s, win_p, win_s, gla_p, gla_s, mc_p, mc_s, mn_p, mn_s,
            mm_p, mm_s, conv_p, conv_s)


_drawn_inputs = setup_inputs


def setup_inputs(seed=0):
    import zlib

    import numpy as np

    out = dict(_drawn_inputs(seed))
    spreads = {}
    factors = {'nsa_gate_b': 8.0,
     'cmp_pe': 3.227,
     'cmp_b1': 33.269,
     'cmp_b2': 8.0,
     'ml_conv_b': 3.079,
     'ml_skip': 3.851}
    for name, (base, spread) in spreads.items():
        noise = np.random.default_rng([zlib.crc32(name.encode()), seed]).standard_normal(out[name].shape)
        drawn = base * np.exp(spread * noise) if base else spread * noise
        out[name] = jnp.asarray(drawn.astype(out[name].dtype))
    for name, factor in factors.items():
        out[name] = (out[name] * factor).astype(out[name].dtype)
    return out
```

```python
import concourse.bass as bass
from concourse import mybir
from contextlib import ExitStack

F32 = mybir.dt.float32
F32R = mybir.dt.float32r
U32 = mybir.dt.uint32
I32 = mybir.dt.int32
ACT = mybir.ActivationFunctionType
ALU = mybir.AluOpType
AX = mybir.AxisListType
ds = bass.ds

P = 128
D = 1024
T = 1024
NS = 8
TT = T + NS
NT = 3
TC = TT // NT
KD = D // P
TQ = T // P
HD = 64
IN_W = 3120
EPS = 1e-6


def tiles(eng, n, unroll):
    with eng.Fori(0, n // unroll) as it:
        for slot in range(unroll):
            yield it * unroll + slot, slot


def semaphores(nc, ctx, stage):
    held = []

    def give_back():
        nc.clear_and_free_semaphores(held)
        nc.all_engine_barrier()

    ctx.callback(give_back)

    def sem(name):
        held.append(nc.alloc_semaphore(f"{stage}_{name}"))
        return held[-1]

    return sem


def split_product(nc, out, weights, moving):
    n = len(weights)
    for k, ((wH, wL), (mH, mL)) in enumerate(zip(weights, moving)):
        nc.tensor.matmul(out, wH, mH, start=(k == 0), stop=False)
        nc.tensor.matmul(out, wH, mL, start=False, stop=False)
        last = nc.tensor.matmul(out, wL, mH, start=False, stop=(k == n - 1))
    return last


def norm_and_project(nc, io, keep):
    x_p = io["x_prompt"].rearrange("b t d -> (b t) d")
    x_s = io["x_sample"].rearrange("b t d -> (b t) d")
    w_in = io["w_in"].rearrange("l d n -> (l d) n").rearrange("(k p) n -> p k n", p=P)
    zT, zS = io["zT"], io["zS"]
    ident = keep["ident"]
    NM = IN_W // P
    MR = IN_W - NM * P
    with ExitStack() as ctx:
        sb = lambda n, s, d=F32: ctx.enter_context(nc.sbuf_tensor(n, s, d))
        sem = semaphores(nc, ctx, "project")
        hT = sb("hT", [P, KD, TT])
        xT = sb("xT", [P, KD, TT])
        xin = sb("xin", [P, 2, D])
        xn = sb("xn", [P, 2, D])
        sq = sb("sq", [P, D])
        ss = sb("ss", [P, 2])
        rms = sb("rms", [P, 2])
        rstd = sb("rstd", [P, 2])
        eps = sb("eps1", [P, 1])
        g1 = sb("g1", [P, KD])
        win = sb("win", [P, 2, KD, P])
        z = sb("z", [P, 2, TT])
        zs = sb("zs", [NS, IN_W])
        ps = [ctx.enter_context(nc.psum_tensor(f"pa{i}", [P, 512], F32)) for i in range(8)]

        x_in = [sem(f"x_in{i}") for i in range(2)]
        x_used = sem("x_used")
        ss_ready, rms_ready, xn_ready = sem("ss_ready"), sem("rms_ready"), sem("xn_ready")
        xt_stored = sem("xt_stored")
        g_in, const_ready = sem("g_in"), sem("const_ready")
        xt_done, ht_done, xt_copied, ht_copied = sem("xt_done"), sem("ht_done"), sem("xt_copied"), sem("ht_copied")
        w_loaded = [sem(f"w_loaded{i}") for i in range(2)]
        z_done, z_copied = sem("z_done"), sem("z_copied")
        z_stored = [sem(f"z_stored{i}") for i in range(2)]
        zs_done, zs_copied, zs_stored = sem("zs_done"), sem("zs_copied"), sem("zs_stored")

        with nc.Block() as block:

            @block.gpsimd
            def _(pool):
                nc.gpsimd.memset(ident[:, :], 0.0).then_inc(const_ready, 1)
                nc.gpsimd.memset(eps[:, :], EPS).then_inc(const_ready, 1)
                pool.wait_ge(const_ready, 2)
                nc.gpsimd.affine_select(out=ident[:, :], in_=ident[:, :], compare_op=ALU.not_equal, fill=1.0,
                                        base=0, pattern=[[-1, P]], channel_multiplier=1).then_inc(const_ready, 1)

            @block.sync
            def _(sp):
                sp.dma_start(g1[:, :], io["norm1_g"].rearrange("l (k p) -> p (l k)", p=P)).then_inc(g_in, 16)

                def load_x(slot, n, src):
                    sp.dma_start(xin[0:n, slot, :], src).then_inc(x_in[slot], 16)

                for slot in range(2):
                    load_x(slot, P, x_p[slot * P:(slot + 1) * P, :])
                with sp.Fori(1, TQ // 2) as it:
                    for slot in range(2):
                        sp.wait_ge(x_used, 2 * (it - 1) + slot + 1)
                        load_x(slot, P, x_p[ds((it * 2 + slot) * P, P), :])
                sp.wait_ge(x_used, TQ - 1)
                load_x(0, NS, x_s[:, :])

                for slot in range(2):
                    sp.dma_start(win[:, slot, :, :], w_in[:, :, slot * P:(slot + 1) * P]).then_inc(w_loaded[slot], 16)
                with sp.Fori(1, NM // 2) as it:
                    for slot in range(2):
                        sp.wait_ge(z_done, NT * (2 * (it - 1) + slot + 1))
                        sp.dma_start(win[:, slot, :, :], w_in[:, :, ds((it * 2 + slot) * P, P)]).then_inc(w_loaded[slot], 16)
                sp.wait_ge(z_done, NT * (NM - 1))
                sp.dma_start(win[:, 0, :, 0:MR], w_in[:, :, NM * P:IN_W]).then_inc(w_loaded[0], 16)

            @block.tensor
            def _(pe):
                pe.wait_ge(const_ready, 3)

                def transposes(t, slot, n, loads, first=False):
                    pe.wait_ge(x_in[slot], loads)
                    if not first:
                        pe.wait_ge(xt_copied, 2 * t)
                    for k in range(KD):
                        last = nc.tensor.transpose(ps[k // 4][:, (k % 4) * P:(k % 4) * P + n],
                                                   xin[0:n, slot, k * P:(k + 1) * P], ident[0:n, 0:n])
                    last.then_inc(xt_done, 1)
                    pe.wait_ge(xn_ready, t + 1)
                    if not first:
                        pe.wait_ge(ht_copied, 2 * t)
                    for k in range(KD):
                        last = nc.tensor.transpose(ps[2 + k // 4][:, (k % 4) * P:(k % 4) * P + n],
                                                   xn[0:n, slot, k * P:(k + 1) * P], ident[0:n, 0:n])
                    last.then_inc(ht_done, 1)

                transposes(0, 0, P, 16, first=True)
                with pe.Fori(0, TQ // 2 - 1) as it:
                    for u in range(2):
                        transposes(it * 2 + 1 + u, (1 + u) % 2, P, 16 * (it + 1 + u))
                transposes(TQ - 1, 1, P, 16 * (TQ // 2))
                transposes(TQ, 0, NS, 16 * (TQ // 2 + 1))

                pe.wait_ge(ht_copied, 2 * (TQ + 1))
                pe.wait_ge(xt_copied, 2 * (TQ + 1))

                def product(slot, cols, loads, freed):
                    pe.wait_ge(w_loaded[slot], loads)
                    if freed is not None:
                        pe.wait_ge(z_copied, freed)
                    for third in range(NT):
                        for k in range(KD):
                            last = nc.tensor.matmul(ps[slot * 3 + third][0:cols, 0:TC], win[:, slot, k, 0:cols],
                                                    hT[:, k, third * TC:(third + 1) * TC], start=(k == 0), stop=(k == KD - 1))
                        last.then_inc(z_done, 1)

                def decoded(m, slot, cols, freed):
                    pe.wait_ge(z_copied, NT * m + NT)
                    if freed is not None:
                        pe.wait_ge(zs_copied, freed)
                    nc.tensor.transpose(ps[6 + slot][0:NS, 0:cols], z[0:cols, slot, T:TT],
                                        ident[0:cols, 0:cols]).then_inc(zs_done, 1)

                product(0, P, 16, None)
                product(1, P, 16, None)
                decoded(0, 0, P, None)
                product(0, P, 32, NT)
                decoded(1, 1, P, None)
                product(1, P, 32, 2 * NT)
                with pe.Fori(2, NM // 2) as it:
                    for slot in range(2):
                        m = it * 2 + slot
                        decoded(m - 2, slot, P, m - 3)
                        product(slot, P, 16 * (it + 1), NT * (m - 1))
                decoded(NM - 2, 0, P, NM - 3)
                product(0, MR, 16 * (NM // 2 + 1), NT * (NM - 1))
                decoded(NM - 1, 1, P, NM - 2)
                decoded(NM, 0, MR, NM - 1)

            @block.scalar
            def _(act):
                def row_square(t, slot, n, loads, first=False):
                    act.wait_ge(x_in[slot], loads)
                    if not first:
                        act.wait_ge(xn_ready, t)
                    nc.scalar.activation(sq[0:n, :], xin[0:n, slot, :], ACT.Square, accum_out=ss[0:n, slot:slot + 1])
                    nc.scalar.drain()
                    nc.scalar.activation(rms[0:n, slot:slot + 1], ss[0:n, slot:slot + 1], ACT.Sqrt,
                                         scale=1.0 / D, bias=eps[0:n, :]).then_inc(rms_ready, 1)
                    act.wait_ge(xt_done, t + 1)
                    for half in range(2):
                        nc.scalar.activation(xT[:, half * 4:half * 4 + 4, ds(t * P, n)],
                                             ps[half][:, :].rearrange("p (k t) -> p k t", k=4)[:, :, 0:n],
                                             ACT.Copy).then_inc(xt_copied, 1)

                act.wait_ge(const_ready, 3)
                row_square(0, 0, P, 16, first=True)
                with act.Fori(0, TQ // 2 - 1) as it:
                    for u in range(2):
                        row_square(it * 2 + 1 + u, (1 + u) % 2, P, 16 * (it + 1 + u))
                row_square(TQ - 1, 1, P, 16 * (TQ // 2))
                row_square(TQ, 0, NS, 16 * (TQ // 2 + 1))
                act.wait_ge(xt_copied, 2 * (TQ + 1))
                for k in range(KD):
                    act.dma_start(io["xT"][k * P:(k + 1) * P, :], xT[:, k, :]).then_inc(xt_stored, 16)

                def copy_z(m, slot, cols, stored):
                    if stored is not None:
                        act.wait_ge(z_stored[slot], stored)
                        act.wait_ge(zs_done, m - 1)
                    for third in range(NT):
                        act.wait_ge(z_done, NT * m + third + 1)
                        nc.scalar.activation(z[0:cols, slot, third * TC:(third + 1) * TC], ps[slot * 3 + third][0:cols, 0:TC],
                                             ACT.Copy).then_inc(z_copied, 1)
                    act.wait_ge(z_copied, NT * m + NT)
                    act.dma_start(zT[ds(m * P, cols), :], z[0:cols, slot, :]).then_inc(z_stored[slot], 16)

                copy_z(0, 0, P, None)
                copy_z(1, 1, P, None)
                with act.Fori(1, NM // 2) as it:
                    for slot in range(2):
                        copy_z(it * 2 + slot, slot, P, 16 * it)
                copy_z(NM, 0, MR, 16 * (NM // 2))
                act.wait_ge(z_stored[0], 16 * (NM // 2 + 1))
                act.wait_ge(z_stored[1], 16 * (NM // 2))
                act.wait_ge(xt_stored, 16 * KD)
                act.wait_ge(zs_copied, NM + 1)
                act.dma_start(zS[:, :], zs[:, :]).then_inc(zs_stored, 16)
                act.wait_ge(zs_stored, 16)

            @block.vector
            def _(dve):
                dve.wait_ge(g_in, 16)

                def normalise(t, slot, n):
                    dve.wait_ge(rms_ready, t + 1)
                    nc.vector.reciprocal(rstd[0:n, slot:slot + 1], rms[0:n, slot:slot + 1])
                    nc.vector.drain()
                    nc.vector.tensor_scalar(xn[0:n, slot, :], xin[0:n, slot, :], rstd[0:n, slot:slot + 1], None,
                                            ALU.mult).then_inc(xn_ready, 1)
                    dve.wait_ge(ht_done, t + 1)
                    dve.wait_ge(xt_done, t + 1)
                    for half in range(2):
                        last = nc.vector.tensor_tensor(
                            hT[:, half * 4:half * 4 + 4, ds(t * P, n)],
                            ps[2 + half][:, :].rearrange("p (k t) -> p k t", k=4)[:, :, 0:n],
                            g1[:, half * 4:half * 4 + 4].unsqueeze(2).broadcast_to([P, 4, n]), ALU.mult)
                        last.then_inc(ht_copied, 1)
                    nc.vector.engine_nop().then_inc(x_used, 1)

                normalise(0, 0, P)
                with dve.Fori(0, TQ // 2 - 1) as it:
                    for u in range(2):
                        normalise(it * 2 + 1 + u, (1 + u) % 2, P)
                normalise(TQ - 1, 1, P)
                normalise(TQ, 0, NS)

                def copy_decoded(m, slot, cols):
                    dve.wait_ge(zs_done, m + 1)
                    nc.vector.tensor_copy(zs[:, ds(m * P, cols)], ps[6 + slot][0:NS, 0:cols]).then_inc(zs_copied, 1)

                for m, slot in tiles(dve, NM, 2):
                    copy_decoded(m, slot, P)
                copy_decoded(NM, 0, MR)


GQ, GK, GV, GR, GA = 0, 256, 512, 768, 1024
NQ, NG, MU, MV, MI, MF, MO = 1040, 2320, 2344, 2600, 2856, 2860, 2864
HP = 2
CH = 128
NCH = T // CH
NB = T // 16 - 1
Q_TILES = (0, 1, 2, 3, 6, 8)


def prepare_prompt(nc, io, keep):
    zT = io["zT"]
    ident, eps = keep["ident"], keep["eps"]
    nat, gnat = keep["rows_nat"], keep["gates_nat"]
    kcmp, vcmp = keep["kcmpT"], keep["vcmp"]
    decay, vnat, mqk, mknat = keep["decay"], keep["v_nat"], keep["mqk"], keep["mk_nat"]
    R, RN, uact = keep["rows"], keep["rows_cols"], keep["uact"]
    cbias, w2 = keep["cbias"], keep["w2"]
    b2 = keep["b2"]
    with ExitStack() as ctx:
        sb = lambda n, s, d=F32: ctx.enter_context(nc.sbuf_tensor(n, s, d))
        sem = semaphores(nc, ctx, "prepare")
        zin = sb("zin", [P, 10, TT])
        sqt = sb("sqt", [P, 2, TT])
        rtum = sb("rtum", [P, HP * (3 + TT)])
        rt = rtum[:, 0:2 * TT].rearrange("p (k t) -> p k t", k=2)
        um = rtum[:, :].rearrange("p (k t) -> p k t", k=HP)
        g4 = keep["g4"]
        blk1 = sb("blk1", [P, P])
        ga = uact[0:16, 0, :]
        aw = sb("aw", [16, 256])
        ab = sb("ab", [P, HP])
        spare = keep["onat_flat"]
        gv = spare[:, 0:4 * TT].rearrange("p (j t) -> p j t", j=4)
        t1, t2 = spare[:, 4 * TT:5 * TT], spare[:, 5 * TT:6 * TT]
        resets = spare[:, 6 * TT:6 * TT + T].rearrange("p (i t) -> p i t", t=CH)
        st_nat = sb("st_nat", [3 * NS, 256])
        stT = sb("stT", [P, HP, NS, 3])
        wc = sb("wc", [P, HP, 4])
        bc = sb("bc", [P, HP])
        bd = sb("bd", [P, 4, P])
        spare2 = keep["hs"][:, :, :, :].rearrange("p i h e -> p (i h e)")
        gates = spare2[:, 0:TT]
        gi, ngt = gates[0:4, :], gates[32:56, :]
        gf = spare2[0:4, TT:2 * TT]
        gbias = sb("gbias", [4, 2])
        mm = sb("mm", [4, 1 + T])
        fc = sb("fc", [4, T])
        ngb = sb("ngb", [P, 1])[32:56, :]
        pe_nat = sb("pe_nat", [64, HD])
        peT = sb("peT", [64, 64])
        kcv = zin[0:64, 0:4, 0:T].rearrange("d (s h) t -> d s h t", s=2)
        w1c = zin[0:64, 4:8, 0:T].rearrange("d (s a) (r b e) -> d s a r b e", s=2, r=8, b=2)
        hi = sb("hi", [64, 2, 2, 64])
        hid = sb("hid", [64, 2, 2, 64])
        sg = sb("sg", [64, 2, 2, 64])
        ksq = sb("ksq", [64, 2, 64])
        krt = sb("krt", [64, 2, 64])
        b1 = sb("b1", [64, 2])
        ones = keep["ones"]
        pq = [ctx.enter_context(nc.psum_tensor(f"pq{i}", [P, 512], F32)) for i in range(3)]
        pn = [ctx.enter_context(nc.psum_tensor(f"pn{i}", [P, 512], F32)) for i in range(2)]
        pl = [ctx.enter_context(nc.psum_tensor(f"pl{i}", [P, 512], F32)) for i in range(3)]

        zin_in = [sem(f"zin_in{j}") for j in range(10)]
        small_in, gla_in, conv_in, cmp_in, zeroed, zeroed2 = (sem("small_in"), sem("gla_in"), sem("conv_in"), sem("cmp_in"),
                                                     sem("zeroed"), sem("zeroed2"))
        sq_ready, ssq_done, rt_ready, qn_ready = sem("sq_ready"), sem("ssq_done"), sem("rt_ready"), sem("qn_ready")
        la_done, ls_abs, ls_ln, ls_min, scanned = sem("la_done"), sem("ls_abs"), sem("ls_ln"), sem("ls_min"), sem("scanned")
        st_done, st_copied, conv_done, sig_done, u_ready = (sem("st_done"), sem("st_copied"), sem("conv_done"),
                                                            sem("sig_done"), sem("u_ready"))
        mqk_done, mqk_copied = sem("mqk_done"), sem("mqk_copied")
        rows_ready, m_ready, em_ready, gates_ready, gates_done, gates_copied = (
            sem("rows_ready"), sem("m_ready"), sem("em_ready"), sem("gates_ready"), sem("gates_done"), sem("gates_copied"))
        nA_done, nB_done, nA_copied, nB_copied = sem("nA_done"), sem("nB_done"), sem("nA_copied"), sem("nB_copied")
        pe_done, pe_copied, cb_done, cb_ready, hid_done, hi_copied, hid_ready, act_sig, act_ready = (
            sem("pe_done"), sem("pe_copied"), sem("cb_done"), sem("cb_ready"), sem("hid_done"), sem("hi_copied"),
            sem("hid_ready"), sem("act_sig"), sem("act_ready"))
        kc_done, kc_copied, kss_done, krt_ready, kn_ready, vc_done, vc_copied = (
            sem("kc_done"), sem("kc_copied"), sem("kss_done"), sem("krt_ready"), sem("kn_ready"), sem("vc_done"), sem("vc_copied"))
        out_done, q_stored, um_zeroed = sem("out_done"), sem("q_stored"), sem("um_zeroed")

        with nc.Block() as block:

            @block.gpsimd
            def _(pool):
                nc.gpsimd.memset(eps[:, :], EPS)
                nc.gpsimd.memset(blk1[:, :], 0.0)
                nc.gpsimd.memset(ones[:, :], 1.0)
                nc.gpsimd.memset(bd[:, :, :], 0.0)
                nc.gpsimd.memset(R[:, :], 0.0)
                nc.gpsimd.memset(vcmp[:, :, :], 0.0)
                nc.gpsimd.drain()
                nc.gpsimd.memset(kcmp[:, :, :], 0.0)
                nc.gpsimd.drain()
                nc.gpsimd.memset(resets[:, :, :], 1.0)
                nc.gpsimd.drain()
                nc.gpsimd.memset(mm[:, 0:1], 0.0).then_inc(zeroed, 1)
                pool.wait_ge(zeroed, 1)
                nc.gpsimd.memset(blk1[0:64, 0:64], 1.0)
                nc.gpsimd.drain()
                nc.gpsimd.memset(blk1[64:128, 64:128], 1.0)
                nc.gpsimd.drain()
                nc.gpsimd.memset(resets[:, :, 0:1], 0.0).then_inc(zeroed2, 1)
                pool.wait_ge(qn_ready, len(Q_TILES))
                nc.gpsimd.memset(um[:, :, 0:3], 0.0).then_inc(um_zeroed, 1)

            @block.sync
            def _(sp):
                for j in range(10):
                    sp.dma_start(zin[:, j, :], zT[NQ + j * P:NQ + (j + 1) * P, :]).then_inc(zin_in[j], 16)
                for half in range(2):
                    sp.dma_start(g4[half * 64:half * 64 + 64, :], io["nsa_qk_g"].rearrange("l k d -> d (l k)")).then_inc(small_in, 16)
                sp.dma_start(ngb[:, :], io["nsa_gate_b"].rearrange("l k -> k l")).then_inc(small_in, 16)
                sp.dma_start(ngt[:, :], zT[NG:NG + 24, :]).then_inc(small_in, 16)
                sp.dma_start(gbias[:, :], io["ml_gate_b"].rearrange("l k h -> h (l k)")).then_inc(small_in, 16)
                sp.dma_start(gi[:, :], zT[MI:MI + 4, :]).then_inc(small_in, 16)
                sp.dma_start(gf[:, :], zT[MF:MF + 4, :]).then_inc(small_in, 16)
                sp.dma_start(gv[:, 0:2, :], zT[GV:GV + 2 * P, :].rearrange("(j p) t -> p j t", p=P)).then_inc(gla_in, 16)
                sp.dma_start(gv[:, 2:4, :], zT[MV:MV + 2 * P, :].rearrange("(j p) t -> p j t", p=P)).then_inc(gla_in, 16)
                sp.dma_start(ga[:, :], zT[GA:GA + 16, :]).then_inc(gla_in, 16)
                sp.dma_start(aw[:, :], io["gla_a_w"].rearrange("l k n -> (l k) n")).then_inc(gla_in, 16)
                sp.dma_start(ab[:, :], io["gla_a_b"].rearrange("l (j p) -> p (l j)", p=P)).then_inc(gla_in, 16)
                sp.dma_start(st_nat[:, :], io["state_mlstm_conv"].rearrange("l s j c -> (l s j) c")).then_inc(conv_in, 16)
                for hp in range(HP):
                    sp.dma_start(wc[:, hp, :], io["ml_conv_w"][0, :, hp * P:(hp + 1) * P].rearrange("j p -> p j")).then_inc(conv_in, 16)
                sp.dma_start(bc[:, :], io["ml_conv_b"].rearrange("l (k p) -> p (l k)", p=P)).then_inc(conv_in, 16)
                sp.wait_ge(zeroed2, 1)
                for idx in range(4):
                    w = io["ml_wq"] if idx < 2 else io["ml_wk"]
                    for h2 in range(2):
                        sp.dma_start(bd[h2 * 64:h2 * 64 + 64, idx, h2 * 64:h2 * 64 + 64],
                                     w[0, (idx % 2) * 2 + h2, :, :]).then_inc(conv_in, 16)
                for n, j in enumerate(Q_TILES):
                    sp.wait_ge(qn_ready, n + 1)
                    sp.dma_start(io["qkT"][n * P:(n + 1) * P, :], zin[:, j, :]).then_inc(q_stored, 16)
                sp.wait_ge(um_zeroed, 1)
                sp.dma_start(um[:, :, 3:3 + TT], zT[MU:MU + 2 * P, :].rearrange("(j p) t -> p j t", p=P)).then_inc(conv_in, 16)
                sp.wait_ge(conv_in, 16 * 13)
                for hp in range(HP):
                    sp.dma_start(io["out14"][0, 0, :, hp * P:(hp + 1) * P].rearrange("j p -> p j"), um[:, hp, T:T + 3]).then_inc(out_done, 16)
                sp.dma_start(io["out15"][0, :, 0:2, :], io["state_mlstm_conv"][0, :, 1:3, :]).then_inc(out_done, 16)
                sp.dma_start(io["out15"][0, :, 2, :], io["zS"][:, MU:MU + 256]).then_inc(out_done, 16)
                sp.wait_ge(nA_copied, 9)
                sp.wait_ge(nB_copied, 9)
                sp.dma_start(io["out2"].rearrange("l b (i p) k h d -> p (l b i) (k h d)", p=P), nat[:, 0:TQ, 0:512]).then_inc(out_done, 16)
                sp.dma_start(io["out4"].rearrange("l b (i p) k h d -> p (l b i) (k h d)", p=P), nat[:, 4:TQ, 512:768]).then_inc(out_done, 16)
                sp.dma_start(io["out3"].rearrange("l b t k h d -> (l b t) (k h d)"), nat[0:NS, TQ, 0:512]).then_inc(out_done, 16)
                sp.dma_start(io["out5"][0, :, 511, :, :, :].rearrange("b k h d -> b (k h d)"), nat[0:NS, TQ, 512:768]).then_inc(out_done, 16)
                for s in range(NS):
                    sp.dma_start(io["out5"][0, s, 0:511, :, :, :].rearrange("t k h d -> t (k h d)"),
                                 io["cache_nsa_win"][0, s, 1:512, :, :, :].rearrange("t k h d -> t (k h d)")).then_inc(out_done, 16)
                sp.wait_ge(q_stored, 16 * len(Q_TILES))
                sp.dma_start(pe_nat[:, :], io["cmp_pe"].rearrange("l s r d -> (l s r) d")).then_inc(cmp_in, 16)
                for slot in range(2):
                    for half in range(2):
                        for a in range(2):
                            at = half * 16 + a * 8
                            sp.dma_start(w1c[:, slot, a, :, half, :],
                                         io["cmp_w1"][0, slot, at:at + 8, :, :].rearrange("r d e -> d r e")).then_inc(cmp_in, 16)
                sp.dma_start(w2[:, :, :], io["cmp_w2"].rearrange("l s e d -> e (l s) d")).then_inc(cmp_in, 16)
                sp.dma_start(b1[:, :], io["cmp_b1"].rearrange("l s e -> e (l s)")).then_inc(cmp_in, 16)
                sp.dma_start(b2[:, 0:1], io["cmp_b2"][0, 0:1, :].rearrange("l d -> d l")).then_inc(cmp_in, 16)
                sp.dma_start(b2[0:1, 1:65], io["cmp_b2"][0, 1:2, :]).then_inc(cmp_in, 16)
                for slot in range(2):
                    for h in range(2):
                        at = NQ + (4 + slot) * P + h * 64
                        sp.dma_start(kcv[:, slot, h, :], zT[at:at + 64, 0:T]).then_inc(cmp_in, 16)
                sp.wait_ge(m_ready, 1)
                sp.dma_start(io["out12"].rearrange("l b h -> h (l b)"), mm[:, T:T + 1]).then_inc(out_done, 16)
                sp.wait_ge(out_done, 16 * (4 + 4 + NS + 1))

            @block.tensor
            def _(pe):
                pe.wait_ge(zeroed2, 1)
                for n, j in enumerate(Q_TILES):
                    pe.wait_ge(sq_ready, n + 1)
                    if n:
                        pe.wait_ge(rt_ready, 3 * n)
                    for third in range(NT):
                        nc.tensor.matmul(pq[third][:, 0:TC], blk1[:, :], sqt[:, n % 2, third * TC:(third + 1) * TC],
                                         start=True, stop=True).then_inc(ssq_done, 1)
                pe.wait_ge(gla_in, 16 * 5)
                for hp in range(HP):
                    if hp:
                        pe.wait_ge(ls_abs, NT)
                        pe.wait_ge(ls_min, NT)
                    for third in range(NT):
                        nc.tensor.matmul(pl[third][:, 0:TC], aw[:, hp * P:(hp + 1) * P], ga[:, third * TC:(third + 1) * TC],
                                         start=True, stop=True).then_inc(la_done, 1)
                pe.wait_ge(conv_in, 16 * 13)
                for hp in range(HP):
                    nc.tensor.transpose(pn[0][:, hp * 32:hp * 32 + 24], st_nat[:, hp * P:(hp + 1) * P],
                                        ident[0:24, 0:24]).then_inc(st_done, 1)
                pe.wait_ge(ls_abs, 2 * NT)
                pe.wait_ge(ls_min, 2 * NT)
                pe.wait_ge(u_ready, HP)
                for idx in range(4):
                    for third in range(NT):
                        if idx:
                            pe.wait_ge(mqk_copied, (idx - 1) * NT + third + 1)
                        nc.tensor.matmul(pl[third][:, 0:TC], bd[:, idx, :], uact[:, idx % 2, third * TC:(third + 1) * TC],
                                         start=True, stop=True).then_inc(mqk_done, 1)
                pe.wait_ge(qn_ready, len(Q_TILES))
                for j in (4, 5, 7, 9):
                    pe.wait_ge(zin_in[j], 16)
                pe.wait_ge(st_copied, 1)
                for i in range(9):
                    n = P if i < 8 else NS
                    if i:
                        pe.wait_ge(nA_copied, i)
                    for c in range(4):
                        last = nc.tensor.transpose(pn[0][0:n, c * P:(c + 1) * P], zin[:, 4 + c, i * P:i * P + n], ident[:, :])
                    last.then_inc(nA_done, 1)
                    if i:
                        pe.wait_ge(nB_copied, i)
                    for c in range(2):
                        last = nc.tensor.transpose(pn[1][0:n, c * P:(c + 1) * P], zin[:, 8 + c, i * P:i * P + n], ident[:, :])
                    last.then_inc(nB_done, 1)
                pe.wait_ge(rows_ready, 4)
                pe.wait_ge(mqk_copied, 4 * NT)
                for i in range(NCH):
                    pe.wait_ge(nA_copied, 9 + i)
                    for c in range(4):
                        last = nc.tensor.transpose(pn[0][:, c * P:(c + 1) * P], gv[:, c, i * P:(i + 1) * P], ident[:, :])
                    last.then_inc(nA_done, 1)
                    pe.wait_ge(nB_copied, 9 + i)
                    for c in range(2):
                        nc.tensor.transpose(pn[1][:, c * P:(c + 1) * P], mqk[:, 2 + c, i * P:(i + 1) * P], ident[:, :])
                    nc.tensor.transpose(pn[1][:, 256:384], R[:, i * P:(i + 1) * P], ident[:, :]).then_inc(nB_done, 1)
                pe.wait_ge(gates_ready, 1)
                pe.wait_ge(rt_ready, 3 * len(Q_TILES))
                for i in range(9):
                    n = P if i < 8 else NS
                    last = nc.tensor.transpose(pq[0][0:n, i * 24:(i + 1) * 24], ngt[:, i * P:i * P + n], ident[32:56, 32:56])
                last.then_inc(gates_done, 1)
                pe.wait_ge(cmp_in, 16 * 17)
                nc.tensor.transpose(pq[1][0:64, 0:64], pe_nat[:, :], ident[0:64, 0:64]).then_inc(pe_done, 1)
                pe.wait_ge(pe_copied, 1)
                for slot in range(2):
                    for half in range(2):
                        for r in range(16):
                            c = slot * 32 + half * 16 + r
                            last = nc.tensor.matmul(pq[2][0:64, slot:slot + 1], w1c[:, slot, r // 8, r % 8, half, :], peT[:, c:c + 1],
                                                    start=(half == 0 and r == 0), stop=(half == 1 and r == 15))
                last.then_inc(cb_done, 1)
                for slot in range(2):
                    for r in range(16):
                        last = nc.tensor.matmul(pl[slot][:, 0:128], w1c[:, slot, r // 8, r % 8, :, :],
                                                kcv[:, slot, :, :].rearrange("d h (n r) -> d h n r", r=16)[:, :, :, r],
                                                start=(r == 0), stop=(r == 15))
                    last.then_inc(hid_done, 1)
                pe.wait_ge(act_ready, 1)
                nc.tensor.matmul(pl[2][0:64, 0:2 * NB], w2[:, 0, :], hid[:, 0, :, 0:NB], start=True, stop=True).then_inc(kc_done, 1)
                pe.wait_ge(act_ready, 2)
                pe.wait_ge(hi_copied, 2)
                pe.wait_ge(hid_ready, 2)
                for h in range(2):
                    nc.tensor.matmul(pl[0][0:NB, h * 64:h * 64 + 64], hid[:, 1, h, 0:NB], w2[:, 1, :], start=True, stop=False)
                    last = nc.tensor.matmul(pl[0][0:NB, h * 64:h * 64 + 64], ones[0:1, 0:NB], b2[0:1, 1:65], start=False, stop=True)
                last.then_inc(vc_done, 1)
                pe.wait_ge(kc_copied, 2)
                nc.tensor.matmul(pl[1][0:64, 0:2 * NB], blk1[0:64, 0:64], ksq[:, :, 0:NB], start=True, stop=True).then_inc(kss_done, 1)

            @block.scalar
            def _(act):
                act.wait_ge(zeroed2, 1)

                def square(n):
                    act.wait_ge(zin_in[Q_TILES[n]], 16)
                    if n >= 2:
                        act.wait_ge(ssq_done, 3 * (n - 1))
                    nc.scalar.activation(sqt[:, n % 2, :], zin[:, Q_TILES[n], :], ACT.Square).then_inc(sq_ready, 1)

                square(0)
                for n in range(len(Q_TILES)):
                    if n + 1 < len(Q_TILES):
                        square(n + 1)
                    if n >= 2:
                        act.wait_ge(qn_ready, n - 1)
                    for third in range(NT):
                        act.wait_ge(ssq_done, 3 * n + third + 1)
                        nc.scalar.activation(rt[:, n % 2, third * TC:(third + 1) * TC], pq[third][:, 0:TC], ACT.Sqrt,
                                             scale=1.0 / HD, bias=eps[:, :]).then_inc(rt_ready, 1)

                for hp in range(HP):
                    if hp:
                        act.wait_ge(scanned, hp)
                    for third in range(NT):
                        act.wait_ge(la_done, hp * NT + third + 1)
                        nc.scalar.activation(t1[:, third * TC:(third + 1) * TC], pl[third][:, 0:TC], ACT.Abs,
                                             bias=ab[:, hp:hp + 1]).then_inc(ls_abs, 1)
                    nc.scalar.drain()
                    nc.scalar.activation(t1[:, :], t1[:, :], ACT.Exp, scale=-1.0)
                    nc.scalar.drain()
                    nc.scalar.activation(t1[:, :], t1[:, :], ACT.Ln, bias=1.0).then_inc(ls_ln, 1)
                act.wait_ge(scanned, HP)
                act.wait_ge(small_in, 16 * 7)
                nc.scalar.activation(t1[0:4, :], gf[:, :], ACT.Abs, bias=gbias[:, 1:2])
                nc.scalar.drain()
                nc.scalar.activation(t1[0:4, :], t1[0:4, :], ACT.Exp, scale=-1.0)
                nc.scalar.drain()
                nc.scalar.activation(t1[0:4, :], t1[0:4, :], ACT.Ln, bias=1.0).then_inc(ls_ln, 1)
                act.wait_ge(em_ready, 1)
                nc.scalar.activation(R[64:68, :], fc[:, :], ACT.Exp).then_inc(rows_ready, 1)
                nc.scalar.activation(R[96:100, :], mm[:, 1:1 + T], ACT.Exp, scale=-1.0).then_inc(rows_ready, 1)
                act.wait_ge(st_done, 2)
                nc.scalar.activation(stT[:, :, :, :], pn[0][:, 0:64].rearrange("p (k c) -> p k c", k=2)[:, :, 0:24]
                                     .rearrange("p k (s j) -> p k s j", j=3), ACT.Copy).then_inc(st_copied, 1)
                for hp in range(HP):
                    act.wait_ge(conv_done, hp + 1)
                    nc.scalar.activation(sqt[:, hp, :], uact[:, hp, :], ACT.Sigmoid).then_inc(sig_done, 1)
                nc.scalar.activation(ngt[:, :], ngt[:, :], ACT.Sigmoid, bias=ngb[:, :]).then_inc(gates_ready, 1)
                for idx in range(4):
                    for third in range(NT):
                        act.wait_ge(mqk_done, idx * NT + third + 1)
                        nc.scalar.activation(mqk[:, idx, third * TC:(third + 1) * TC], pl[third][:, 0:TC], ACT.Copy,
                                             scale=1.0 if idx < 2 else HD ** -0.5).then_inc(mqk_copied, 1)
                nc.scalar.drain()
                nc.scalar.activation(keep["mqk_dec"][:, :, :], mqk[:, :, T:TT], ACT.Copy)
                for i in range(9):
                    n = P if i < 8 else NS
                    act.wait_ge(nB_done, i + 1)
                    nc.scalar.activation(nat[0:n, i, 512:768], pn[1][0:n, 0:256], ACT.Copy).then_inc(nB_copied, 1)
                for i in range(NCH):
                    act.wait_ge(nB_done, 9 + i + 1)
                    nc.scalar.activation(mknat[:, i, :], pn[1][:, 0:256], ACT.Copy)
                    nc.scalar.activation(RN[:, i, :].rearrange("p (k h) -> p k h", h=4),
                                         pn[1][:, 256:384].rearrange("p (k c) -> p k c", k=4)[:, :, 0:4], ACT.Copy).then_inc(nB_copied, 1)
                act.wait_ge(gates_done, 1)
                nc.scalar.activation(gnat[:, 0:8, :], pq[0][:, 0:192].rearrange("p (i c) -> p i c", c=24), ACT.Copy)
                nc.scalar.activation(gnat[0:NS, 8, :], pq[0][0:NS, 192:216], ACT.Copy).then_inc(gates_copied, 1)
                act.wait_ge(pe_done, 1)
                nc.scalar.activation(peT[:, :], pq[1][0:64, 0:64], ACT.Copy).then_inc(pe_copied, 1)
                for slot in range(2):
                    act.wait_ge(hid_done, slot + 1)
                    nc.scalar.activation(hi[:, slot, :, :], pl[slot][64:128, 0:128].rearrange("p (h n) -> p h n", h=2),
                                         ACT.Copy).then_inc(hi_copied, 1)
                act.wait_ge(cb_ready, 1)
                for slot in range(2):
                    act.wait_ge(hid_ready, slot + 1)
                    nc.scalar.activation(sg[:, slot, :, 0:NB], hid[:, slot, :, 0:NB], ACT.Sigmoid,
                                         bias=cbias[:, slot:slot + 1]).then_inc(act_sig, 1)
                act.wait_ge(kc_done, 1)
                kv = pl[2][0:64, 0:2 * NB].rearrange("p (h n) -> p h n", h=2)
                nc.scalar.activation(kcmp[:, :, 0:NB], kv, ACT.Identity, bias=b2[:, 0:1]).then_inc(kc_copied, 1)
                nc.scalar.activation(ksq[:, :, 0:NB], kv, ACT.Square, bias=b2[:, 0:1]).then_inc(kc_copied, 1)
                act.wait_ge(vc_done, 1)
                nc.scalar.activation(vcmp[0:NB, :, :], pl[0][0:NB, 0:128].rearrange("p (h d) -> p h d", h=2), ACT.Copy).then_inc(vc_copied, 1)
                act.wait_ge(kss_done, 1)
                nc.scalar.activation(krt[:, :, 0:NB], pl[1][0:64, 0:2 * NB].rearrange("p (h n) -> p h n", h=2), ACT.Sqrt,
                                     scale=1.0 / HD, bias=eps[0:64, :]).then_inc(krt_ready, 1)

            @block.vector
            def _(dve):
                dve.wait_ge(zeroed2, 1)
                dve.wait_ge(small_in, 16 * 7)
                nc.vector.tensor_scalar(g4[:, 0:1], g4[:, 0:1], HD ** -0.5, None, ALU.mult)
                nc.vector.drain()
                for n, j in enumerate(Q_TILES):
                    gain = g4[:, 0:1] if j < 4 else g4[:, 2:3] if j == 6 else g4[:, 3:4]
                    dve.wait_ge(rt_ready, 3 * n + 3)
                    nc.vector.reciprocal(rt[:, n % 2, :], rt[:, n % 2, :])
                    nc.vector.drain()
                    nc.vector.scalar_tensor_tensor(out=zin[:, j, :], in0=zin[:, j, :], scalar=gain, in1=rt[:, n % 2, :],
                                                   op0=ALU.mult, op1=ALU.mult).then_inc(qn_ready, 1)
                dve.wait_ge(gla_in, 16 * 5)
                for hp in range(HP):
                    for third in range(NT):
                        dve.wait_ge(ls_abs, hp * NT + third + 1)
                        nc.vector.tensor_scalar(t2[:, third * TC:(third + 1) * TC], pl[third][:, 0:TC], ab[:, hp:hp + 1], 0.0,
                                                ALU.add, ALU.min).then_inc(ls_min, 1)
                    dve.wait_ge(ls_ln, hp + 1)
                    nc.vector.drain()
                    nc.vector.tensor_tensor(t2[:, :], t2[:, :], t1[:, :], ALU.subtract)
                    nc.vector.drain()
                    nc.vector.tensor_tensor_scan(decay[:, hp, 0:T], resets[:, :, :].rearrange("p i t -> p (i t)"), t2[:, 0:T],
                                                 0.0, ALU.mult, ALU.add)
                    nc.vector.tensor_copy(keep["decay_dec"][:, hp, :], t2[:, T:TT]).then_inc(scanned, 1)
                    nc.vector.drain()
                dve.wait_ge(ls_ln, 3)
                nc.vector.tensor_scalar(gf[:, :], gf[:, :], gbias[:, 1:2], 0.0, ALU.add, ALU.min)
                nc.vector.tensor_scalar(gi[:, :], gi[:, :], gbias[:, 0:1], None, ALU.add)
                nc.vector.drain()
                nc.vector.tensor_tensor(gf[:, :], gf[:, :], t1[0:4, :], ALU.subtract)
                nc.vector.drain()
                nc.vector.tensor_tensor_scan(mm[:, 1:1 + T], gf[:, 0:T], gi[:, 0:T], 0.0, ALU.add, ALU.max).then_inc(m_ready, 1)
                nc.vector.tensor_tensor_scan(fc[:, :], resets[0:4, :, :].rearrange("p i t -> p (i t)"), gf[:, 0:T], 0.0, ALU.mult, ALU.add)
                nc.vector.drain()
                nc.vector.tensor_tensor(R[0:4, :], fc[:, :], mm[:, 1:1 + T], ALU.subtract).then_inc(rows_ready, 1)
                nc.vector.tensor_tensor(R[32:36, :], gi[:, 0:T], fc[:, :], ALU.subtract).then_inc(rows_ready, 1)
                nc.vector.drain()
                nc.vector.tensor_tensor(fc[:, :], fc[:, :], mm[:, 1:1 + T], ALU.subtract)
                nc.vector.drain()
                nc.vector.tensor_tensor(fc[:, :].rearrange("p (i t) -> p i t", t=CH), fc[:, :].rearrange("p (i t) -> p i t", t=CH),
                                        mm[:, 0:T].rearrange("p (i t) -> p i t", t=CH)[:, :, 0:1].broadcast_to([4, NCH, CH]),
                                        ALU.add).then_inc(em_ready, 1)
                dve.wait_ge(conv_in, 16 * 13)
                dve.wait_ge(st_copied, 1)
                dve.wait_ge(ssq_done, 3 * len(Q_TILES))
                for hp in range(HP):
                    nc.vector.tensor_scalar(uact[:, hp, 0:T], um[:, hp, 0:T], wc[:, hp, 0:1], bc[:, hp:hp + 1], ALU.mult, ALU.add)
                    nc.vector.tensor_scalar(uact[:, hp, T:TT], stT[:, hp, :, 0], wc[:, hp, 0:1], bc[:, hp:hp + 1], ALU.mult, ALU.add)
                    nc.vector.drain()
                    for j in range(1, 4):
                        nc.vector.scalar_tensor_tensor(out=uact[:, hp, 0:T], in0=um[:, hp, j:j + T], scalar=wc[:, hp, j:j + 1],
                                                       in1=uact[:, hp, 0:T], op0=ALU.mult, op1=ALU.add)
                        old = stT[:, hp, :, j] if j < 3 else um[:, hp, 3 + T:3 + TT]
                        last = nc.vector.scalar_tensor_tensor(out=uact[:, hp, T:TT], in0=old, scalar=wc[:, hp, j:j + 1],
                                                              in1=uact[:, hp, T:TT], op0=ALU.mult, op1=ALU.add)
                        if j < 3:
                            nc.vector.drain()
                    last.then_inc(conv_done, 1)
                for hp in range(HP):
                    dve.wait_ge(sig_done, hp + 1)
                    nc.vector.tensor_tensor(uact[:, hp, :], uact[:, hp, :], sqt[:, hp, :], ALU.mult).then_inc(u_ready, 1)
                for i in range(9):
                    n = P if i < 8 else NS
                    dve.wait_ge(nA_done, i + 1)
                    nc.vector.tensor_copy(nat[0:n, i, 0:512], pn[0][0:n, :]).then_inc(nA_copied, 1)
                for i in range(NCH):
                    dve.wait_ge(nA_done, 9 + i + 1)
                    nc.vector.tensor_copy(vnat[:, i, :], pn[0][:, :]).then_inc(nA_copied, 1)
                dve.wait_ge(cb_done, 1)
                nc.vector.tensor_tensor(cbias[:, :], pq[2][0:64, 0:2], b1[:, :], ALU.add).then_inc(cb_ready, 1)
                nc.vector.drain()
                for slot in range(2):
                    dve.wait_ge(hi_copied, slot + 1)
                    nc.vector.tensor_tensor(hid[:, slot, :, 0:NB], pl[slot][0:64, 0:128].rearrange("p (h n) -> p h n", h=2)[:, :, 0:NB],
                                            hi[:, slot, :, 1:NB + 1], ALU.add).then_inc(hid_ready, 1)
                nc.vector.drain()
                for slot in range(2):
                    dve.wait_ge(act_sig, slot + 1)
                    nc.vector.scalar_tensor_tensor(out=hid[:, slot, :, 0:NB], in0=hid[:, slot, :, 0:NB], scalar=cbias[:, slot:slot + 1],
                                                   in1=sg[:, slot, :, 0:NB], op0=ALU.add, op1=ALU.mult).then_inc(act_ready, 1)
                dve.wait_ge(krt_ready, 1)
                nc.vector.reciprocal(krt[:, :, 0:NB], krt[:, :, 0:NB])
                nc.vector.drain()
                nc.vector.scalar_tensor_tensor(out=kcmp[:, :, 0:NB], in0=kcmp[:, :, 0:NB], scalar=g4[0:64, 1:2], in1=krt[:, :, 0:NB],
                                               op0=ALU.mult, op1=ALU.mult).then_inc(kn_ready, 1)


BIG = 1e30
FULL, WIN, CMP = 1, 2, 0


def steps_of_head():
    for i in range(TQ):
        yield i, CMP, 0, 1
        yield i, FULL, 0, i + 1
        yield i, WIN, max(0, i - 4), min(i + 1, 5)


STEPS = list(steps_of_head())
NSTEP = len(STEPS)
GROUPS = [-(-s[3] // 4) for s in STEPS]
GAT = [sum(GROUPS[:n]) for n in range(NSTEP + 1)]
NGROUP = GAT[NSTEP]


def attend_prompt(nc, io, keep):
    ident, nat, gnat, kcmp, vcmp, onat = (keep[k] for k in ("ident", "rows_nat", "gates_nat", "kcmpT", "vcmp", "onat"))
    with ExitStack() as ctx:
        sb = lambda n, s, d=F32: ctx.enter_context(nc.sbuf_tensor(n, s, d))
        sem = semaphores(nc, ctx, "attend")
        qT, kT, wT = sb("qT", [64, 2, T]), sb("kT", [64, 2, T]), sb("wT", [64, 2, T])
        diag, edge, cmask = sb("diag", [P, P]), sb("edge", [P, P]), sb("cmask", [P, TQ, P])
        pm = sb("pm", [P, 2, T])
        ptT = sb("ptT", [P, 2, 4 * P])
        mx, nm, den, rs = sb("mx", [P, 2]), sb("nm", [P, 2]), sb("den", [P, 2]), sb("rs", [P, 2])
        S = [ctx.enter_context(nc.psum_tensor(f"pS{i}", [P, 1024], F32)) for i in range(2)]
        PT = [ctx.enter_context(nc.psum_tensor(f"pT{i}", [P, 512], F32)) for i in range(2)]
        O = [ctx.enter_context(nc.psum_tensor(f"pO{i}", [P, 512], F32)) for i in range(2)]
        loaded = [sem(f"head_loaded{i}") for i in range(2)]
        masks, s_done, nm_ready, p_ready, pt_done, pt_copied, pv_done, o_used = (
            sem("masks"), sem("s_done"), sem("nm_ready"), sem("p_ready"), sem("pt_done"), sem("pt_copied"), sem("pv_done"),
            sem("o_used"))

        with nc.Block() as block:

            @block.gpsimd
            def _(pool):
                nc.gpsimd.memset(diag[:, :], 0.0)
                nc.gpsimd.memset(edge[:, :], 0.0)
                nc.gpsimd.memset(cmask[:, :, :], 0.0).then_inc(masks, 1)
                pool.wait_ge(masks, 1)
                nc.gpsimd.affine_select(out=diag[:, :], in_=diag[:, :], compare_op=ALU.is_ge, fill=-BIG,
                                        base=0, pattern=[[-1, P]], channel_multiplier=1)
                nc.gpsimd.affine_select(out=edge[:, :], in_=edge[:, :], compare_op=ALU.is_gt, fill=-BIG,
                                        base=0, pattern=[[1, P]], channel_multiplier=-1)
                nc.gpsimd.affine_select(out=cmask[:, :, :], in_=cmask[:, :, :], compare_op=ALU.is_ge, fill=-BIG,
                                        base=-31, pattern=[[P, TQ], [-16, P]], channel_multiplier=1)
                nc.gpsimd.drain()
                nc.gpsimd.memset(cmask[:, :, NB:P], -BIG).then_inc(masks, 1)

            @block.sync
            def _(sp):
                def load(h, kv, slot):
                    for dst, at in ((qT, h * 64), (kT, 4 * P + kv * 64), (wT, 5 * P + kv * 64)):
                        sp.dma_start(dst[:, slot, :], io["qkT"][ds(at, 64), 0:T]).then_inc(loaded[slot], 16)

                for slot in range(2):
                    load(slot, 0, slot)
                with sp.Fori(1, 4) as it:
                    for slot in range(2):
                        sp.wait_ge(s_done, NSTEP * ((it - 1) * 2 + slot + 1))
                        load(it * 2 + slot, it // 2, slot)

            @block.tensor
            def _(pe):
                pe.wait_ge(masks, 2)
                with pe.Fori(0, 4) as it:
                    for slot in range(2):
                        kv = it // 2
                        s0 = NSTEP * (it * 2 + slot)
                        pe.wait_ge(loaded[slot], 48 * (it + 1))

                        def score(n):
                            i, branch, k0, nk = STEPS[n]
                            q = qT[:, slot, i * P:(i + 1) * P]
                            bank = S[n % 2]
                            if n >= 2:
                                pe.wait_ge(p_ready, s0 + n - 1)
                            else:
                                pe.wait_ge(p_ready, s0)
                            if branch == CMP:
                                nc.tensor.matmul(bank[:, 0:P], ident[:, :], cmask[:, i, :], start=True, stop=False)
                                nc.tensor.matmul(bank[:, 0:P], q, kcmp[:, kv, :], start=False, stop=True).then_inc(s_done, 1)
                                return
                            keys = kT if branch == FULL else wT
                            for b in range(0, nk, 4):
                                m = min(4, nk - b)
                                cut = [(c, mask) for c, mask in ((nk - 1, diag), (0 if branch == WIN and i >= 4 else -1, edge))
                                       if b <= c < b + m]
                                last = nc.tensor.matmul(bank[:, b * P:(b + m) * P], q, keys[:, slot, (k0 + b) * P:(k0 + b + m) * P],
                                                        start=True, stop=not cut)
                                for u, (c, mask) in enumerate(cut):
                                    last = nc.tensor.matmul(bank[:, c * P:(c + 1) * P], ident[:, :], mask[:, :],
                                                            start=False, stop=u == len(cut) - 1)
                            last.then_inc(s_done, 1)

                        def transpose_group(n, g):
                            nk = STEPS[n][3]
                            at = GAT[n] + g
                            u = (at + NGROUP * slot) % 2
                            pe.wait_ge(pt_copied, NGROUP * (it * 2 + slot) + at - 1) if at or slot else pe.wait_ge(pt_copied, NGROUP * it * 2)
                            for c in range(4 * g, min(4 * g + 4, nk)):
                                last = nc.tensor.transpose(PT[u][:, (c % 4) * P:(c % 4 + 1) * P], pm[:, n % 2, c * P:(c + 1) * P], ident[:, :])
                            last.then_inc(pt_done, 1)

                        def weigh_group(n, g):
                            i, branch, k0, nk = STEPS[n]
                            at = GAT[n] + g
                            u = (at + NGROUP * slot) % 2
                            pe.wait_ge(pt_copied, NGROUP * (it * 2 + slot) + at + 1)
                            for c in range(4 * g, min(4 * g + 4, nk)):
                                v = (vcmp[:, kv, :] if branch == CMP else
                                     nat[:, k0 + c, ds((384 if branch == FULL else 640) + kv * 64, 64)])
                                last = nc.tensor.matmul(O[n % 2][:, 0:64], ptT[:, u, (c % 4) * P:(c % 4 + 1) * P], v,
                                                        start=(c == 0), stop=(c == nk - 1))
                            last.then_inc(pv_done, 1)

                        score(0)
                        score(1)
                        for n in range(NSTEP):
                            pe.wait_ge(p_ready, s0 + n + 1)
                            ahead = min(2, GROUPS[n])
                            for g in range(ahead):
                                transpose_group(n, g)
                            if n + 2 < NSTEP:
                                score(n + 2)
                            pe.wait_ge(o_used, s0 + n - 1) if n >= 2 else pe.wait_ge(o_used, s0)
                            for g in range(GROUPS[n]):
                                weigh_group(n, g)
                                if g + ahead < GROUPS[n]:
                                    transpose_group(n, g + ahead)

            @block.scalar
            def _(act):
                with act.Fori(0, 4) as it:
                    for slot in range(2):
                        s0 = NSTEP * (it * 2 + slot)
                        g0 = NGROUP * (it * 2 + slot)

                        def exponentials(n):
                            w = STEPS[n][3] * P
                            act.wait_ge(nm_ready, s0 + n + 1)
                            if n >= 2:
                                act.wait_ge(pt_done, g0 + GAT[n - 1])
                            else:
                                act.wait_ge(pt_done, g0)
                            nc.scalar.activation(pm[:, n % 2, 0:w], S[n % 2][:, 0:w], ACT.Exp, bias=nm[:, n % 2:n % 2 + 1],
                                                 accum_out=den[:, n % 2:n % 2 + 1]).then_inc(p_ready, 1)

                        exponentials(0)
                        for n in range(NSTEP):
                            nk = STEPS[n][3]
                            if n + 1 < NSTEP:
                                exponentials(n + 1)
                            for g in range(GROUPS[n]):
                                at = GAT[n] + g
                                u = (at + NGROUP * slot) % 2
                                act.wait_ge(pt_done, g0 + at + 1)
                                if slot or at >= 2:
                                    act.wait_ge(pv_done, g0 + at - 1)
                                else:
                                    act.wait_ge(pv_done, g0)
                                cols = min(4, nk - 4 * g) * P
                                nc.scalar.activation(ptT[:, u, 0:cols], PT[u][:, 0:cols], ACT.Copy).then_inc(pt_copied, 1)

            @block.vector
            def _(dve):
                with dve.Fori(0, 4) as it:
                    for slot in range(2):
                        h = it * 2 + slot
                        s0 = NSTEP * h
                        g0 = NGROUP * h

                        def row_max(n):
                            i, branch, k0, nk = STEPS[n]
                            w = nk * P
                            dve.wait_ge(s_done, s0 + n + 1)
                            nc.vector.reduce_max(mx[:, n % 2:n % 2 + 1], S[n % 2][:, 0:w], AX.X)
                            nc.vector.drain()
                            nc.vector.tensor_scalar(nm[:, n % 2:n % 2 + 1], mx[:, n % 2:n % 2 + 1], -1e20, -1.0,
                                                    ALU.max, ALU.mult).then_inc(nm_ready, 1)

                        row_max(0)
                        row_max(1)
                        for n in range(NSTEP):
                            i, branch, k0, nk = STEPS[n]
                            u = n % 2
                            dve.wait_ge(p_ready, s0 + n + 1)
                            nc.vector.tensor_scalar(rs[:, u:u + 1], den[:, u:u + 1], 1e-30, None, ALU.max)
                            nc.vector.drain()
                            nc.vector.reciprocal(rs[:, u:u + 1], rs[:, u:u + 1])
                            nc.vector.drain()
                            nc.vector.tensor_tensor(rs[:, u:u + 1], rs[:, u:u + 1], gnat[:, i, ds(h * 3 + branch, 1)], ALU.mult)
                            if n + 2 < NSTEP:
                                row_max(n + 2)
                            nc.vector.drain()
                            dve.wait_ge(pv_done, g0 + GAT[n + 1])
                            out = onat[:, i, ds(256 + h * 64, 64)]
                            if branch == CMP:
                                nc.vector.tensor_scalar(out, O[u][:, 0:64], rs[:, u:u + 1], None, ALU.mult).then_inc(o_used, 1)
                            else:
                                nc.vector.scalar_tensor_tensor(out=out, in0=O[u][:, 0:64], scalar=rs[:, u:u + 1], in1=out,
                                                               op0=ALU.mult, op1=ALU.add).then_inc(o_used, 1)


SIDES = 11
NL = 7
KEND, QIN, RAW = 7, 8, 8


def recur_prompt(nc, io, keep):
    ident, vnat, mqk, mknat, R, RN, decay, onat, hs, ones = (
        keep[k] for k in ("ident", "v_nat", "mqk", "mk_nat", "rows", "rows_cols", "decay", "onat", "hs", "ones"))
    zT = io["zT"]
    with ExitStack() as ctx:
        sb = lambda n, s, d=F32: ctx.enter_context(nc.sbuf_tensor(n, s, d))
        sem = semaphores(nc, ctx, "recur")
        zg = sb("zg", [P, 4, T])
        dd = sb("dd", [P, HP, 9, P])
        qd, kd = sb("qd", [P, HP, 9, P]), sb("kd", [P, HP, 9, P])
        lvl = sb("lvl", [P, 8, P], U32)
        pT = sb("pTg", [P, 4, P])
        kn = sb("kn", [P, HP, P])
        G = sb("Gst", [P, HP, 64])
        sel4 = sb("sel4", [4, 4, P])
        sel127 = sb("sel127", [P, P])
        maskT = sb("maskT", [P, 4, P])
        kst, qst = sb("kst", [P, HP, P]), sb("qst", [P, HP, P])
        wT = sb("wTm", [P, 4, P])
        pTm = sb("pTm", [P, 4, P])
        vaug = sb("vaug", [P, NCH, 4, 65])
        kw = sb("kw", [P, 4, 64])
        C = sb("Cst", [P, HP, 65])
        wcb = sb("wcb", [P, NCH, 16])
        bs = sb("bs", [P, 4, 65])
        carry = sb("carry", [1, 1])
        ps = [ctx.enter_context(nc.psum_tensor(f"pr{i}", [P, 512], F32)) for i in range(8)]
        sc = ps[0:2]
        og, kt, dl, pw, pb, pd = ps[2], ps[3], ps[3], ps[4], ps[6], ps[7]
        pa = ps[5]

        g_in, setup, setup2, lv_ready, diffs, factors, keyed, queried, raws = (
            sem("g_in2"), sem("setup"), sem("setup2"), sem("lv_ready"), sem("diffs"), sem("factors"), sem("keyed"),
            sem("queried"), sem("raws"))
        sc_done, sc_used, og_done, og_copied, kt_done, kt_copied, dl_done, g_updated = (
            sem("sc_done"), sem("sc_used"), sem("og_done"), sem("og_copied"), sem("kt_done"), sem("kt_copied"),
            sem("dl_done"), sem("g_updated"))
        side_done = sem("side_done")
        pw_done, w_ready, st_done, p_ready, num_done, h_ready, kw_ready, pd_done, c_updated, wc_done, wc_ready, states_out = (
            sem("pw_done"), sem("w_ready"), sem("st_done2"), sem("p_ready2"), sem("num_done"), sem("h_ready"),
            sem("kw_ready"), sem("pd_done"), sem("c_updated"), sem("wc_done"), sem("wc_ready"), sem("states_out"))

        with nc.Block() as block:

            @block.sync
            def _(sp):
                sp.dma_start(zg[:, :, :], zT[GQ:GQ + 4 * P, 0:T].rearrange("(j p) t -> p j t", p=P)).then_inc(g_in, 16)
                sp.wait_ge(g_updated, NCH)
                sp.wait_ge(c_updated, NCH)
                for h in range(4):
                    at = slice((h % 2) * 64, (h % 2) * 64 + 64)
                    sp.dma_start(io["out6"][0, 0, h, :, :], G[at, h // 2, :]).then_inc(states_out, 16)
                    sp.dma_start(io["out8"][0, 0, h, :, :], C[at, h // 2, 0:64]).then_inc(states_out, 16)
                    sp.dma_start(io["out10"][0, 0, h, :].rearrange("(d a) -> d a", a=1), C[at, h // 2, 64:65]).then_inc(states_out, 16)
                sp.wait_ge(states_out, 16 * 12)

            @block.gpsimd
            def _(pool):
                nc.gpsimd.memset(lvl[:, :, :].bitcast(I32), 1)
                nc.gpsimd.memset(pT[:, :, :], 0.0)
                nc.gpsimd.memset(G[:, :, :], 0.0)
                nc.gpsimd.memset(C[:, :, :], 0.0)
                nc.gpsimd.memset(vaug[:, :, :, :], 1.0)
                nc.gpsimd.memset(maskT[:, :, :], 0.0)
                nc.gpsimd.memset(sel127[:, :], 0.0)
                nc.gpsimd.memset(sel4[:, :, :], 0.0).then_inc(setup, 1)
                pool.wait_ge(setup, 1)
                nc.gpsimd.affine_select(out=maskT[:, :, :], in_=maskT[:, :, :], compare_op=ALU.is_ge, fill=-BIG,
                                        base=0, pattern=[[0, 4], [1, P]], channel_multiplier=-1)
                nc.gpsimd.affine_select(out=sel127[:, :], in_=sel127[:, :], compare_op=ALU.not_equal, fill=1.0,
                                        base=-(P - 1), pattern=[[0, P]], channel_multiplier=1)
                nc.gpsimd.affine_select(out=lvl[:, 7, :].bitcast(I32), in_=lvl[:, 7, :].bitcast(I32), compare_op=ALU.is_equal, fill=0,
                                        base=0, pattern=[[1, P]], channel_multiplier=-1)
                for l in range(NL):
                    half = 1 << l
                    v = lvl[:, l, :].bitcast(I32).rearrange("p (b h c) -> p b h c", h=2, c=half)
                    nc.gpsimd.memset(v[:, :, 0, :], 0)
                nc.gpsimd.drain()
                for l in range(NL):
                    half = 1 << l
                    v = lvl[:, l, :].bitcast(I32).rearrange("p (b h c) -> p b h c", h=2, c=half)[:, :, 1, :]
                    nb = P // (2 * half)
                    nc.gpsimd.affine_select(out=v, in_=v, compare_op=ALU.is_gt, fill=0,
                                            base=half, pattern=[[2 * half, nb], [0, half]], channel_multiplier=-1)
                nc.gpsimd.drain()
                for l in range(NL):
                    half = 1 << l
                    v = lvl[:, l, :].bitcast(I32).rearrange("p (b h c) -> p b h c", h=2, c=half)[:, :, 1, :]
                    nb = P // (2 * half)
                    nc.gpsimd.affine_select(out=v, in_=v, compare_op=ALU.is_ge, fill=0,
                                            base=0, pattern=[[-2 * half, nb], [0, half]], channel_multiplier=1)
                nc.gpsimd.affine_select(out=sel4[:, :, :], in_=sel4[:, :, :], compare_op=ALU.not_equal, fill=1.0,
                                        base=0, pattern=[[-1, 4], [0, P]], channel_multiplier=1)
                nc.gpsimd.tensor_copy(vaug[:, :, :, 0:64], vnat[:, :, 256:512].rearrange("p i (h e) -> p i h e", h=4)).then_inc(setup, 1)
                pool.wait_ge(g_in, 16)
                with pool.Fori(0, NCH) as c:
                    pool.wait_ge(factors, c + 1)
                    pool.wait_ge(og_done, c)
                    pool.wait_ge(kt_done, c)
                    nc.gpsimd.tensor_tensor(kd[:, :, 0:8, :],
                                            zg[:, 2:4, ds(c * P, P)].unsqueeze(2).broadcast_to([P, HP, 8, P]),
                                            dd[:, :, 0:8, :], ALU.mult).then_inc(keyed, 1)

            @block.scalar
            def _(act):
                act.wait_ge(setup, 2)
                act.wait_ge(wc_done, 1)
                nc.scalar.activation(wcb[:, :, :], ps[7][:, 0:P].rearrange("p (i k) -> p i k", i=NCH), ACT.Copy).then_inc(wc_ready, 1)
                act.wait_ge(lv_ready, 1)
                with act.Fori(0, NCH) as c:
                    act.wait_ge(og_done, c)
                    act.wait_ge(num_done, c)
                    for dst, src in ((qd[:, :, RAW, :], zg[:, 0:2, :]), (kd[:, :, RAW, :], zg[:, 2:4, :]),
                                     (qst[:, :, :], mqk[:, 0:2, :]), (kst[:, :, :], mqk[:, 2:4, :])):
                        last = nc.scalar.activation(dst, src[:, :, ds(c * P, P)], ACT.Copy)
                    last.then_inc(raws, 1)
                    act.wait_ge(diffs, c + 1)
                    nc.scalar.activation(dd[:, :, :, :], dd[:, :, :, :], ACT.Abs)
                    nc.scalar.drain()
                    nc.scalar.activation(dd[:, :, :, :], dd[:, :, :, :], ACT.Exp, scale=-1.0 / 16.0).then_inc(factors, 1)
                    act.wait_ge(pw_done, c + 1)
                    for h in range(4):
                        last = nc.scalar.activation(wT[:, h, :], pw[:, h * P:(h + 1) * P], ACT.Exp, bias=RN[:, c, 4 + h:5 + h])
                    last.then_inc(w_ready, 1)
                    act.wait_ge(kt_done, c + 1)
                    nc.scalar.activation(kn[:, :, :], kt[:, 0:2 * P].rearrange("p (k c) -> p k c", k=2), ACT.Copy).then_inc(kt_copied, 1)
                    act.wait_ge(og_done, c + 1)
                    nc.scalar.activation(onat[:, c, 0:256], og[:, 0:256], ACT.Copy).then_inc(og_copied, 1)

            @block.tensor
            def _(pe):
                pe.wait_ge(setup, 2)
                nc.tensor.matmul(ps[7][:, 0:P], sel127[:, :], RN[:, :, :].rearrange("p i k -> p (i k)"), start=True, stop=True).then_inc(wc_done, 1)
                pe.wait_ge(wc_ready, 1)
                with pe.Fori(0, NCH) as c:
                    sides = [0]

                    def by_side(product):
                        for h in (0, 2):
                            last = product(h, slice(0, 64))
                        last.then_inc(side_done, 1)
                        sides[0] += 1
                        pe.wait_ge(side_done, SIDES * c + sides[0])
                        for h in (1, 3):
                            last = product(h, slice(64, 128))
                        return last

                    pe.wait_ge(w_ready, c)
                    nc.tensor.matmul(pw[:, :], ident[:, :], maskT[:, :, :].rearrange("p h t -> p (h t)"), start=True, stop=False)
                    for h in range(4):
                        last = nc.tensor.matmul(pw[:, h * P:(h + 1) * P], sel4[:, h, :], R[0:4, ds(c * P, P)], start=False, stop=h == 3)
                    last.then_inc(pw_done, 1)
                    pe.wait_ge(raws, c + 1)
                    pe.wait_ge(h_ready, c)
                    by_side(lambda h, at: nc.tensor.matmul(pb[:, h * P:(h + 1) * P], kst[at, h // 2, :], qst[at, h // 2, :],
                                                           start=True, stop=True)).then_inc(st_done, 1)
                    pe.wait_ge(keyed, c + 1)
                    pe.wait_ge(queried, c + 1)
                    for l in range(NL + 1):
                        pe.wait_ge(sc_used, 8 * c + l - 1) if l >= 2 else pe.wait_ge(sc_used, 8 * c)
                        ql = RAW if l == NL else l
                        by_side(lambda h, at: nc.tensor.matmul(sc[l % 2][:, h * P:(h + 1) * P], kd[at, h // 2, ql, :],
                                                               qd[at, h // 2, ql, :], start=True, stop=True)).then_inc(sc_done, 1)
                    pe.wait_ge(g_updated, c)
                    for hp in range(HP):
                        last = nc.tensor.transpose(kt[:, hp * P:(hp + 1) * P], kd[:, hp, KEND, :], ident[:, :])
                    last.then_inc(kt_done, 1)
                    pe.wait_ge(p_ready, c + 1)
                    for h in range(4):
                        nc.tensor.matmul(pa[:, h * 65:(h + 1) * 65], pTm[:, h, :], vaug[:, c, h, :], start=True, stop=True)
                    pe.wait_ge(c_updated, c)
                    by_side(lambda h, at: nc.tensor.matmul(pb[:, h * 65:(h + 1) * 65], qst[at, h // 2, :], C[at, h // 2, :],
                                                           start=True, stop=True)).then_inc(num_done, 1)
                    pe.wait_ge(kw_ready, c + 1)
                    for hp in range(HP):
                        last = nc.tensor.matmul(pd[:, hp * 130:(hp + 1) * 130], kw[:, 2 * hp:2 * hp + 2, :].rearrange("p h d -> p (h d)"),
                                                vaug[:, c, 2 * hp:2 * hp + 2, :].rearrange("p h d -> p (h d)"), start=True, stop=True)
                    last.then_inc(pd_done, 1)
                    pe.wait_ge(sc_used, 8 * c + 8)
                    pe.wait_ge(og_copied, c)
                    for h in range(4):
                        nc.tensor.matmul(og[:, h * 64:(h + 1) * 64], pT[:, h, :], vnat[:, c, h * 64:(h + 1) * 64], start=(h == 0), stop=False)
                    by_side(lambda h, at: nc.tensor.matmul(og[:, h * 64:(h + 1) * 64], qd[at, h // 2, KEND, :], G[at, h // 2, :],
                                                           start=False, stop=(h == 3))).then_inc(og_done, 1)
                    pe.wait_ge(kt_copied, c + 1)
                    for hp in range(HP):
                        last = nc.tensor.matmul(dl[:, 256 + hp * P:256 + (hp + 1) * P], kn[:, hp, :], vnat[:, c, hp * P:(hp + 1) * P],
                                                start=True, stop=True)
                    last.then_inc(dl_done, 1)

            @block.vector
            def _(dve):
                dve.wait_ge(g_in, 16)
                dve.wait_ge(setup, 2)
                dve.wait_ge(wc_ready, 1)
                nc.vector.tensor_scalar(zg[:, 0:2, :], zg[:, 0:2, :], HD ** -0.5, None, ALU.mult).then_inc(lv_ready, 1)
                nc.vector.drain()
                with dve.Fori(0, NCH) as c:
                    b = decay[:, :, ds(c * P, P)]
                    dve.wait_ge(keyed, c)
                    dve.wait_ge(g_updated, c)
                    for l in range(NL):
                        half = 1 << l
                        nb = P // (2 * half)
                        blocks = b.rearrange("p k (b w) -> p k b w", w=2 * half)
                        nc.vector.tensor_tensor(dd[:, :, l, :].rearrange("p k (b w) -> p k b w", w=2 * half), blocks,
                                                blocks[:, :, :, half - 1:half].broadcast_to([P, HP, nb, 2 * half]), ALU.subtract)
                    nc.vector.tensor_tensor(dd[:, :, KEND, :], b, b[:, :, P - 1:P].broadcast_to([P, HP, P]), ALU.subtract)
                    nc.vector.tensor_copy(dd[:, :, QIN, :], b).then_inc(diffs, 1)
                    dve.wait_ge(w_ready, c + 1)
                    dve.wait_ge(st_done, c + 1)
                    nc.vector.tensor_tensor(pTm[:, :, :], pb[:, :].rearrange("p (h t) -> p h t", h=4), wT[:, :, :], ALU.mult).then_inc(p_ready, 1)
                    nc.vector.tensor_tensor(kw[:, :, :], mknat[:, c, :].rearrange("p (h d) -> p h d", h=4),
                                            wT[:, :, P - 1:P].broadcast_to([P, 4, 64]), ALU.mult).then_inc(kw_ready, 1)
                    dve.wait_ge(factors, c + 1)
                    q = zg[:, 0:2, ds(c * P, P)]
                    nc.vector.tensor_tensor(qd[:, :, 0:NL, :], q.unsqueeze(2).broadcast_to([P, HP, NL, P]), dd[:, :, 0:NL, :], ALU.mult)
                    nc.vector.tensor_tensor(qd[:, :, KEND, :], q, dd[:, :, QIN, :], ALU.mult).then_inc(queried, 1)
                    for l in range(NL + 1):
                        nc.vector.drain()
                        if l == 0:
                            dve.wait_ge(og_done, c)
                        dve.wait_ge(sc_done, 8 * c + l + 1)
                        nc.vector.tensor_copy(carry[0:1, 0:1], wcb[0:1, 0, 0:1])
                        nc.vector.copy_predicated(pT[:, :, :], lvl[:, l, :].unsqueeze(1).broadcast_to([P, 4, P]),
                                                  sc[l % 2][:, :].rearrange("p (h t) -> p h t", h=4)).then_inc(sc_used, 1)
                    dve.wait_ge(num_done, c + 1)
                    nc.vector.tensor_tensor(bs[:, :, :], pb[:, 0:260].rearrange("p (h e) -> p h e", h=4),
                                            RN[:, c, 8:12].unsqueeze(2).broadcast_to([P, 4, 65]), ALU.mult)
                    nc.vector.drain()
                    nc.vector.tensor_tensor(hs[:, c, :, :], pa[:, 0:260].rearrange("p (h e) -> p h e", h=4), bs[:, :, :], ALU.add).then_inc(h_ready, 1)
                    dve.wait_ge(pd_done, c + 1)
                    for h in range(4):
                        at = slice((h % 2) * 64, (h % 2) * 64 + 64)
                        off = (h // 2) * 130 + (h % 2) * 65
                        last = nc.vector.scalar_tensor_tensor(out=C[at, h // 2, :], in0=C[at, h // 2, :], scalar=wcb[at, c, 8 + h:9 + h],
                                                              in1=pd[at, off:off + 65], op0=ALU.mult, op1=ALU.add)
                    last.then_inc(c_updated, 1)
                    dve.wait_ge(dl_done, c + 1)
                    for h in range(4):
                        at = slice((h % 2) * 64, (h % 2) * 64 + 64)
                        off = 256 + (h // 2) * P + (h % 2) * 64
                        last = nc.vector.scalar_tensor_tensor(out=G[at, h // 2, :], in0=G[at, h // 2, :], scalar=dd[at, h // 2, QIN, P - 1:P],
                                                              in1=dl[at, off:off + 64], op0=ALU.mult, op1=ALU.add)
                    last.then_inc(g_updated, 1)


NR = 8 * NS
L = 2048
NG16 = L // 16
NBD = NG16 - 1
WIN_ROWS = 512


def decode_recurrences(nc, io, keep):
    ident, eps, ones, mixS, mqd, dcd = (keep[k] for k in ("ident", "eps", "ones", "mixS", "mqk_dec", "decay_dec"))
    zT, zS = io["zT"], io["zS"]
    with ExitStack() as ctx:
        sb = lambda n, s, d=F32: ctx.enter_context(nc.sbuf_tensor(n, s, d))
        sem = semaphores(nc, ctx, "step")
        qk = sb("qkd", [P, 4, NS])
        vb, kv, Gs = sb("vb", [P, HP, NS, 65]), sb("kvd", [P, HP, NS, 65]), sb("Gs", [P, HP, NS, 64])
        vm, Cs = sb("vm", [P, HP, NS, 65]), sb("Cs", [P, HP, NS, 65])
        m0, gi, gf = sb("m0", [P, HP, NS]), sb("gid", [P, HP, NS]), sb("gfd", [P, HP, NS])
        gb = sb("gbd", [P, 2, HP])
        lf, mt, wc, wl, em = (sb(n, [P, HP, NS]) for n in ("lf", "mt", "wcd", "wld", "emd"))
        qbd, qbm = sb("qbd", [P, HP, NS, 2]), sb("qbm", [P, HP, NS, 2])
        qn, blk = sb("qn", [P, HP, NS]), sb("blkd", [P, P])
        o, sqo, em64, dn, nd = (sb(n, [64, 2, HP, NS]) for n in ("od", "sqo", "em64", "dnd", "ndd"))
        ps = [ctx.enter_context(nc.psum_tensor(f"pdr{i}", [P, 512], F32)) for i in range(6)]
        loads, zeroed, act_done, dve_done, pe_done, stored = (sem("d_loads"), sem("d_zeroed"), sem("d_act"), sem("d_dve"), sem("d_pe"),
                                                              sem("d_stored"))
        G_IN, G_FACT, G_STATE, G_OUT, G_SQ, G_SUM, G_RT, G_NORM = (sem(f"dg{n}") for n in range(8))
        F_ABS, M_T, M_EXP, C_STATE, M_OUT, M_DEN, M_DIV, M_SQ, M_SUM, M_RT = (sem(f"dm{n}") for n in range(10))
        NLOAD = 1 + 4 * 3 + 4 * 3 + 2 + 8
        view = lambda a: a.rearrange("p k s -> p (k s)")

        with nc.Block() as block:

            @block.gpsimd
            def _(pool):
                nc.gpsimd.memset(vm[:, :, :, 64:65], 1.0)
                nc.gpsimd.memset(qbd[:, :, :, :], 0.0)
                nc.gpsimd.memset(qbm[:, :, :, :], 0.0)
                nc.gpsimd.memset(blk[:, :], 0.0)
                nc.gpsimd.drain()
                nc.gpsimd.memset(blk[0:64, 0:64], 1.0)
                nc.gpsimd.drain()
                nc.gpsimd.memset(blk[64:128, 64:128], 1.0).then_inc(zeroed, 1)

            @block.sync
            def _(sp):
                def load(dst, src):
                    sp.dma_start(dst, src).then_inc(loads, 16)

                load(qk[:, :, :], zT[GQ:GQ + 4 * P, T:TT].rearrange("(j p) s -> p j s", p=P))
                for h in range(4):
                    at, hp = slice((h % 2) * 64, (h % 2) * 64 + 64), h // 2
                    load(vb[at, hp, :, 0:64], zS[:, GV + h * 64:GV + h * 64 + 64].unsqueeze(0).broadcast_to([64, NS, 64]))
                    load(Gs[at, hp, :, :], io["state_gla"][0, :, h, :, :].rearrange("s d e -> d s e"))
                    load(vm[at, hp, :, 0:64], zS[:, MV + h * 64:MV + h * 64 + 64].unsqueeze(0).broadcast_to([64, NS, 64]))
                    load(Cs[at, hp, :, 0:64], io["state_mlstm_c"][0, :, h, :, :].rearrange("s d e -> d s e"))
                    load(Cs[at, hp, :, 64:65], io["state_mlstm_n"][0, :, h, :].rearrange("s (d a) -> d s a", a=1))
                    load(m0[at, hp, :], io["state_mlstm_m"][0, :, h:h + 1].rearrange("s a -> a s").broadcast_to([64, NS]))
                    load(gi[at, hp, :], zT[MI + h:MI + h + 1, T:TT].broadcast_to([64, NS]))
                    load(gf[at, hp, :], zT[MF + h:MF + h + 1, T:TT].broadcast_to([64, NS]))
                for h2 in range(2):
                    load(gb[h2 * 64:h2 * 64 + 64, :, :],
                         io["ml_gate_b"][0:1, :, :].rearrange("l k (a b) -> l k a b", b=2)[:, :, :, h2].broadcast_to([64, 2, HP]))
                sp.wait_ge(G_STATE, 1)
                sp.wait_ge(C_STATE, 1)
                for h in range(4):
                    at, hp = slice((h % 2) * 64, (h % 2) * 64 + 64), h // 2
                    sp.dma_start(io["out7"][0, :, h, :, :].rearrange("s d e -> d s e"), Gs[at, hp, :, :]).then_inc(stored, 16)
                    sp.dma_start(io["out9"][0, :, h, :, :].rearrange("s d e -> d s e"), Cs[at, hp, :, 0:64]).then_inc(stored, 16)
                    sp.dma_start(io["out11"][0, :, h, :].rearrange("s (d a) -> d s a", a=1), Cs[at, hp, :, 64:65]).then_inc(stored, 16)
                    sp.dma_start(io["out13"][0, :, h:h + 1].rearrange("s a -> a s"), mt[(h % 2) * 64:(h % 2) * 64 + 1, hp, :]).then_inc(stored, 16)
                sp.wait_ge(stored, 16 * 16)

            @block.scalar
            def _(act):
                act.wait_ge(loads, 16 * (1 + 4 * 8 + 2))
                nc.scalar.activation(dcd[:, :, :], dcd[:, :, :], ACT.Exp, scale=1.0 / 16.0).then_inc(G_FACT, 1)
                for hp in range(HP):
                    last = nc.scalar.activation(lf[:, hp, :], gf[:, hp, :], ACT.Abs, bias=gb[:, 1, hp:hp + 1])
                nc.scalar.drain()
                nc.scalar.activation(lf[:, :, :], lf[:, :, :], ACT.Exp, scale=-1.0)
                nc.scalar.drain()
                nc.scalar.activation(lf[:, :, :], lf[:, :, :], ACT.Ln, bias=1.0).then_inc(F_ABS, 1)
                act.wait_ge(M_T, 1)
                nc.scalar.activation(wc[:, :, :], wc[:, :, :], ACT.Exp)
                nc.scalar.activation(wl[:, :, :], wl[:, :, :], ACT.Exp)
                nc.scalar.activation(em[:, :, :], mt[:, :, :], ACT.Exp, scale=-1.0)
                nc.scalar.drain()
                for h2 in range(2):
                    last = nc.scalar.activation(em64[:, h2, :, :], em[h2 * 64:h2 * 64 + 64, :, :], ACT.Copy)
                last.then_inc(M_EXP, 1)
                act.wait_ge(G_OUT, 1)
                nc.scalar.activation(o[:, :, :, :], ps[0][0:64, 0:32].rearrange("p (a k s) -> p a k s", a=2, k=2), ACT.Copy)
                nc.scalar.activation(sqo[:, :, :, :], ps[0][0:64, 0:32].rearrange("p (a k s) -> p a k s", a=2, k=2), ACT.Square).then_inc(G_SQ, 1)
                act.wait_ge(G_SUM, 1)
                nc.scalar.activation(sqo[:, :, :, :], ps[1][0:64, 0:32].rearrange("p (a k s) -> p a k s", a=2, k=2), ACT.Sqrt,
                                     scale=1.0 / HD, bias=eps[0:64, :]).then_inc(G_RT, 1)
                act.wait_ge(M_DIV, 1)
                act.wait_ge(G_NORM, 1)
                nc.scalar.activation(sqo[:, :, :, :], o[:, :, :, :], ACT.Square).then_inc(M_SQ, 1)
                act.wait_ge(M_SUM, 1)
                nc.scalar.activation(sqo[:, :, :, :], ps[4][0:64, 0:32].rearrange("p (a k s) -> p a k s", a=2, k=2), ACT.Sqrt,
                                     scale=1.0 / HD, bias=eps[0:64, :]).then_inc(M_RT, 1)

            @block.vector
            def _(dve):
                dve.wait_ge(loads, 16 * (1 + 4 * 8 + 2))
                dve.wait_ge(zeroed, 1)
                dve.wait_ge(G_FACT, 1)
                bc = lambda a, n: a.unsqueeze(3).broadcast_to([P, HP, NS, n])
                for h2 in range(2):
                    at = slice(h2 * 64, h2 * 64 + 64)
                    nc.vector.tensor_scalar(qbd[at, :, :, h2], qk[at, 0:2, :], HD ** -0.5, None, ALU.mult)
                    nc.vector.tensor_copy(qbm[at, :, :, h2], mqd[at, 0:2, :])
                nc.vector.tensor_tensor(Gs[:, :, :, :], Gs[:, :, :, :], bc(dcd[:, :, :], 64), ALU.mult)
                nc.vector.tensor_tensor(kv[:, :, :, 0:64], vb[:, :, :, 0:64], bc(qk[:, 2:4, :], 64), ALU.mult)
                nc.vector.drain()
                nc.vector.tensor_tensor(Gs[:, :, :, :], Gs[:, :, :, :], kv[:, :, :, 0:64], ALU.add).then_inc(G_STATE, 1)
                nc.vector.drain()
                dve.wait_ge(F_ABS, 1)
                for hp in range(HP):
                    nc.vector.tensor_scalar(gf[:, hp, :], gf[:, hp, :], gb[:, 1, hp:hp + 1], 0.0, ALU.add, ALU.min)
                    nc.vector.tensor_scalar(gi[:, hp, :], gi[:, hp, :], gb[:, 0, hp:hp + 1], None, ALU.add)
                nc.vector.drain()
                nc.vector.tensor_tensor(lf[:, :, :], gf[:, :, :], lf[:, :, :], ALU.subtract)
                nc.vector.drain()
                nc.vector.tensor_tensor(lf[:, :, :], lf[:, :, :], m0[:, :, :], ALU.add)
                nc.vector.drain()
                nc.vector.tensor_tensor(mt[:, :, :], lf[:, :, :], gi[:, :, :], ALU.max)
                nc.vector.drain()
                nc.vector.tensor_tensor(wc[:, :, :], lf[:, :, :], mt[:, :, :], ALU.subtract)
                nc.vector.tensor_tensor(wl[:, :, :], gi[:, :, :], mt[:, :, :], ALU.subtract).then_inc(M_T, 1)
                dve.wait_ge(M_EXP, 1)
                nc.vector.tensor_tensor(wl[:, :, :], wl[:, :, :], mqd[:, 2:4, :], ALU.mult)
                nc.vector.tensor_tensor(Cs[:, :, :, :], Cs[:, :, :, :], bc(wc[:, :, :], 65), ALU.mult)
                nc.vector.drain()
                nc.vector.tensor_tensor(kv[:, :, :, :], vm[:, :, :, :], bc(wl[:, :, :], 65), ALU.mult)
                nc.vector.drain()
                nc.vector.tensor_tensor(Cs[:, :, :, :], Cs[:, :, :, :], kv[:, :, :, :], ALU.add)
                nc.vector.drain()
                nc.vector.tensor_tensor(qn[:, :, :], mqd[:, 0:2, :], Cs[:, :, :, 64], ALU.mult).then_inc(C_STATE, 1)
                dve.wait_ge(G_RT, 1)
                nc.vector.reciprocal(sqo[:, :, :, :], sqo[:, :, :, :])
                nc.vector.drain()
                for h2 in range(2):
                    last = nc.vector.tensor_tensor(mixS[h2 * 64:h2 * 64 + 64, 0:2, :], o[:, h2, :, :], sqo[:, h2, :, :], ALU.mult)
                last.then_inc(G_NORM, 1)
                dve.wait_ge(M_DEN, 1)
                den = ps[3][0:64, 0:32].rearrange("p (a k s) -> p a k s", a=2, k=2)
                nc.vector.tensor_copy(dn[:, :, :, :], den)
                nc.vector.tensor_scalar(nd[:, :, :, :], den, -1.0, None, ALU.mult)
                nc.vector.drain()
                nc.vector.tensor_tensor(nd[:, :, :, :], nd[:, :, :, :], dn[:, :, :, :], ALU.max)
                nc.vector.drain()
                nc.vector.tensor_tensor(nd[:, :, :, :], nd[:, :, :, :], em64[:, :, :, :], ALU.max)
                nc.vector.drain()
                nc.vector.reciprocal(nd[:, :, :, :], nd[:, :, :, :])
                nc.vector.drain()
                nc.vector.tensor_tensor(o[:, :, :, :], ps[2][0:64, 0:32].rearrange("p (a k s) -> p a k s", a=2, k=2), nd[:, :, :, :],
                                        ALU.mult).then_inc(M_DIV, 1)
                dve.wait_ge(M_RT, 1)
                nc.vector.reciprocal(sqo[:, :, :, :], sqo[:, :, :, :])
                nc.vector.drain()
                for h2 in range(2):
                    nc.vector.tensor_tensor(mixS[h2 * 64:h2 * 64 + 64, 6:8, :], o[:, h2, :, :], sqo[:, h2, :, :], ALU.mult)

            @block.tensor
            def _(pe):
                out = lambda bank: bank[0:64, 0:32].rearrange("p (a k s) -> p k s a", a=2, k=2)
                pe.wait_ge(G_STATE, 1)
                for hp in range(HP):
                    for s in range(NS):
                        last = nc.tensor.matmul(out(ps[0])[:, hp, s, :], Gs[:, hp, s, :], qbd[:, hp, s, :], start=True, stop=True)
                last.then_inc(G_OUT, 1)
                pe.wait_ge(G_SQ, 1)
                nc.tensor.matmul(ps[1][0:64, 0:32], ones[0:64, 0:64], sqo[:, :, :, :].rearrange("p a k s -> p (a k s)"),
                                 start=True, stop=True).then_inc(G_SUM, 1)
                pe.wait_ge(C_STATE, 1)
                for hp in range(HP):
                    for s in range(NS):
                        nc.tensor.matmul(out(ps[2])[:, hp, s, :], Cs[:, hp, s, 0:64], qbm[:, hp, s, :], start=True, stop=True)
                for h2 in range(2):
                    last = nc.tensor.matmul(ps[3][0:64, h2 * 16:h2 * 16 + 16], blk[:, h2 * 64:h2 * 64 + 64],
                                            qn[:, :, :].rearrange("p k s -> p (k s)"), start=True, stop=True)
                last.then_inc(M_DEN, 1)
                pe.wait_ge(M_SQ, 1)
                nc.tensor.matmul(ps[4][0:64, 0:32], ones[0:64, 0:64], sqo[:, :, :, :].rearrange("p a k s -> p (a k s)"),
                                 start=True, stop=True).then_inc(M_SUM, 1)



def decode_queries(nc, io, keep, at):
    with ExitStack() as ctx:
        sb = lambda n, s, d=F32: ctx.enter_context(nc.sbuf_tensor(n, s, d))
        sem = semaphores(nc, ctx, "queries")
        q2, gbias = sb("q2", [P, 4, NS]), sb("gbias2", [NR, 3])
        loads, zeroed, gated = sem("q_loads"), sem("q_zeroed"), sem("q_gated")
        qbd, q64, gates, rows_of, of_rows, kwn, ksn, v_new = (
            at[k] for k in ("qbd", "q64", "gates", "rows_of", "of_rows", "kwn", "ksn", "v_new"))
        with nc.Block() as block:

            @block.sync
            def _(sp):
                def load(dst, src):
                    sp.dma_start(dst, src).then_inc(loads, 16)

                for h in range(2):
                    rows = slice(h * 64, h * 64 + 64)
                    load(q2[rows, :, :], io["qkT"][h * 256:h * 256 + 256, T:TT].rearrange("(g d) s -> d g s", d=64))
                    load(ksn[:, :, h], io["qkT"][4 * P + h * 64:4 * P + h * 64 + 64, T:TT])
                    load(kwn[:, :, h], io["qkT"][5 * P + h * 64:5 * P + h * 64 + 64, T:TT])
                for slot, tile in ((0, 7), (1, 9)):
                    for s in range(NS):
                        load(v_new[2 * s:2 * s + 2, slot, :],
                             io["zS"][s, NQ + tile * P:NQ + (tile + 1) * P].rearrange("(h d) -> h d", h=2))
                for s in range(NS):
                    load(gates[8 * s:8 * s + 8, :], io["zS"][s, NG:NG + 24].rearrange("(r b) -> r b", b=3))
                    load(gbias[8 * s:8 * s + 8, :], io["nsa_gate_b"][0, :].rearrange("(r b) -> r b", b=3))

            @block.gpsimd
            def _(pool):
                nc.gpsimd.memset(qbd[:, :, :], 0.0)
                nc.gpsimd.memset(rows_of[:, :], 1.0)
                nc.gpsimd.memset(of_rows[:, :], 1.0).then_inc(zeroed, 1)
                pool.wait_ge(zeroed, 1)
                nc.gpsimd.affine_select(out=rows_of[:, :], in_=rows_of[:, :], compare_op=ALU.is_ge, fill=0.0,
                                        base=0, pattern=[[-4, 16]], channel_multiplier=1)
                nc.gpsimd.affine_select(out=of_rows[:, :], in_=of_rows[:, :], compare_op=ALU.is_ge, fill=0.0,
                                        base=0, pattern=[[1, NR]], channel_multiplier=-4)
                nc.gpsimd.drain()
                nc.gpsimd.affine_select(out=rows_of[:, :], in_=rows_of[:, :], compare_op=ALU.is_ge, fill=0.0,
                                        base=3, pattern=[[4, 16]], channel_multiplier=-1)
                nc.gpsimd.affine_select(out=of_rows[:, :], in_=of_rows[:, :], compare_op=ALU.is_ge, fill=0.0,
                                        base=3, pattern=[[-1, NR]], channel_multiplier=4).then_inc(zeroed, 1)

            @block.vector
            def _(dve):
                dve.wait_ge(loads, 16 * (6 + 4 * NS))
                dve.wait_ge(zeroed, 2)
                for h in range(2):
                    rows = slice(h * 64, h * 64 + 64)
                    nc.vector.tensor_copy(qbd[rows, :, h * 4:h * 4 + 4], q2[rows, :, :].rearrange("p g s -> p s g"))
                    nc.vector.tensor_copy(q64[:, :].rearrange("p (s h g) -> p s h g", h=2, g=4)[:, :, h, :],
                                          q2[rows, :, :].rearrange("p g s -> p s g"))
                nc.vector.tensor_tensor(gates[:, :], gates[:, :], gbias[:, :], ALU.add).then_inc(gated, 1)

            @block.scalar
            def _(act):
                act.wait_ge(gated, 1)
                nc.scalar.activation(gates[:, :], gates[:, :], ACT.Sigmoid)


def decode_window(nc, io, keep, at):
    ident = keep["ident"]
    qbd, q64, gates, rows_of, kwn, v_new, oT = (at[k] for k in ("qbd", "q64", "gates", "rows_of", "kwn", "v_new", "oT"))
    with ExitStack() as ctx:
        sb = lambda n, s, d=F32: ctx.enter_context(nc.sbuf_tensor(n, s, d))
        sem = semaphores(nc, ctx, "window")
        win = sb("win_rows", [P, NS, 4, 256])
        kT = sb("kTw", [P, 2, 4 * P])
        sT = sb("sTw", [P, 4, NR])
        S = sb("Sw", [NR, WIN_ROWS + 1])
        pT = sb("pTw", [P, 4, NR])
        t16, nw = sb("t16", [NR, 16]), sb("nw", [NR, 1])
        den, mx = sb("denw", [NR, 1]), sb("mxw", [NR, 1])
        pg, pgT = sb("pg", [NR, 16]), sb("pgT", [16, NR])
        ps = [ctx.enter_context(nc.psum_tensor(f"pw{i}", [P, 512], F32)) for i in range(8)]
        win_in, kt_done, kt_copied, sc_done, st_copied, s_done, new_done, mx_ready, p_ready, scaled, pt_done, pt_copied, o_done = (
            sem(n) for n in ("win_in", "kt_done", "kt_copied", "wsc_done", "wst_copied", "ws_done", "new_done", "mx_ready", "wp_ready",
                             "scaled", "wpt_done", "wpt_copied", "wo_done"))

        with nc.Block() as block:

            @block.sync
            def _(sp):
                sp.dma_start(win[:, :, :, :].rearrange("p s c x -> p s (c x)"),
                             io["cache_nsa_win"].rearrange("l s (p c) k h d -> p (l s) (c k h d)", c=4)).then_inc(win_in, 16)

            @block.tensor
            def _(pe):
                pe.wait_ge(win_in, 16)
                for s in range(NS):
                    if s >= 2:
                        pe.wait_ge(kt_copied, s - 1)
                    for c in range(4):
                        last = nc.tensor.transpose(ps[s % 2][:, c * P:(c + 1) * P], win[:, s, c, 0:P], ident[:, :])
                    last.then_inc(kt_done, 1)
                    if s:
                        pe.wait_ge(kt_copied, s)
                        for c in range(4):
                            nc.tensor.matmul(ps[2][:, c * NR + (s - 1) * 8:c * NR + s * 8], kT[:, (s - 1) % 2, c * P:(c + 1) * P],
                                             qbd[:, s - 1, :], start=True, stop=True).then_inc(sc_done, 1)
                pe.wait_ge(kt_copied, NS)
                for c in range(4):
                    nc.tensor.matmul(ps[2][:, c * NR + (NS - 1) * 8:c * NR + NS * 8], kT[:, (NS - 1) % 2, c * P:(c + 1) * P],
                                     qbd[:, NS - 1, :], start=True, stop=True).then_inc(sc_done, 1)
                nc.tensor.matmul(ps[3][0:NR, 0:16], q64[:, :], kwn[:, :, :].rearrange("p s h -> p (s h)"), start=True, stop=True).then_inc(new_done, 1)
                pe.wait_ge(st_copied, 1)
                for c in range(4):
                    last = nc.tensor.transpose(ps[4][0:NR, c * P:(c + 1) * P], sT[:, c, :], ident[:, :])
                last.then_inc(s_done, 1)
                pe.wait_ge(scaled, 1)
                for c in range(4):
                    last = nc.tensor.transpose(ps[5][:, c * NR:(c + 1) * NR], S[:, c * P:(c + 1) * P], ident[0:NR, 0:NR])
                last.then_inc(pt_done, 1)
                nc.tensor.transpose(ps[6][0:16, 0:NR], pg[:, :], ident[0:NR, 0:NR]).then_inc(pt_done, 1)
                pe.wait_ge(pt_copied, 2)
                for s in range(NS):
                    for c in range(4):
                        nc.tensor.matmul(ps[7][:, s * 8:s * 8 + 8], win[:, s, c, P:2 * P], pT[:, c, s * 8:s * 8 + 8],
                                         start=(c == 0), stop=(c == 3))
                nc.tensor.matmul(ps[0][0:64, 0:NR], v_new[:, 1, :], pgT[:, :], start=True, stop=True).then_inc(o_done, 1)

            @block.scalar
            def _(act):
                for s in range(NS):
                    act.wait_ge(kt_done, s + 1)
                    if s >= 2:
                        act.wait_ge(sc_done, 4 * (s - 1))
                    nc.scalar.activation(kT[:, s % 2, :], ps[s % 2][:, :], ACT.Copy).then_inc(kt_copied, 1)
                act.wait_ge(sc_done, 4 * NS)
                nc.scalar.activation(sT[:, :, :], ps[2][:, 0:4 * NR].rearrange("p (c r) -> p c r", c=4), ACT.Copy).then_inc(st_copied, 1)
                act.wait_ge(mx_ready, 1)
                nc.scalar.activation(S[:, :], S[:, :], ACT.Exp, bias=mx[:, :], accum_out=den[:, :]).then_inc(p_ready, 1)
                act.wait_ge(pt_done, 2)
                nc.scalar.activation(pT[:, :, :], ps[5][:, 0:4 * NR].rearrange("p (c r) -> p c r", c=4), ACT.Copy).then_inc(pt_copied, 1)
                nc.scalar.activation(pgT[:, :], ps[6][0:16, 0:NR], ACT.Copy).then_inc(pt_copied, 1)

            @block.vector
            def _(dve):
                dve.wait_ge(new_done, 1)
                nc.vector.tensor_tensor(t16[:, :], ps[3][0:NR, 0:16], rows_of[:, :], ALU.mult)
                nc.vector.drain()
                nc.vector.reduce_sum(S[:, WIN_ROWS:WIN_ROWS + 1], t16[:, :], AX.X)
                dve.wait_ge(s_done, 1)
                nc.vector.tensor_copy(S[:, 0:WIN_ROWS], ps[4][0:NR, :])
                nc.vector.drain()
                nc.vector.memset(S[:, 0:1], -BIG)
                nc.vector.drain()
                nc.vector.reduce_max(mx[:, :], S[:, :], AX.X)
                nc.vector.drain()
                nc.vector.tensor_scalar(mx[:, :], mx[:, :], -1.0, None, ALU.mult).then_inc(mx_ready, 1)
                dve.wait_ge(p_ready, 1)
                nc.vector.tensor_scalar(den[:, :], den[:, :], 1e-30, None, ALU.max)
                nc.vector.drain()
                nc.vector.reciprocal(den[:, :], den[:, :])
                nc.vector.drain()
                nc.vector.tensor_tensor(den[:, :], den[:, :], gates[:, WIN:WIN + 1], ALU.mult)
                nc.vector.drain()
                nc.vector.tensor_scalar(S[:, :], S[:, :], den[:, :], None, ALU.mult)
                nc.vector.drain()
                nc.vector.tensor_scalar(pg[:, :], rows_of[:, :], S[:, WIN_ROWS:WIN_ROWS + 1], None, ALU.mult).then_inc(scaled, 1)
                dve.wait_ge(o_done, 1)
                for h in range(2):
                    rows = lambda a: a.rearrange("p (s h g) -> p s h g", h=2, g=4)[:, :, h, :]
                    nc.vector.tensor_copy(rows(oT[:, :]), rows(ps[7][h * 64:h * 64 + 64, 0:NR]))
                nc.vector.drain()
                nc.vector.tensor_tensor(oT[:, :], ps[0][0:64, 0:NR], oT[:, :], ALU.add)


def decode_blocks(nc, io, keep, at):
    ident, eps, ones, g4, cbias, w2, b2, mixS = (keep[k] for k in ("ident", "eps", "ones", "g4", "cbias", "w2", "b2", "mixS"))
    qbd, q64, gates, rows_of, of_rows, ksn, v_new, oT = (
        at[k] for k in ("qbd", "q64", "gates", "rows_of", "of_rows", "ksn", "v_new", "oT"))
    cache = io["cache_nsa_kv"].rearrange("l n (g r) k h d -> (l n g) (r k h d)", r=8)
    NPAGE = L // 128
    with ExitStack() as ctx:
        sb = lambda n, s, d=F32: ctx.enter_context(nc.sbuf_tensor(n, s, d))
        sem = semaphores(nc, ctx, "blocks")
        rows = sb("page_rows", [P, 2, 8 * 512])
        kv = [rows[:, half, :].rearrange("p (r k h d) -> p r k h d", r=8, k=4, h=2) for half in range(2)]
        vall = sb("vall", [P, NS, 16, P])
        w1s = sb("w1s", [P, 2, 16, P])
        tr = sb("tr", [P, 4, 512])
        sTa = sb("sTa", [P, 16, NR])
        hi, hid, sg = sb("hid_hi", [64, 2 * P]), sb("hid_d", [64, 2, 2, P]), sb("sg_d", [64, 2, 2, P])
        kc, ksq = sb("kc", [64, 2, P]), sb("ksq_d", [64, 2, P])
        krt = ksq
        scC, vcall = sb("scC", [P, NR]), sb("vcall", [P, NS, P])
        S = sb("Sd", [NR, L + 1])
        pc = sb("pc", [NR, P])
        pT, pcT = sb("pTd", [P, 16, NR]), sb("pcT", [P, NR])
        pages, off, idx = sb("pages", [P, NS], I32), sb("off", [P, 1], I32), sb("idx", [P, 2, NS], I32)
        grp, cand, rank, pick, pen = (
            sb("grp", [16, 130]), sb("cand", [16, 32]), sb("rank", [16, 30]), sb("pick", [16, 32]), sb("pen", [NR, 32]))
        pairs = tr[0:16, :, :].rearrange("p a b -> p (a b)")
        better, tie = (pairs[:, n * 900:(n + 1) * 900].rearrange("p (a b) -> p a b", b=30) for n in range(2))
        earlier = sb("earlier", [16, 30, 30])
        t16, mx, den, mc, dc = sb("t16d", [NR, 16]), sb("mxd", [NR, 1]), sb("dend", [NR, 1]), sb("mxc", [NR, 1]), sb("denc", [NR, 1])
        pg, pgT = sb("pgd", [NR, 16]), sb("pgTd", [16, NR])
        ps = [ctx.enter_context(nc.psum_tensor(f"pb{i}", [P, 512], F32)) for i in range(8)]
        TP, HIDP, SCP, MA, MB = ps[0:3], ps[3:5], ps[5], ps[6], ps[7]
        NFILL = 12

        pages_in, idx_ready, w_in, gathered = sem("pages_in"), sem("idx_ready"), sem("bw_in"), [sem(f"gathered{i}") for i in range(2)]
        f_done, f_copied, f_used, v_kept = sem("f_done"), sem("f_copied"), sem("f_used"), sem("v_kept")
        sc_copied, hi_copied, hid_ready, sg_ready, act_ready = (sem("bsc_copied"), sem("bhi_copied"), sem("bhid_ready"),
                                                                sem("bsg_ready"), sem("bact_ready"))
        kc_done, kc_copied, kss_done, krt_ready, kn_ready, scc_done, vc_done, vc_copied = (
            sem(n) for n in ("bkc_done", "bkc_copied", "bkss_done", "bkrt_ready", "bkn_ready", "bscc_done", "bvc_done", "bvc_copied"))
        c_nat, c_max, c_exp, c_norm, grp_done, pick_ready, pen_done, pen_ready = (
            sem(n) for n in ("c_nat", "c_max", "c_exp", "c_norm", "grp_done", "pick_ready", "pen_done", "pen_ready"))
        s_nat, s_out, new_done, s_max, s_exp, s_norm, pc_done, pc_copied, pt_done, pt_copied, o_done, earl = (
            sem(n) for n in ("s_nat", "s_out", "bnew_done", "s_max", "s_exp", "s_norm", "pc_done", "pc_copied", "bpt_done", "bpt_copied",
                             "bo_done", "earl"))

        with nc.Block() as block:

            @block.sync
            def _(sp):
                for p in range(NPAGE):
                    sp.dma_start(pages[p * 8:p * 8 + 8, :], io["page_table"][:, p:p + 1].rearrange("s a -> a s").broadcast_to([8, NS])).then_inc(pages_in, 16)
                for j in range(2):
                    for h in range(2):
                        for half in range(2):
                            sp.dma_start(w1s[h * 64:h * 64 + 64, j, :, half * 64:half * 64 + 64],
                                         io["cmp_w1"][0, j, half * 16:half * 16 + 16, :, :].rearrange("r d e -> d r e")).then_inc(w_in, 16)

            @block.gpsimd
            def _(pool):
                nc.gpsimd.iota(off[:, :], pattern=[[0, 1]], base=0, channel_multiplier=1).then_inc(earl, 1)
                nc.gpsimd.memset(earlier[:, :, :], 1.0)
                nc.gpsimd.drain()
                nc.gpsimd.affine_select(out=earlier[:, :, :], in_=earlier[:, :, :], compare_op=ALU.is_gt, fill=0.0,
                                        base=0, pattern=[[1, 30], [-1, 30]], channel_multiplier=0).then_inc(earl, 1)
                pool.wait_ge(idx_ready, 1)
                for s in range(NS):
                    for half in range(2):
                        n = 2 * s + half
                        if s:
                            pool.wait_ge(f_done, 6 * (n - 1))
                        nc.gpsimd.indirect_dma_start(out=rows[:, half, :], out_offset=None, in_=cache,
                                                     in_offset=bass.IndirectOffsetOnAxis(ap=idx[:, half, s:s + 1].bitcast(U32), axis=0)
                                                     ).then_inc(gathered[half], 16)
                        if n:
                            m = n - 1
                            pool.wait_ge(gathered[m % 2], 16 * (m // 2 + 1))
                            nc.gpsimd.tensor_copy(vall[:, m // 2, (m % 2) * 8:(m % 2) * 8 + 8, :].rearrange("p r (h d) -> p r h d", h=2),
                                                  kv[m % 2][:, :, 3, :, :]).then_inc(v_kept, 1)
                            pool.wait_ge(v_kept, n)
                pool.wait_ge(gathered[1], 16 * NS)
                nc.gpsimd.tensor_copy(vall[:, NS - 1, 8:16, :].rearrange("p r (h d) -> p r h d", h=2), kv[1][:, :, 3, :, :]).then_inc(v_kept, 1)

            @block.tensor
            def _(pe):
                pe.wait_ge(w_in, 16 * 8)
                with pe.Fori(0, NS) as s:
                    f0 = NFILL * s
                    uses = []

                    def fill(half, f):
                        n = half * 6 + f
                        src = kv[half]
                        pe.wait_ge(f_copied, f0 + n - 2) if n >= 3 else pe.wait_ge(f_copied, f0)
                        for u in range(4):
                            token = src[:, (f % 2) * 4 + u, f // 2, :, :].rearrange("p h d -> p (h d)")
                            last = nc.tensor.transpose(TP[n % 3][:, u * P:(u + 1) * P], token, ident[:, :])
                        last.then_inc(f_done, 1)

                    def use(half, f):
                        n = half * 6 + f
                        pe.wait_ge(f_copied, f0 + n + 1)
                        if f < 4:
                            j = f // 2
                            if n == 0:
                                pe.wait_ge(hid_ready, 2 * s)
                            for u in range(4):
                                r = half * 8 + (f % 2) * 4 + u
                                for h in range(2):
                                    d = slice(h * 64, h * 64 + 64)
                                    last = nc.tensor.matmul(HIDP[h][:, j * P:(j + 1) * P], w1s[d, j, r, :], tr[d, n % 4, u * P:(u + 1) * P],
                                                            start=(j == 0 and r == 0), stop=(j == 1 and r == 15))
                        else:
                            if n == 4:
                                pe.wait_ge(sc_copied, s)
                            for u in range(4):
                                r = half * 8 + (f - 4) * 4 + u
                                last = nc.tensor.matmul(SCP[:, r * 8:r * 8 + 8], tr[:, n % 4, u * P:(u + 1) * P],
                                                        qbd[:, ds(s, 1), :].rearrange("p a c -> p (a c)"), start=True, stop=True)
                        last.then_inc(f_used, 1)

                    for half in range(2):
                        pe.wait_ge(gathered[half], 16 * (s + 1))
                        for f in range(6):
                            fill(half, f)
                            if f:
                                use(half, f - 1)
                        use(half, 5)
                    pe.wait_ge(act_ready, 2 * s + 1)
                    nc.tensor.matmul(MA[:, 0:2 * NBD], w2[:, :, :].rearrange("p a b -> p (a b)"), hid[:, 0, :, 0:NBD], start=True, stop=True).then_inc(kc_done, 1)
                    pe.wait_ge(act_ready, 2 * s + 2)
                    for h in range(2):
                        nc.tensor.matmul(MB[0:NBD, 256 + h * 64:256 + h * 64 + 64], hid[:, 1, h, 0:NBD], w2[:, 1, :], start=True, stop=False)
                        last = nc.tensor.matmul(MB[0:NBD, 256 + h * 64:256 + h * 64 + 64], ones[0:1, 0:NBD], b2[0:1, 1:65], start=False, stop=True)
                    last.then_inc(vc_done, 1)
                    pe.wait_ge(vc_copied, s + 1)
                    pe.wait_ge(kc_copied, 2 * s + 2)
                    nc.tensor.matmul(MA[:, 0:2 * NBD], ones[0:64, :], ksq[:, :, 0:NBD], start=True, stop=True).then_inc(kss_done, 1)
                    pe.wait_ge(kn_ready, s + 1)
                    for h in range(2):
                        last = nc.tensor.matmul(MB[0:NBD, h * 4:h * 4 + 4], kc[:, h, 0:NBD], q64[:, ds(s * 8 + h * 4, 4)], start=True, stop=True)
                    last.then_inc(scc_done, 1)

                pe.wait_ge(c_nat, 1)
                nc.tensor.transpose(MA[0:NR, 0:NBD], scC[0:NBD, :], ident[0:NBD, 0:NBD]).then_inc(c_nat, 1)
                nc.tensor.matmul(MB[0:NR, 0:16], q64[:, :], ksn[:, :, :].rearrange("p s h -> p (s h)"), start=True, stop=True).then_inc(new_done, 1)
                pe.wait_ge(sc_copied, NS)

                def selected(b):
                    for u in range(4):
                        last = nc.tensor.transpose(TP[b % 3][0:NR, u * P:(u + 1) * P], sTa[:, b * 4 + u, :], ident[:, :])
                    last.then_inc(s_nat, 1)

                for b in range(3):
                    selected(b)
                pe.wait_ge(c_norm, 1)
                nc.tensor.matmul(HIDP[0][0:16, 0:NBD], rows_of[:, :], pc[:, 0:NBD], start=True, stop=True).then_inc(grp_done, 1)
                pe.wait_ge(pick_ready, 1)
                nc.tensor.matmul(HIDP[1][0:NR, 0:32], of_rows[:, :], pick[:, :], start=True, stop=True).then_inc(pen_done, 1)
                pe.wait_ge(s_out, 1)
                selected(3)
                pe.wait_ge(c_norm, 2)
                nc.tensor.transpose(MA[0:NBD, 0:NR], pc[:, 0:NBD], ident[0:NR, 0:NR]).then_inc(pc_done, 1)
                pe.wait_ge(s_norm, 1)
                pe.wait_ge(s_out, 4)
                for b in range(4):
                    if b >= 3:
                        pe.wait_ge(pt_copied, 1)
                    for u in range(4):
                        r = b * 4 + u
                        last = nc.tensor.transpose(TP[b % 3][:, u * NR:(u + 1) * NR], S[:, r * P:(r + 1) * P], ident[0:NR, 0:NR])
                    last.then_inc(pt_done, 1)
                nc.tensor.transpose(MB[0:16, 0:NR], pg[:, :], ident[0:NR, 0:NR]).then_inc(pt_done, 1)
                pe.wait_ge(pc_copied, 1)
                pe.wait_ge(pt_copied, 5)
                pe.wait_ge(v_kept, 2 * NS)
                for s in range(NS):
                    cols = slice(s * 8, s * 8 + 8)
                    nc.tensor.matmul(SCP[:, cols], vcall[0:NBD, s, :], pcT[0:NBD, cols], start=True, stop=False)
                    for r in range(16):
                        nc.tensor.matmul(SCP[:, cols], vall[:, s, r, :], pT[:, r, cols], start=False, stop=(r == 15))
                nc.tensor.matmul(HIDP[0][0:64, 0:NR], v_new[:, 0, :], pgT[:, :], start=True, stop=True).then_inc(o_done, 1)

            @block.scalar
            def _(act):
                with act.Fori(0, NS) as s:
                    f0 = NFILL * s
                    for n in range(0, NFILL, 2):
                        act.wait_ge(f_done, f0 + n + 1)
                        if n >= 4:
                            act.wait_ge(f_used, f0 + n - 3)
                        else:
                            act.wait_ge(f_used, f0)
                        act.wait_ge(f_copied, f0 + n)
                        nc.scalar.activation(tr[:, n % 4, :], TP[n % 3][:, :], ACT.Copy).then_inc(f_copied, 1)
                    act.wait_ge(f_used, f0 + NFILL)
                    for h in range(2):
                        act.wait_ge(hid_ready, 2 * s + h)
                        nc.scalar.activation(hi[:, :], HIDP[h][64:128, 0:2 * P], ACT.Copy).then_inc(hi_copied, 1)
                    act.wait_ge(hid_ready, 2 * s + 2)
                    for j in range(2):
                        nc.scalar.activation(sg[:, j, :, 0:NBD], hid[:, j, :, 0:NBD], ACT.Sigmoid, bias=cbias[:, j:j + 1]).then_inc(sg_ready, 1)
                    nc.scalar.activation(sTa[:, :, ds(s * 8, 8)], SCP[:, 0:P].rearrange("p (r c) -> p r c", r=16), ACT.Copy).then_inc(sc_copied, 1)
                    act.wait_ge(kc_done, s + 1)
                    v = MA[0:64, 0:2 * NBD].rearrange("p (h n) -> p h n", h=2)
                    nc.scalar.activation(kc[:, :, 0:NBD], v, ACT.Identity, bias=b2[:, 0:1]).then_inc(kc_copied, 1)
                    nc.scalar.activation(ksq[:, :, 0:NBD], v, ACT.Square, bias=b2[:, 0:1]).then_inc(kc_copied, 1)
                    act.wait_ge(vc_done, s + 1)
                    nc.scalar.activation(vcall[0:NBD, ds(s, 1), :], MB[0:NBD, 256:384].unsqueeze(1), ACT.Copy).then_inc(vc_copied, 1)
                    act.wait_ge(kss_done, s + 1)
                    nc.scalar.activation(krt[:, :, 0:NBD], v, ACT.Sqrt, scale=1.0 / HD, bias=eps[0:64, :]).then_inc(krt_ready, 1)
                    act.wait_ge(scc_done, s + 1)
                    nc.scalar.activation(scC[0:NBD, ds(s * 8, 8)], MB[0:NBD, 0:8], ACT.Copy)
                    nc.scalar.drain()
                nc.scalar.activation(mc[:, :], gates[:, 0:1], ACT.Copy).then_inc(c_nat, 1)
                act.wait_ge(c_max, 1)
                nc.scalar.activation(pc[:, 0:NBD], pc[:, 0:NBD], ACT.Exp, bias=mc[:, :], accum_out=dc[:, :]).then_inc(c_exp, 1)
                act.wait_ge(s_max, 1)
                nc.scalar.activation(S[:, :], S[:, :], ACT.Exp, bias=mx[:, :], accum_out=den[:, :]).then_inc(s_exp, 1)
                act.wait_ge(pc_done, 1)
                nc.scalar.activation(pcT[0:NBD, :], MA[0:NBD, 0:NR], ACT.Copy).then_inc(pc_copied, 1)
                for b in range(4):
                    act.wait_ge(pt_done, b + 1)
                    nc.scalar.activation(pT[:, b * 4:b * 4 + 4, :], TP[b % 3][:, 0:4 * NR].rearrange("p (u r) -> p u r", u=4),
                                         ACT.Copy).then_inc(pt_copied, 1)
                act.wait_ge(pt_done, 5)
                nc.scalar.activation(pgT[:, :], MB[0:16, 0:NR], ACT.Copy).then_inc(pt_copied, 1)

            @block.vector
            def _(dve):
                dve.wait_ge(pages_in, 16 * NPAGE)
                dve.wait_ge(earl, 1)
                nc.vector.tensor_scalar(off[:, :], off[:, :], 7, 1, ALU.bitwise_and, ALU.logical_shift_left)
                nc.vector.tensor_scalar(pages[:, :], pages[:, :], 4, None, ALU.logical_shift_left)
                nc.vector.drain()
                nc.vector.tensor_tensor(idx[:, 0, :], pages[:, :], off[:, :].broadcast_to([P, NS]), ALU.bitwise_or)
                nc.vector.drain()
                nc.vector.tensor_scalar(idx[:, 1, :], idx[:, 0, :], 1, None, ALU.bitwise_or).then_inc(idx_ready, 1)
                with dve.Fori(0, NS) as s:
                    f0 = NFILL * s
                    for n in range(1, NFILL, 2):
                        dve.wait_ge(f_done, f0 + n + 1)
                        if n >= 4:
                            dve.wait_ge(f_used, f0 + n - 3)
                        else:
                            dve.wait_ge(f_used, f0)
                        dve.wait_ge(f_copied, f0 + n)
                        nc.vector.tensor_copy(tr[:, n % 4, :], TP[n % 3][:, :]).then_inc(f_copied, 1)
                    for h in range(2):
                        dve.wait_ge(hi_copied, 2 * s + h + 1)
                        nc.vector.tensor_tensor(hid[:, :, h, 0:NBD], HIDP[h][0:64, 0:2 * P].rearrange("p (j n) -> p j n", j=2)[:, :, 0:NBD],
                                                hi[:, :].rearrange("p (j n) -> p j n", j=2)[:, :, 1:P], ALU.add).then_inc(hid_ready, 1)
                    nc.vector.drain()
                    for j in range(2):
                        dve.wait_ge(sg_ready, 2 * s + j + 1)
                        nc.vector.scalar_tensor_tensor(out=hid[:, j, :, 0:NBD], in0=hid[:, j, :, 0:NBD], scalar=cbias[:, j:j + 1],
                                                       in1=sg[:, j, :, 0:NBD], op0=ALU.add, op1=ALU.mult).then_inc(act_ready, 1)
                    dve.wait_ge(krt_ready, s + 1)
                    nc.vector.reciprocal(krt[:, :, 0:NBD], krt[:, :, 0:NBD])
                    nc.vector.drain()
                    nc.vector.scalar_tensor_tensor(out=kc[:, :, 0:NBD], in0=kc[:, :, 0:NBD], scalar=g4[0:64, 1:2], in1=krt[:, :, 0:NBD],
                                                   op0=ALU.mult, op1=ALU.mult).then_inc(kn_ready, 1)
                dve.wait_ge(c_nat, 2)
                nc.vector.tensor_copy(pc[:, 0:NBD], MA[0:NR, 0:NBD])
                nc.vector.drain()
                nc.vector.reduce_max(mc[:, :], pc[:, 0:NBD], AX.X)
                nc.vector.drain()
                nc.vector.tensor_scalar(mc[:, :], mc[:, :], -1.0, None, ALU.mult).then_inc(c_max, 1)
                dve.wait_ge(c_exp, 1)
                nc.vector.tensor_scalar(dc[:, :], dc[:, :], 1e-30, None, ALU.max)
                nc.vector.drain()
                nc.vector.reciprocal(dc[:, :], dc[:, :])
                nc.vector.drain()
                nc.vector.tensor_scalar(pc[:, 0:NBD], pc[:, 0:NBD], dc[:, :], None, ALU.mult).then_inc(c_norm, 1)
                nc.vector.memset(grp[:, :], 0.0)
                nc.vector.drain()
                dve.wait_ge(grp_done, 1)
                nc.vector.tensor_copy(grp[:, 1:1 + NBD], HIDP[0][0:16, 0:NBD])
                nc.vector.drain()
                nc.vector.tensor_scalar(pc[:, 0:NBD], pc[:, 0:NBD], gates[:, CMP:CMP + 1], None, ALU.mult).then_inc(c_norm, 1)
                nc.vector.tensor_tensor(tie[:, 0:5, :].rearrange("p a b -> p (a b)")[:, 0:P], grp[:, 1:1 + P], grp[:, 0:P], ALU.add)
                nc.vector.drain()
                nc.vector.reduce_sum(cand[:, :], tie[:, 0:5, :].rearrange("p a b -> p (a b)")[:, 0:P].rearrange("p (j r) -> p j r", r=4), AX.X)
                nc.vector.drain()
                own = cand[:, 1:31].unsqueeze(2).broadcast_to([16, 30, 30])
                other = cand[:, 1:31].unsqueeze(1).broadcast_to([16, 30, 30])
                nc.vector.tensor_tensor(better[:, :, :], other, own, ALU.is_gt)
                nc.vector.tensor_tensor(tie[:, :, :], other, own, ALU.is_equal)
                nc.vector.drain()
                dve.wait_ge(earl, 2)
                nc.vector.tensor_tensor(tie[:, :, :], tie[:, :, :], earlier[:, :, :], ALU.mult)
                nc.vector.drain()
                nc.vector.tensor_tensor(better[:, :, :], better[:, :, :], tie[:, :, :], ALU.add)
                nc.vector.drain()
                nc.vector.reduce_sum(rank[:, :], better[:, :, :], AX.X)
                nc.vector.memset(pick[:, :], 1.0)
                nc.vector.drain()
                nc.vector.tensor_scalar(pick[:, 1:31], rank[:, :], 12.5, None, ALU.is_lt).then_inc(pick_ready, 1)
                dve.wait_ge(pen_done, 1)
                nc.vector.tensor_scalar(pen[:, :], HIDP[1][0:NR, 0:32], -1.0, BIG, ALU.add, ALU.mult)
                nc.vector.drain()
                for b in range(4):
                    dve.wait_ge(s_nat, b + 1)
                    nc.vector.tensor_tensor(S[:, b * 512:(b + 1) * 512].rearrange("p (u j w) -> p u j w", u=4, w=4),
                                            TP[b % 3][0:NR, :].rearrange("p (u j w) -> p u j w", u=4, w=4),
                                            pen[:, :].unsqueeze(1).unsqueeze(3).broadcast_to([NR, 4, 32, 4]), ALU.add).then_inc(s_out, 1)
                dve.wait_ge(new_done, 1)
                nc.vector.tensor_tensor(t16[:, :], MB[0:NR, 0:16], rows_of[:, :], ALU.mult)
                nc.vector.drain()
                nc.vector.reduce_sum(S[:, L:L + 1], t16[:, :], AX.X)
                nc.vector.drain()
                nc.vector.reduce_max(mx[:, :], S[:, :], AX.X)
                nc.vector.drain()
                nc.vector.tensor_scalar(mx[:, :], mx[:, :], -1.0, None, ALU.mult).then_inc(s_max, 1)
                dve.wait_ge(s_exp, 1)
                nc.vector.tensor_scalar(den[:, :], den[:, :], 1e-30, None, ALU.max)
                nc.vector.drain()
                nc.vector.reciprocal(den[:, :], den[:, :])
                nc.vector.drain()
                nc.vector.tensor_tensor(den[:, :], den[:, :], gates[:, FULL:FULL + 1], ALU.mult)
                nc.vector.drain()
                nc.vector.tensor_scalar(S[:, :], S[:, :], den[:, :], None, ALU.mult)
                nc.vector.drain()
                nc.vector.tensor_scalar(pg[:, :], rows_of[:, :], S[:, L:L + 1], None, ALU.mult).then_inc(s_norm, 1)
                dve.wait_ge(o_done, 1)
                nc.vector.tensor_tensor(oT[:, :], HIDP[0][0:64, 0:NR], oT[:, :], ALU.add)
                nc.vector.drain()
                for h in range(2):
                    rws = lambda a: a.rearrange("p (s h g) -> p s h g", h=2, g=4)[:, :, h, :]
                    nc.vector.tensor_tensor(rws(oT[:, :]), rws(SCP[h * 64:h * 64 + 64, 0:NR]), rws(oT[:, :]), ALU.add)
                nc.vector.drain()
                for g2 in range(2):
                    for h in range(2):
                        nc.vector.tensor_copy(mixS[g2 * 64:g2 * 64 + 64, 2 + 2 * h:4 + 2 * h, :],
                                              oT[:, :].rearrange("p (s h g a) -> p h a g s", h=2, g=2, a=2)[:, h, g2, :, :])


def decode(nc, io, keep):
    decode_recurrences(nc, io, keep)
    with ExitStack() as ctx:
        sb = lambda n, s, d=F32: ctx.enter_context(nc.sbuf_tensor(n, s, d))
        at = {
            "qbd": sb("qbd_n", [P, NS, 8]), "q64": sb("q64", [64, NR]), "gates": sb("gates_dec", [NR, 3]),
            "rows_of": sb("rows_of", [NR, 16]), "of_rows": sb("of_rows", [16, NR]),
            "kwn": sb("kwn", [64, NS, 2]), "ksn": sb("ksn", [64, NS, 2]), "v_new": sb("v_new", [16, 2, 64]),
            "oT": sb("oT", [64, NR]),
        }
        decode_queries(nc, io, keep, at)
        decode_window(nc, io, keep, at)
        decode_blocks(nc, io, keep, at)


def mix_and_project(nc, io, keep, x2T, hH, hL):
    ident, eps, ones, uact, onat, hs, RN, mixS = (keep[k] for k in ("ident", "eps", "ones", "uact", "onat", "hs", "rows_cols", "mixS"))
    zT = io["zT"]
    w_out = io["w_out"].rearrange("l (k p) n -> p (l k) n", p=P)
    with ExitStack() as ctx:
        sb = lambda n, s, d=F32: ctx.enter_context(nc.sbuf_tensor(n, s, d))
        sem = semaphores(nc, ctx, "mix")
        mixH, mixL = hH, hL
        wo, woH, woL = sb("wo", [P, KD, P]), sb("woH", [P, KD, P], F32R), sb("woL", [P, KD, P], F32R)
        mixc = sb("mixc", [P, KD, P])
        gr, mo, sig = sb("gr", [P, HP, TT]), sb("mo", [P, HP, TT]), sb("sig", [P, HP, TT])
        ss = sb("ssh", [P, 2, NCH * 4])
        nd = sb("nd", [P, NCH, 4])
        tmp = sb("tmpm", [P, HP, P])
        gains = sb("gains", [P, 2])
        skip, g2 = sb("skip", [P, HP]), sb("g2", [P, KD])
        sqx = sb("sqx", [P, 2, TT])
        sq = sqx[:, :, :].rearrange("p a t -> p (a t)")[:, 0:NCH * 4 * 64].rearrange("p (n e) -> p n e", e=64)
        rn = sb("rn", [P, TT])
        ps = [ctx.enter_context(nc.psum_tensor(f"pg{i}", [P, 512], F32)) for i in range(8)]
        gates_in, x_in, sig_done, div_done, sq_done, ss_done, rt_done, normed, gated = (
            sem("gates_in"), [sem(f"x_in{i}") for i in range(2)], sem("sig_done3"), sem("div_done"), sem("sq_done"), sem("ssum_done"), sem("rt_done"),
            sem("normed"), sem("gated"))
        t_done, t_used = sem("t_done"), sem("t_used")
        wo_in, woH_ready, woL_ready = sem("wo_in"), sem("woH_ready"), sem("woL_ready")
        mixc_ready, mixH_ready, mixL_ready = sem("mixc_ready"), sem("mixH_ready"), sem("mixL_ready")
        hc_ready, hH_ready, hL_ready = sem("hc_ready"), sem("hH_ready"), sem("hL_ready")
        y_done, y_added, sqx_done, sum_done, rn_done = (
            sem("y_done"), sem("y_added"), sem("sqx_done"), sem("sum_done"), sem("rn_done"))
        heads = lambda at: onat[:, :, at:at + 256].rearrange("p i (h e) -> p i h e", h=4)

        with nc.Block() as block:

            @block.sync
            def _(sp):
                sp.dma_start(gr[:, :, :], zT[GR:GR + 256, :].rearrange("(j p) t -> p j t", p=P)).then_inc(gates_in, 16)
                sp.dma_start(mo[:, :, :], zT[MO:MO + 256, :].rearrange("(j p) t -> p j t", p=P)).then_inc(gates_in, 16)
                for half in range(2):
                    at = slice(half * 64, half * 64 + 64)
                    sp.dma_start(gains[at, 0:1], io["gla_norm_g"].rearrange("l d -> d l")).then_inc(gates_in, 16)
                    sp.dma_start(gains[at, 1:2], io["ml_norm_g"].rearrange("l d -> d l")).then_inc(gates_in, 16)
                sp.dma_start(skip[:, :], io["ml_skip"].rearrange("l (k p) -> p (l k)", p=P)).then_inc(gates_in, 16)
                sp.dma_start(g2[:, :], io["norm2_g"].rearrange("l (k p) -> p (l k)", p=P)).then_inc(gates_in, 16)
                sp.dma_start(wo[:, :, :], w_out[:, :, 0:P]).then_inc(wo_in, 16)
                sp.wait_ge(t_done, TQ)
                for half in range(2):
                    at = slice(half * KD // 2, (half + 1) * KD // 2)
                    sp.dma_start(x2T[:, at, :], io["xT"].rearrange("(k p) t -> p k t", p=P)[:, at, :]).then_inc(x_in[half], 16)
                with sp.Fori(1, KD) as m:
                    sp.wait_ge(woL_ready, m)
                    sp.dma_start(wo[:, :, :], w_out[:, :, ds(m * P, P)]).then_inc(wo_in, 16)

            @block.scalar
            def _(act):
                act.wait_ge(gates_in, 16 * 8)
                nc.scalar.activation(sig[:, :, :], gr[:, :, :], ACT.Sigmoid).then_inc(sig_done, 1)
                nc.scalar.activation(mo[:, :, :], mo[:, :, :], ACT.Sigmoid).then_inc(sig_done, 1)
                for n, at in enumerate((0, 768)):
                    if n:
                        act.wait_ge(div_done, 1)
                        act.wait_ge(ss_done, 1)
                    nc.scalar.activation(sq[:, :, :].rearrange("p (i h) e -> p i h e", h=4), heads(at), ACT.Square).then_inc(sq_done, 1)
                    act.wait_ge(ss_done, n + 1)
                    nc.scalar.activation(ss[:, n, :], ss[:, n, :], ACT.Sqrt, scale=1.0 / HD, bias=eps[:, :]).then_inc(rt_done, 1)
                for i in range(TQ + 1):
                    n = P if i < TQ else NS
                    act.wait_ge(mixc_ready, i + 1)
                    nc.scalar.activation(mixH[:, :, i * P:i * P + n], mixc[:, :, 0:n], ACT.Copy).then_inc(mixH_ready, 1)
                act.wait_ge(wo_in, 16)
                nc.scalar.activation(woH[:, :, :], wo[:, :, :], ACT.Copy).then_inc(woH_ready, 1)
                for m in range(1, KD):
                    act.wait_ge(wo_in, 16 * (m + 1))
                    act.wait_ge(y_done, NT * m)
                    nc.scalar.activation(woH[:, :, :], wo[:, :, :], ACT.Copy).then_inc(woH_ready, 1)
                for k in range(KD):
                    act.wait_ge(y_added, NT * (k + 1))
                    if k >= 2:
                        act.wait_ge(sum_done, k - 1)
                    nc.scalar.activation(sqx[:, k % 2, :], x2T[:, k, :], ACT.Square).then_inc(sqx_done, 1)
                act.wait_ge(sum_done, KD)
                for third in range(NT):
                    last = nc.scalar.activation(rn[:, third * TC:(third + 1) * TC], ps[third][:, 0:TC], ACT.Sqrt, scale=1.0 / D, bias=eps[:, :])
                last.then_inc(rn_done, 1)
                for k in range(KD):
                    act.wait_ge(hc_ready, k + 1)
                    nc.scalar.activation(hH[:, k, :], sqx[:, k % 2, :], ACT.Copy).then_inc(hH_ready, 1)

            @block.vector
            def _(dve):
                den = hs[:, :, :, 64]
                nc.vector.tensor_scalar(nd[:, :, :], den, -1.0, None, ALU.mult)
                nc.vector.drain()
                nc.vector.tensor_tensor(nd[:, :, :], nd[:, :, :], den, ALU.max)
                nc.vector.drain()
                nc.vector.tensor_tensor(nd[:, :, :], nd[:, :, :], RN[:, :, 12:16], ALU.max)
                nc.vector.drain()
                nc.vector.reciprocal(nd[:, :, :], nd[:, :, :])
                nc.vector.drain()
                nc.vector.tensor_tensor(heads(768), hs[:, :, :, 0:64], nd[:, :, :].unsqueeze(3).broadcast_to([P, NCH, 4, 64]),
                                        ALU.mult).then_inc(div_done, 1)
                dve.wait_ge(gates_in, 16 * 8)
                dve.wait_ge(sig_done, 2)
                for hp in range(HP):
                    nc.vector.scalar_tensor_tensor(out=gr[:, hp, :], in0=gr[:, hp, :], scalar=gains[:, 0:1], in1=sig[:, hp, :],
                                                   op0=ALU.mult, op1=ALU.mult)
                    nc.vector.scalar_tensor_tensor(out=uact[:, hp, :], in0=uact[:, hp, :], scalar=skip[:, hp:hp + 1], in1=mo[:, hp, :],
                                                   op0=ALU.mult, op1=ALU.mult)
                nc.vector.drain()
                nc.vector.tensor_scalar(mo[:, :, :], mo[:, :, :], gains[:, 1:2], None, ALU.mult)
                for n, at in enumerate((0, 768)):
                    dve.wait_ge(sq_done, n + 1)
                    nc.vector.reduce_sum(ss[:, n, :], sq[:, :, :], AX.X).then_inc(ss_done, 1)
                    dve.wait_ge(rt_done, n + 1)
                    nc.vector.reciprocal(ss[:, n, :], ss[:, n, :])
                    nc.vector.drain()
                    nc.vector.tensor_tensor(heads(at), heads(at),
                                            ss[:, n, :].rearrange("p (i h) -> p i h", h=4).unsqueeze(3).broadcast_to([P, NCH, 4, 64]),
                                            ALU.mult).then_inc(normed, 1)
                nc.vector.drain()
                def split_mix(i, n):
                    dve.wait_ge(mixH_ready, i + 1)
                    nc.vector.tensor_tensor(mixL[:, :, i * P:i * P + n], mixc[:, :, 0:n], mixH[:, :, i * P:i * P + n].bitcast(F32),
                                            ALU.subtract).then_inc(mixL_ready, 1)

                for i in range(TQ):
                    at = slice(i * P, (i + 1) * P)
                    a, b = ps[2 * (i % 2)], ps[2 * (i % 2) + 1]
                    pair = lambda bank, lo: bank[:, lo * P:(lo + 2) * P].rearrange("p (k t) -> p k t", k=2)
                    dve.wait_ge(t_done, i + 1)
                    nc.vector.tensor_tensor(mixc[:, 0:2, :], pair(a, 0), gr[:, :, at], ALU.mult)
                    nc.vector.tensor_copy(mixc[:, 2:4, :], pair(a, 2))
                    nc.vector.tensor_copy(mixc[:, 4:6, :], pair(b, 0))
                    nc.vector.tensor_tensor(tmp[:, :, :], pair(b, 2), mo[:, :, at], ALU.mult).then_inc(t_used, 1)
                    nc.vector.drain()
                    nc.vector.tensor_tensor(mixc[:, 6:8, :], tmp[:, :, :], uact[:, :, at], ALU.add).then_inc(mixc_ready, 1)
                    split_mix(i, P)
                    nc.vector.drain()
                at = slice(T, TT)
                nc.vector.tensor_tensor(mixc[:, 0:2, 0:NS], mixS[:, 0:2, :], gr[:, :, at], ALU.mult)
                nc.vector.tensor_copy(mixc[:, 2:6, 0:NS], mixS[:, 2:6, :])
                nc.vector.tensor_tensor(tmp[:, :, 0:NS], mixS[:, 6:8, :], mo[:, :, at], ALU.mult)
                nc.vector.drain()
                nc.vector.tensor_tensor(mixc[:, 6:8, 0:NS], tmp[:, :, 0:NS], uact[:, :, at], ALU.add).then_inc(mixc_ready, 1)
                split_mix(TQ, NS)
                def low_weights(m):
                    dve.wait_ge(woH_ready, m + 1)
                    nc.vector.tensor_tensor(woL[:, :, :], wo[:, :, :], woH[:, :, :].bitcast(F32), ALU.subtract).then_inc(woL_ready, 1)

                low_weights(0)
                for m in range(KD):
                    dve.wait_ge(x_in[m // (KD // 2)], 16)
                    for third in range(NT):
                        cols = slice(third * TC, (third + 1) * TC)
                        dve.wait_ge(y_done, NT * m + third + 1)
                        if third == NT - 1 and m + 1 < KD:
                            low_weights(m + 1)
                        nc.vector.tensor_tensor(x2T[:, m, cols], ps[2 + (m % 2) * 3 + third][:, 0:TC], x2T[:, m, cols],
                                                ALU.add).then_inc(y_added, 1)
                dve.wait_ge(rn_done, 1)
                nc.vector.reciprocal(rn[:, :], rn[:, :])
                nc.vector.drain()
                for k in range(KD):
                    hc = sqx[:, k % 2, :]
                    nc.vector.scalar_tensor_tensor(out=hc, in0=x2T[:, k, :], scalar=g2[:, k:k + 1], in1=rn[:, :],
                                                   op0=ALU.mult, op1=ALU.mult).then_inc(hc_ready, 1)
                    dve.wait_ge(hH_ready, k + 1)
                    nc.vector.tensor_tensor(hL[:, k, :], hc, hH[:, k, :].bitcast(F32), ALU.subtract).then_inc(hL_ready, 1)

            @block.tensor
            def _(pe):
                pe.wait_ge(normed, 2)
                for i in range(TQ):
                    if i >= 2:
                        pe.wait_ge(t_used, i - 1)
                    for k in range(KD):
                        last = nc.tensor.transpose(ps[2 * (i % 2) + k // 4][:, (k % 4) * P:(k % 4 + 1) * P],
                                                   onat[:, i, k * P:(k + 1) * P], ident[:, :])
                    last.then_inc(t_done, 1)
                pe.wait_ge(mixH_ready, TQ + 1)
                pe.wait_ge(mixL_ready, TQ + 1)
                for m in range(KD):
                    pe.wait_ge(woH_ready, m + 1)
                    pe.wait_ge(woL_ready, m + 1)
                    if m >= 2:
                        pe.wait_ge(y_added, NT * (m - 1))
                    for third in range(NT):
                        split_product(nc, ps[2 + (m % 2) * 3 + third][:, 0:TC], [(woH[:, k, :], woL[:, k, :]) for k in range(KD)],
                                      [(mixH[:, k, third * TC:(third + 1) * TC], mixL[:, k, third * TC:(third + 1) * TC])
                                       for k in range(KD)]).then_inc(y_done, 1)
                pe.wait_ge(y_added, NT * KD)
                for k in range(KD):
                    pe.wait_ge(sqx_done, k + 1)
                    for third in range(NT):
                        last = nc.tensor.matmul(ps[third][:, 0:TC], ones[:, :], sqx[:, k % 2, third * TC:(third + 1) * TC],
                                                start=(k == 0), stop=(k == KD - 1))
                    last.then_inc(sum_done, 1)


FG = 2
NFG = 4 * D // P // FG


def channel_mixer(nc, io, keep, x2T, hH, hL):
    ident = keep["ident"]
    w_up = io["w_up"].rearrange("l (k p) n -> p (l k) n", p=P)
    w_down = io["w_down"].rearrange("l (f p) n -> p (l f) n", p=P)
    y_p, y_s = io["out0"].rearrange("b t d -> (b t) d"), io["out1"].rearrange("b t d -> (b t) d")
    with ExitStack() as ctx:
        sb = lambda n, s, d=F32: ctx.enter_context(nc.sbuf_tensor(n, s, d))
        sem = semaphores(nc, ctx, "channel")
        wu = keep["uact"][:, :, :].rearrange("p a t -> p (a t)")[:, 0:KD * FG * P].rearrange("p (k n) -> p k n", k=KD)
        wd = keep["hs"][:, :, :, :].rearrange("p i h e -> p (i h e)")[:, 0:FG * D].rearrange("p (f n) -> p f n", f=FG)
        wuH, wuL = sb("wuH", [P, FG, KD, P], F32R), sb("wuL", [P, FG, KD, P], F32R)
        wdH, wdL = sb("wdH", [P, FG, D], F32R), sb("wdL", [P, FG, D], F32R)
        act2 = sb("act2", [P, FG, TT])
        hidH, hidL = sb("hidH", [P, 2, FG, TT], F32R), sb("hidL", [P, 2, FG, TT], F32R)
        ynat = act2[:, :, 0:D]
        ps = [ctx.enter_context(nc.psum_tensor(f"ph{i}", [P, 512], F32)) for i in range(8)]
        wu_in, wuH_ready, wuL_ready = sem("wu_in"), sem("wuH_ready"), sem("wuL_ready")
        wd_in, wdH_ready, wdL_ready = sem("wd_in"), sem("wdH_ready"), sem("wdL_ready")
        up_done, relu_done, hidH_ready, hidL_ready, down_done, added = (
            sem("up_done"), sem("relu_done"), sem("hidH_ready"), sem("hidL_ready"), sem("down_done"), sem("added"))
        out_t, out_a, out_b = sem("out_t"), sem("out_a"), sem("out_b")
        stored = [sem(f"y_stored{i}") for i in range(2)]
        NUP, NDN = FG * NT, KD * NT

        with nc.Block() as block:

            @block.sync
            def _(sp):
                sp.dma_start(wu[:, :, :], w_up[:, :, 0:FG * P]).then_inc(wu_in, 16)
                sp.dma_start(wd[:, :, :], w_down[:, 0:FG, :]).then_inc(wd_in, 16)
                with sp.Fori(1, NFG) as g:
                    sp.wait_ge(wuL_ready, FG * g)
                    sp.dma_start(wu[:, :, :], w_up[:, :, ds(g * FG * P, FG * P)]).then_inc(wu_in, 16)
                    sp.wait_ge(wdL_ready, g)
                    sp.dma_start(wd[:, :, :], w_down[:, ds(g * FG, FG), :]).then_inc(wd_in, 16)
                for i in range(9):
                    n, dst = (P, y_p[i * P:(i + 1) * P, :]) if i < 8 else (NS, y_s)
                    sp.wait_ge(out_a, i + 1)
                    sp.wait_ge(out_b, i + 1)
                    sp.dma_start(dst, ynat[0:n, i % 2, :]).then_inc(stored[i % 2], 16)
                sp.wait_ge(stored[0], 16 * 5)
                sp.wait_ge(stored[1], 16 * 4)

            @block.tensor
            def _(pe):
                def up(g, first=False):
                    for f in range(FG):
                        pe.wait_ge(wuH_ready, FG * g + f + 1)
                        pe.wait_ge(wuL_ready, FG * g + f + 1)
                        for third in range(NT):
                            n = f * NT + third
                            cols = slice(third * TC, (third + 1) * TC)
                            if not first or n >= 3:
                                pe.wait_ge(relu_done, NUP * g + n - 2)
                            split_product(nc, ps[n % 3][:, 0:TC], [(wuH[:, f, k, :], wuL[:, f, k, :]) for k in range(KD)],
                                          [(hH[:, k, cols], hL[:, k, cols]) for k in range(KD)]).then_inc(up_done, 1)

                def down(g, slot):
                    pe.wait_ge(wdH_ready, g + 1)
                    pe.wait_ge(wdL_ready, g + 1)
                    pe.wait_ge(hidH_ready, FG * g + FG)
                    pe.wait_ge(hidL_ready, FG * g + FG)
                    for m in range(KD):
                        out = slice(m * P, (m + 1) * P)
                        for third in range(NT):
                            n = m * NT + third
                            cols = slice(third * TC, (third + 1) * TC)
                            if n >= 4:
                                pe.wait_ge(added, NDN * g + n - 3)
                            else:
                                pe.wait_ge(added, NDN * g)
                            split_product(nc, ps[4 + n % 4][:, 0:TC], [(wdH[:, f, out], wdL[:, f, out]) for f in range(FG)],
                                          [(hidH[:, slot, f, cols], hidL[:, slot, f, cols]) for f in range(FG)]).then_inc(down_done, 1)

                up(0, first=True)
                with pe.Fori(0, NFG // 2 - 1) as it:
                    for slot in range(2):
                        up(2 * it + slot + 1)
                        down(2 * it + slot, slot)
                up(NFG - 1)
                down(NFG - 2, 0)
                down(NFG - 1, 1)
                pe.wait_ge(added, NDN * NFG)
                for i in range(9):
                    n = P if i < 8 else NS
                    if i >= 2:
                        pe.wait_ge(out_a, i - 1)
                        pe.wait_ge(out_b, i - 1)
                    for k in range(KD):
                        last = nc.tensor.transpose(ps[2 * (i % 2) + k // 4][0:n, (k % 4) * P:(k % 4 + 1) * P],
                                                   x2T[:, k, i * P:i * P + n], ident[:, :])
                    last.then_inc(out_t, 1)

            @block.scalar
            def _(act):
                def high_up(g, f, fresh=False):
                    act.wait_ge(wu_in, 16 * (g + 1))
                    if not fresh:
                        act.wait_ge(up_done, NUP * (g - 1) + NT * (f + 1))
                    nc.scalar.activation(wuH[:, f, :, :], wu[:, :, f * P:(f + 1) * P], ACT.Copy).then_inc(wuH_ready, 1)

                def high_down(g, fresh=False):
                    act.wait_ge(wd_in, 16 * (g + 1))
                    if not fresh:
                        act.wait_ge(down_done, NDN * g)
                    nc.scalar.activation(wdH[:, :, :], wd[:, :, :], ACT.Copy).then_inc(wdH_ready, 1)

                def hidden(g, slot, f, fresh=False):
                    if not fresh:
                        act.wait_ge(hidL_ready, FG * (g - 1) + f + 1)
                    for third in range(NT):
                        act.wait_ge(up_done, NUP * g + NT * f + third + 1)
                        nc.scalar.activation(act2[:, f, third * TC:(third + 1) * TC], ps[third][:, 0:TC], ACT.Relu).then_inc(relu_done, 1)
                    nc.scalar.drain()
                    nc.scalar.activation(act2[:, f, :], act2[:, f, :], ACT.Square)
                    nc.scalar.drain()
                    nc.scalar.activation(hidH[:, slot, f, :], act2[:, f, :], ACT.Copy).then_inc(hidH_ready, 1)

                for f in range(FG):
                    high_up(0, f, fresh=True)
                high_down(0, fresh=True)
                for f in range(FG):
                    hidden(0, 0, f, fresh=True)
                    high_up(1, f)
                with act.Fori(0, NFG // 2 - 1) as it:
                    for slot in range(2):
                        g = 2 * it + slot
                        for f in range(FG):
                            hidden(g + 1, 1 - slot, f)
                            high_up(g + 2, f)
                        high_down(g + 1)
                for f in range(FG):
                    hidden(NFG - 1, 1, f)
                high_down(NFG - 1)
                act.wait_ge(hidL_ready, FG * NFG)
                for i in range(9):
                    n = P if i < 8 else NS
                    act.wait_ge(out_t, i + 1)
                    if i >= 2:
                        act.wait_ge(stored[i % 2], 16 * (i // 2))
                    nc.scalar.activation(ynat[0:n, i % 2, 0:512], ps[2 * (i % 2)][0:n, :], ACT.Copy).then_inc(out_a, 1)

            @block.vector
            def _(dve):
                def low_up(g, f):
                    dve.wait_ge(wuH_ready, FG * g + f + 1)
                    nc.vector.tensor_tensor(wuL[:, f, :, :], wu[:, :, f * P:(f + 1) * P], wuH[:, f, :, :].bitcast(F32),
                                            ALU.subtract).then_inc(wuL_ready, 1)

                def low_down(g):
                    dve.wait_ge(wdH_ready, g + 1)
                    nc.vector.tensor_tensor(wdL[:, :, :], wd[:, :, :], wdH[:, :, :].bitcast(F32), ALU.subtract).then_inc(wdL_ready, 1)

                def low_hidden(g, slot, f):
                    dve.wait_ge(hidH_ready, FG * g + f + 1)
                    nc.vector.tensor_tensor(hidL[:, slot, f, :], act2[:, f, :], hidH[:, slot, f, :].bitcast(F32),
                                            ALU.subtract).then_inc(hidL_ready, 1)

                def add_down(g):
                    for m in range(KD):
                        for third in range(NT):
                            n = m * NT + third
                            y = x2T[:, m, third * TC:(third + 1) * TC]
                            dve.wait_ge(down_done, NDN * g + n + 1)
                            nc.vector.tensor_tensor(y, ps[4 + n % 4][:, 0:TC], y, ALU.add).then_inc(added, 1)

                for f in range(FG):
                    low_up(0, f)
                low_down(0)
                for f in range(FG):
                    low_hidden(0, 0, f)
                    low_up(1, f)
                with dve.Fori(0, NFG // 2 - 1) as it:
                    for slot in range(2):
                        g = 2 * it + slot
                        for f in range(FG):
                            low_hidden(g + 1, 1 - slot, f)
                            low_up(g + 2, f)
                        add_down(g)
                        low_down(g + 1)
                for f in range(FG):
                    low_hidden(NFG - 1, 1, f)
                add_down(NFG - 2)
                low_down(NFG - 1)
                add_down(NFG - 1)
                for i in range(9):
                    n = P if i < 8 else NS
                    dve.wait_ge(out_t, i + 1)
                    if i >= 2:
                        dve.wait_ge(stored[i % 2], 16 * (i // 2))
                    nc.vector.tensor_copy(ynat[0:n, i % 2, 512:1024], ps[2 * (i % 2) + 1][0:n, :]).then_inc(out_b, 1)


_OUTS = [((1, 1024, 1024), 'float32'), ((8, 1, 1024), 'float32'), ((1, 1, 1024, 4, 2, 64), 'float32'),
         ((1, 8, 1, 4, 2, 64), 'float32'), ((1, 1, 512, 2, 2, 64), 'float32'), ((1, 8, 512, 2, 2, 64), 'float32'),
         ((1, 1, 4, 64, 64), 'float32'), ((1, 8, 4, 64, 64), 'float32'),
         ((1, 1, 4, 64, 64), 'float32'), ((1, 8, 4, 64, 64), 'float32'),
         ((1, 1, 4, 64), 'float32'), ((1, 8, 4, 64), 'float32'), ((1, 1, 4), 'float32'), ((1, 8, 4), 'float32'),
         ((1, 1, 3, 256), 'float32'), ((1, 8, 3, 256), 'float32')]


def program(nc, io):
    scratch = lambda n, s: nc.dram_tensor(f"{n}_scratch", s, F32, kind="Internal").ap()
    io["zT"] = scratch("zT", [IN_W, TT])
    io["zS"] = scratch("zS", [NS, IN_W])
    io["xT"] = scratch("xT", [D, TT])
    io["qkT"] = scratch("qkT", [6 * P, TT])
    with ExitStack() as ctx:
        sb = lambda n, s, d=F32: ctx.enter_context(nc.sbuf_tensor(n, s, d))
        keep = {"ident": sb("ident", [P, P]), "eps": sb("eps", [P, 1]), "ones": sb("ones", [P, P])}
        norm_and_project(nc, io, keep)
        keep.update({
            "g4": sb("g4", [P, 4]), "cbias": sb("cbias", [64, 2]), "w2": sb("w2", [64, 2, HD]), "b2": sb("b2", [64, 65]),
            "uact": sb("uact", [P, HP, TT]), "rows_cols": sb("rows_cols", [P, NCH, 16]),
            "hs": sb("hs", [P, NCH, 4, 65]),
            "mqk_dec": sb("mqk_dec", [P, 4, NS]), "decay_dec": sb("decay_dec", [P, HP, NS]),
            "mixS": sb("mixS", [P, KD, NS]),
        })
        keep["onat_flat"] = sb("onat", [P, KD * TT])
        keep["onat"] = keep["onat_flat"][:, 0:TQ * D].rearrange("p (i d) -> p i d", i=TQ)
        with ExitStack() as inner:
            sbi = lambda n, s, d=F32: inner.enter_context(nc.sbuf_tensor(n, s, d))
            keep.update({
                "decay": sbi("decay", [P, HP, T]), "mqk": sbi("mqk", [P, 4, TT]),
                "rows_nat": sbi("rows_nat", [P, 9, 768]), "gates_nat": sbi("gates_nat", [P, 9, 24]),
                "kcmpT": sbi("kcmpT", [64, 2, P]), "vcmp": sbi("vcmp", [P, 2, 64]),
                "v_nat": sbi("v_nat", [P, NCH, 512]), "mk_nat": sbi("mk_nat", [P, NCH, 256]), "rows": sbi("rows", [P, T]),
            })
            prepare_prompt(nc, io, keep)
            attend_prompt(nc, io, keep)
            recur_prompt(nc, io, keep)
        decode(nc, io, keep)
        x2T = keep["onat_flat"][:, :].rearrange("p (k t) -> p k t", k=KD)
        hH, hL = sb("hH", [P, KD, TT], F32R), sb("hL", [P, KD, TT], F32R)
        mix_and_project(nc, io, keep, x2T, hH, hL)
        channel_mixer(nc, io, keep, x2T, hH, hL)


def kernel(**inputs):
    import numpy as _np
    import concourse.bacc as _bacc
    from concourse import mybir as _mybir
    from concourse.bass_utils import run_bass_kernel_spmd as _run

    nc = _bacc.Bacc("TRN2", target_bir_lowering=False, num_devices=1)
    arrays, io = {}, {}
    for name in inputs:
        a = _np.ascontiguousarray(inputs[name])
        arrays[f"in_{name}_dram"] = a
        io[name] = nc.dram_tensor(f"in_{name}_dram", a.shape, _mybir.dt.from_np(a.dtype), kind="ExternalInput").ap()
    for i, (shape, dtype) in enumerate(_OUTS):
        dt = _mybir.dt.from_np(_np.dtype(dtype))
        io[f"out{i}"] = nc.dram_tensor(f"out_{i}_dram", shape, dt, kind="ExternalOutput").ap()
    with nc.allow_non_contiguous_dma(reason="short vectors and columns"):
        program(nc, io)
    r = _run(nc, [arrays], core_ids=[0])
    return tuple(r.results[0][f"out_{i}_dram"] for i in range(len(_OUTS)))
```

```python
import concourse.bass as bass
from concourse import mybir
from contextlib import ExitStack

F32 = mybir.dt.float32
F32R = mybir.dt.float32r
U32 = mybir.dt.uint32
I32 = mybir.dt.int32
ACT = mybir.ActivationFunctionType
ALU = mybir.AluOpType
AX = mybir.AxisListType
ds = bass.ds

P = 128
D = 1024
T = 1024
NS = 8
TT = T + NS
NT = 3
TC = TT // NT
KD = D // P
TQ = T // P
HD = 64
IN_W = 3120
EPS = 1e-6


def semaphores(nc, ctx, stage):
    held = []

    def give_back():
        nc.clear_and_free_semaphores(held)
        nc.all_engine_barrier()

    ctx.callback(give_back)

    def sem(name):
        held.append(nc.alloc_semaphore(f"{stage}_{name}"))
        return held[-1]

    return sem


def split_product(nc, out, weights, moving):
    n = len(weights)
    for k, ((wH, wL), (mH, mL)) in enumerate(zip(weights, moving)):
        nc.tensor.matmul(out, wH, mH, start=(k == 0), stop=False)
        nc.tensor.matmul(out, wH, mL, start=False, stop=False)
        last = nc.tensor.matmul(out, wL, mH, start=False, stop=(k == n - 1))
    return last


def norm_and_project(nc, io, keep):
    x_p = io["x_prompt"].rearrange("b t d -> (b t) d")
    x_s = io["x_sample"].rearrange("b t d -> (b t) d")
    w_in = io["w_in"].rearrange("l d n -> (l d) n").rearrange("(k p) n -> p k n", p=P)
    zT, zS = io["zT"], io["zS"]
    ident = keep["ident"]
    NM = IN_W // P
    MR = IN_W - NM * P
    with ExitStack() as ctx:
        sb = lambda n, s, d=F32: ctx.enter_context(nc.sbuf_tensor(n, s, d))
        sem = semaphores(nc, ctx, "project")
        hH, hL = sb("hH1", [P, KD, TT], F32R), sb("hL1", [P, KD, TT], F32R)
        hc = sb("hc1", [P, 2, KD, P])
        xT = sb("xT", [P, KD, TT])
        xin = sb("xin", [P, 2, D])
        xn = sb("xn", [P, 2, D])
        sq = sb("sq", [P, D])
        ss = sb("ss", [P, 2])
        rms = sb("rms", [P, 2])
        rstd = sb("rstd", [P, 2])
        eps = sb("eps1", [P, 1])
        g1 = sb("g1", [P, KD])
        win = sb("win", [P, 2, KD, P])
        winH, winL = sb("winH", [P, 2, KD, P], F32R), sb("winL", [P, 2, KD, P], F32R)
        z = sb("z", [P, 2, TT])
        zs = sb("zs", [NS, IN_W])
        ps = [ctx.enter_context(nc.psum_tensor(f"pa{i}", [P, 512], F32)) for i in range(8)]

        x_in = [sem(f"x_in{i}") for i in range(2)]
        x_used = sem("x_used")
        ss_ready, rms_ready, xn_ready = sem("ss_ready"), sem("rms_ready"), sem("xn_ready")
        xt_stored = sem("xt_stored")
        g_in, const_ready = sem("g_in"), sem("const_ready")
        xt_done, ht_done, xt_copied, ht_copied = sem("xt_done"), sem("ht_done"), sem("xt_copied"), sem("ht_copied")
        hH_ready, hL_ready, wH_ready, wL_ready = sem("hH_ready"), sem("hL_ready"), sem("wH_ready"), sem("wL_ready")
        w_loaded = [sem(f"w_loaded{i}") for i in range(2)]
        z_done, z_copied = sem("z_done"), sem("z_copied")
        z_stored = [sem(f"z_stored{i}") for i in range(2)]
        zs_done, zs_copied, zs_stored = sem("zs_done"), sem("zs_copied"), sem("zs_stored")

        with nc.Block() as block:

            @block.gpsimd
            def _(pool):
                nc.gpsimd.memset(ident[:, :], 0.0).then_inc(const_ready, 1)
                nc.gpsimd.memset(eps[:, :], EPS).then_inc(const_ready, 1)
                pool.wait_ge(const_ready, 2)
                nc.gpsimd.affine_select(out=ident[:, :], in_=ident[:, :], compare_op=ALU.not_equal, fill=1.0,
                                        base=0, pattern=[[-1, P]], channel_multiplier=1).then_inc(const_ready, 1)

            @block.sync
            def _(sp):
                sp.dma_start(g1[:, :], io["norm1_g"].rearrange("l (k p) -> p (l k)", p=P)).then_inc(g_in, 16)

                def load_x(slot, n, src):
                    sp.dma_start(xin[0:n, slot, :], src).then_inc(x_in[slot], 16)

                for slot in range(2):
                    load_x(slot, P, x_p[slot * P:(slot + 1) * P, :])
                with sp.Fori(1, TQ // 2) as it:
                    for slot in range(2):
                        sp.wait_ge(x_used, 2 * (it - 1) + slot + 1)
                        load_x(slot, P, x_p[ds((it * 2 + slot) * P, P), :])
                sp.wait_ge(x_used, TQ - 1)
                load_x(0, NS, x_s[:, :])

                for slot in range(2):
                    sp.dma_start(win[:, slot, :, :], w_in[:, :, slot * P:(slot + 1) * P]).then_inc(w_loaded[slot], 16)
                with sp.Fori(1, NM // 2) as it:
                    for slot in range(2):
                        sp.wait_ge(wL_ready, 2 * (it - 1) + slot + 1)
                        sp.dma_start(win[:, slot, :, :], w_in[:, :, ds((it * 2 + slot) * P, P)]).then_inc(w_loaded[slot], 16)
                sp.wait_ge(wL_ready, NM - 1)
                sp.dma_start(win[:, 0, :, 0:MR], w_in[:, :, NM * P:IN_W]).then_inc(w_loaded[0], 16)

            @block.tensor
            def _(pe):
                pe.wait_ge(const_ready, 3)

                def transposes(t, slot, n, loads, first=False):
                    pe.wait_ge(x_in[slot], loads)
                    if not first:
                        pe.wait_ge(xt_copied, 2 * t)
                    for k in range(KD):
                        last = nc.tensor.transpose(ps[k // 4][:, (k % 4) * P:(k % 4) * P + n],
                                                   xin[0:n, slot, k * P:(k + 1) * P], ident[0:n, 0:n])
                    last.then_inc(xt_done, 1)
                    pe.wait_ge(xn_ready, t + 1)
                    if not first:
                        pe.wait_ge(ht_copied, 2 * t)
                    for k in range(KD):
                        last = nc.tensor.transpose(ps[2 + k // 4][:, (k % 4) * P:(k % 4) * P + n],
                                                   xn[0:n, slot, k * P:(k + 1) * P], ident[0:n, 0:n])
                    last.then_inc(ht_done, 1)

                transposes(0, 0, P, 16, first=True)
                with pe.Fori(0, TQ // 2 - 1) as it:
                    for u in range(2):
                        transposes(it * 2 + 1 + u, (1 + u) % 2, P, 16 * (it + 1 + u))
                transposes(TQ - 1, 1, P, 16 * (TQ // 2))
                transposes(TQ, 0, NS, 16 * (TQ // 2 + 1))

                pe.wait_ge(hL_ready, TQ + 1)
                pe.wait_ge(xt_copied, 2 * (TQ + 1))

                def product(m, slot, cols, freed):
                    pe.wait_ge(wH_ready, m + 1)
                    pe.wait_ge(wL_ready, m + 1)
                    if freed is not None:
                        pe.wait_ge(z_copied, freed)
                    for third in range(NT):
                        at = slice(third * TC, (third + 1) * TC)
                        split_product(nc, ps[slot * 3 + third][0:cols, 0:TC],
                                      [(winH[:, slot, k, 0:cols], winL[:, slot, k, 0:cols]) for k in range(KD)],
                                      [(hH[:, k, at], hL[:, k, at]) for k in range(KD)]).then_inc(z_done, 1)

                def decoded(m, slot, cols, freed):
                    pe.wait_ge(z_copied, NT * m + NT)
                    if freed is not None:
                        pe.wait_ge(zs_copied, freed)
                    nc.tensor.transpose(ps[6 + slot][0:NS, 0:cols], z[0:cols, slot, T:TT],
                                        ident[0:cols, 0:cols]).then_inc(zs_done, 1)

                product(0, 0, P, None)
                product(1, 1, P, None)
                decoded(0, 0, P, None)
                product(2, 0, P, NT)
                decoded(1, 1, P, None)
                product(3, 1, P, 2 * NT)
                with pe.Fori(2, NM // 2) as it:
                    for slot in range(2):
                        m = it * 2 + slot
                        decoded(m - 2, slot, P, m - 3)
                        product(m, slot, P, NT * (m - 1))
                decoded(NM - 2, 0, P, NM - 3)
                product(NM, 0, MR, NT * (NM - 1))
                decoded(NM - 1, 1, P, NM - 2)
                decoded(NM, 0, MR, NM - 1)

            @block.scalar
            def _(act):
                def row_square(t, slot, n, loads, first=False):
                    act.wait_ge(x_in[slot], loads)
                    if not first:
                        act.wait_ge(xn_ready, t)
                    nc.scalar.activation(sq[0:n, :], xin[0:n, slot, :], ACT.Square, accum_out=ss[0:n, slot:slot + 1])
                    nc.scalar.drain()
                    nc.scalar.activation(rms[0:n, slot:slot + 1], ss[0:n, slot:slot + 1], ACT.Sqrt,
                                         scale=1.0 / D, bias=eps[0:n, :]).then_inc(rms_ready, 1)
                    act.wait_ge(xt_done, t + 1)
                    for half in range(2):
                        nc.scalar.activation(xT[:, half * 4:half * 4 + 4, ds(t * P, n)],
                                             ps[half][:, :].rearrange("p (k t) -> p k t", k=4)[:, :, 0:n],
                                             ACT.Copy).then_inc(xt_copied, 1)
                    act.wait_ge(ht_copied, 2 * t + 2)
                    nc.scalar.activation(hH[:, :, ds(t * P, n)], hc[:, slot, :, 0:n], ACT.Copy).then_inc(hH_ready, 1)

                def high_weights(m, slot, cols, loads, used):
                    act.wait_ge(w_loaded[slot], loads)
                    if used is not None:
                        act.wait_ge(z_done, used)
                    nc.scalar.activation(winH[:, slot, :, 0:cols], win[:, slot, :, 0:cols], ACT.Copy).then_inc(wH_ready, 1)

                act.wait_ge(const_ready, 3)
                row_square(0, 0, P, 16, first=True)
                with act.Fori(0, TQ // 2 - 1) as it:
                    for u in range(2):
                        row_square(it * 2 + 1 + u, (1 + u) % 2, P, 16 * (it + 1 + u))
                row_square(TQ - 1, 1, P, 16 * (TQ // 2))
                row_square(TQ, 0, NS, 16 * (TQ // 2 + 1))
                for slot in range(2):
                    high_weights(slot, slot, P, 16, None)
                act.wait_ge(xt_copied, 2 * (TQ + 1))
                for k in range(KD):
                    act.dma_start(io["xT"][k * P:(k + 1) * P, :], xT[:, k, :]).then_inc(xt_stored, 16)

                def copy_z(m, slot, cols, stored):
                    if stored is not None:
                        act.wait_ge(z_stored[slot], stored)
                        act.wait_ge(zs_done, m - 1)
                    for third in range(NT):
                        act.wait_ge(z_done, NT * m + third + 1)
                        nc.scalar.activation(z[0:cols, slot, third * TC:(third + 1) * TC], ps[slot * 3 + third][0:cols, 0:TC],
                                             ACT.Copy).then_inc(z_copied, 1)
                    act.wait_ge(z_copied, NT * m + NT)
                    act.dma_start(zT[ds(m * P, cols), :], z[0:cols, slot, :]).then_inc(z_stored[slot], 16)

                copy_z(0, 0, P, None)
                high_weights(2, 0, P, 32, NT)
                copy_z(1, 1, P, None)
                high_weights(3, 1, P, 32, 2 * NT)
                with act.Fori(1, NM // 2 - 1) as it:
                    for slot in range(2):
                        m = it * 2 + slot
                        copy_z(m, slot, P, 16 * it)
                        high_weights(m + 2, slot, P, 16 * (it + 2), NT * (m + 1))
                copy_z(NM - 2, 0, P, 16 * (NM // 2 - 1))
                high_weights(NM, 0, MR, 16 * (NM // 2 + 1), NT * (NM - 1))
                copy_z(NM - 1, 1, P, 16 * (NM // 2 - 1))
                copy_z(NM, 0, MR, 16 * (NM // 2))
                act.wait_ge(z_stored[0], 16 * (NM // 2 + 1))
                act.wait_ge(z_stored[1], 16 * (NM // 2))
                act.wait_ge(xt_stored, 16 * KD)
                act.wait_ge(zs_copied, NM + 1)
                act.dma_start(zS[:, :], zs[:, :]).then_inc(zs_stored, 16)
                act.wait_ge(zs_stored, 16)

            @block.vector
            def _(dve):
                dve.wait_ge(g_in, 16)

                def normalise(t, slot, n):
                    dve.wait_ge(rms_ready, t + 1)
                    nc.vector.reciprocal(rstd[0:n, slot:slot + 1], rms[0:n, slot:slot + 1])
                    nc.vector.drain()
                    nc.vector.tensor_scalar(xn[0:n, slot, :], xin[0:n, slot, :], rstd[0:n, slot:slot + 1], None,
                                            ALU.mult).then_inc(xn_ready, 1)
                    dve.wait_ge(ht_done, t + 1)
                    dve.wait_ge(xt_done, t + 1)
                    for half in range(2):
                        last = nc.vector.tensor_tensor(
                            hc[:, slot, half * 4:half * 4 + 4, 0:n],
                            ps[2 + half][:, :].rearrange("p (k t) -> p k t", k=4)[:, :, 0:n],
                            g1[:, half * 4:half * 4 + 4].unsqueeze(2).broadcast_to([P, 4, n]), ALU.mult)
                        last.then_inc(ht_copied, 1)
                    nc.vector.engine_nop().then_inc(x_used, 1)
                    dve.wait_ge(hH_ready, t + 1)
                    nc.vector.tensor_tensor(hL[:, :, ds(t * P, n)], hc[:, slot, :, 0:n], hH[:, :, ds(t * P, n)].bitcast(F32),
                                            ALU.subtract).then_inc(hL_ready, 1)

                normalise(0, 0, P)
                with dve.Fori(0, TQ // 2 - 1) as it:
                    for u in range(2):
                        normalise(it * 2 + 1 + u, (1 + u) % 2, P)
                normalise(TQ - 1, 1, P)
                normalise(TQ, 0, NS)

                def copy_decoded(m, slot, cols):
                    dve.wait_ge(zs_done, m + 1)
                    nc.vector.tensor_copy(zs[:, ds(m * P, cols)], ps[6 + slot][0:NS, 0:cols]).then_inc(zs_copied, 1)

                def low_weights(m, slot, cols):
                    dve.wait_ge(wH_ready, m + 1)
                    nc.vector.tensor_tensor(winL[:, slot, :, 0:cols], win[:, slot, :, 0:cols], winH[:, slot, :, 0:cols].bitcast(F32),
                                            ALU.subtract).then_inc(wL_ready, 1)

                low_weights(0, 0, P)
                low_weights(1, 1, P)
                with dve.Fori(0, NM // 2 - 1) as it:
                    for slot in range(2):
                        m = it * 2 + slot
                        low_weights(m + 2, slot, P)
                        copy_decoded(m, slot, P)
                low_weights(NM, 0, MR)
                copy_decoded(NM - 2, 0, P)
                copy_decoded(NM - 1, 1, P)
                copy_decoded(NM, 0, MR)


GQ, GK, GV, GR, GA = 0, 256, 512, 768, 1024
NQ, NG, MU, MV, MI, MF, MO = 1040, 2320, 2344, 2600, 2856, 2860, 2864
HP = 2
CH = 128
NCH = T // CH
NB = T // 16 - 1
Q_TILES = (0, 1, 2, 3, 6, 8)


def prepare_prompt(nc, io, keep):
    zT = io["zT"]
    ident, eps = keep["ident"], keep["eps"]
    nat, gnat = keep["rows_nat"], keep["gates_nat"]
    kcmp, vcmp = keep["kcmpT"], keep["vcmp"]
    decay, vnat, mqk, mknat = keep["decay"], keep["v_nat"], keep["mqk"], keep["mk_nat"]
    R, RN, uact = keep["rows"], keep["rows_cols"], keep["uact"]
    cbias, w2 = keep["cbias"], keep["w2"]
    b2 = keep["b2"]
    with ExitStack() as ctx:
        sb = lambda n, s, d=F32: ctx.enter_context(nc.sbuf_tensor(n, s, d))
        sem = semaphores(nc, ctx, "prepare")
        zin = sb("zin", [P, 10, TT])
        sqt = sb("sqt", [P, 2, TT])
        rtum = sb("rtum", [P, HP * (3 + TT)])
        rt = rtum[:, 0:2 * TT].rearrange("p (k t) -> p k t", k=2)
        um = rtum[:, :].rearrange("p (k t) -> p k t", k=HP)
        g4 = keep["g4"]
        blk1 = sb("blk1", [P, P])
        ga = uact[0:16, 0, :]
        aw = sb("aw", [16, 256])
        ab = sb("ab", [P, HP])
        spare = keep["onat_flat"]
        gv = spare[:, 0:4 * TT].rearrange("p (j t) -> p j t", j=4)
        t1, t2 = spare[:, 4 * TT:5 * TT], spare[:, 5 * TT:6 * TT]
        resets = spare[:, 6 * TT:6 * TT + T].rearrange("p (i t) -> p i t", t=CH)
        st_nat = sb("st_nat", [3 * NS, 256])
        stT = sb("stT", [P, HP, NS, 3])
        wc = sb("wc", [P, HP, 4])
        bc = sb("bc", [P, HP])
        bd = sb("bd", [P, 4, P])
        spare2 = keep["hs"][:, :, :, :].rearrange("p i h e -> p (i h e)")
        gates = spare2[:, 0:TT]
        gi, ngt = gates[0:4, :], gates[32:56, :]
        gf = spare2[0:4, TT:2 * TT]
        gbias = sb("gbias", [4, 2])
        mm = sb("mm", [4, 1 + T])
        fc = sb("fc", [4, T])
        ngb = sb("ngb", [P, 1])[32:56, :]
        pe_nat = sb("pe_nat", [64, HD])
        peT = sb("peT", [64, 64])
        kcv = zin[0:64, 0:4, 0:T].rearrange("d (s h) t -> d s h t", s=2)
        w1c = zin[0:64, 4:8, 0:T].rearrange("d (s a) (r b e) -> d s a r b e", s=2, r=8, b=2)
        hi = sb("hi", [64, 2, 2, 64])
        hid = sb("hid", [64, 2, 2, 64])
        sg = sb("sg", [64, 2, 2, 64])
        ksq = sb("ksq", [64, 2, 64])
        krt = sb("krt", [64, 2, 64])
        b1 = sb("b1", [64, 2])
        ones = keep["ones"]
        pq = [ctx.enter_context(nc.psum_tensor(f"pq{i}", [P, 512], F32)) for i in range(3)]
        pn = [ctx.enter_context(nc.psum_tensor(f"pn{i}", [P, 512], F32)) for i in range(2)]
        pl = [ctx.enter_context(nc.psum_tensor(f"pl{i}", [P, 512], F32)) for i in range(3)]

        zin_in = [sem(f"zin_in{j}") for j in range(10)]
        small_in, gla_in, conv_in, cmp_in, zeroed, pads_zeroed = (sem("small_in"), sem("gla_in"), sem("conv_in"), sem("cmp_in"),
                                                     sem("zeroed"), sem("pads_zeroed"))
        sq_ready, ssq_done, rt_ready, qn_ready = sem("sq_ready"), sem("ssq_done"), sem("rt_ready"), sem("qn_ready")
        la_done, ls_abs, ls_ln, ls_min, scanned = sem("la_done"), sem("ls_abs"), sem("ls_ln"), sem("ls_min"), sem("scanned")
        st_done, st_copied, conv_done, sig_done, u_ready = (sem("st_done"), sem("st_copied"), sem("conv_done"),
                                                            sem("sig_done"), sem("u_ready"))
        mqk_done, mqk_copied = sem("mqk_done"), sem("mqk_copied")
        rows_ready, m_ready, em_ready, gates_ready, gates_done, gates_copied = (
            sem("rows_ready"), sem("m_ready"), sem("em_ready"), sem("gates_ready"), sem("gates_done"), sem("gates_copied"))
        nA_done, nB_done, nA_copied, nB_copied = sem("nA_done"), sem("nB_done"), sem("nA_copied"), sem("nB_copied")
        pe_done, pe_copied, cb_done, cb_ready, hid_done, hi_copied, hid_ready, act_sig, act_ready = (
            sem("pe_done"), sem("pe_copied"), sem("cb_done"), sem("cb_ready"), sem("hid_done"), sem("hi_copied"),
            sem("hid_ready"), sem("act_sig"), sem("act_ready"))
        kc_done, kc_copied, kss_done, krt_ready, kn_ready, vc_done, vc_copied = (
            sem("kc_done"), sem("kc_copied"), sem("kss_done"), sem("krt_ready"), sem("kn_ready"), sem("vc_done"), sem("vc_copied"))
        out_done, q_stored, um_zeroed = sem("out_done"), sem("q_stored"), sem("um_zeroed")

        with nc.Block() as block:

            @block.gpsimd
            def _(pool):
                nc.gpsimd.memset(eps[:, :], EPS)
                nc.gpsimd.memset(blk1[:, :], 0.0)
                nc.gpsimd.memset(ones[:, :], 1.0)
                nc.gpsimd.memset(bd[:, :, :], 0.0)
                nc.gpsimd.memset(R[:, :], 0.0)
                nc.gpsimd.memset(vcmp[:, :, :], 0.0)
                nc.gpsimd.drain()
                nc.gpsimd.memset(kcmp[:, :, :], 0.0)
                nc.gpsimd.drain()
                nc.gpsimd.memset(resets[:, :, :], 1.0)
                nc.gpsimd.drain()
                nc.gpsimd.memset(mm[:, 0:1], 0.0).then_inc(zeroed, 1)
                pool.wait_ge(zeroed, 1)
                nc.gpsimd.memset(blk1[0:64, 0:64], 1.0)
                nc.gpsimd.drain()
                nc.gpsimd.memset(blk1[64:128, 64:128], 1.0)
                nc.gpsimd.drain()
                nc.gpsimd.memset(resets[:, :, 0:1], 0.0).then_inc(pads_zeroed, 1)
                pool.wait_ge(qn_ready, len(Q_TILES))
                nc.gpsimd.memset(um[:, :, 0:3], 0.0).then_inc(um_zeroed, 1)

            @block.sync
            def _(sp):
                for j in range(10):
                    sp.dma_start(zin[:, j, :], zT[NQ + j * P:NQ + (j + 1) * P, :]).then_inc(zin_in[j], 16)
                for half in range(2):
                    sp.dma_start(g4[half * 64:half * 64 + 64, :], io["nsa_qk_g"].rearrange("l k d -> d (l k)")).then_inc(small_in, 16)
                sp.dma_start(ngb[:, :], io["nsa_gate_b"].rearrange("l k -> k l")).then_inc(small_in, 16)
                sp.dma_start(ngt[:, :], zT[NG:NG + 24, :]).then_inc(small_in, 16)
                sp.dma_start(gbias[:, :], io["ml_gate_b"].rearrange("l k h -> h (l k)")).then_inc(small_in, 16)
                sp.dma_start(gi[:, :], zT[MI:MI + 4, :]).then_inc(small_in, 16)
                sp.dma_start(gf[:, :], zT[MF:MF + 4, :]).then_inc(small_in, 16)
                sp.dma_start(gv[:, 0:2, :], zT[GV:GV + 2 * P, :].rearrange("(j p) t -> p j t", p=P)).then_inc(gla_in, 16)
                sp.dma_start(gv[:, 2:4, :], zT[MV:MV + 2 * P, :].rearrange("(j p) t -> p j t", p=P)).then_inc(gla_in, 16)
                sp.dma_start(ga[:, :], zT[GA:GA + 16, :]).then_inc(gla_in, 16)
                sp.dma_start(aw[:, :], io["gla_a_w"].rearrange("l k n -> (l k) n")).then_inc(gla_in, 16)
                sp.dma_start(ab[:, :], io["gla_a_b"].rearrange("l (j p) -> p (l j)", p=P)).then_inc(gla_in, 16)
                sp.dma_start(st_nat[:, :], io["state_mlstm_conv"].rearrange("l s j c -> (l s j) c")).then_inc(conv_in, 16)
                for hp in range(HP):
                    sp.dma_start(wc[:, hp, :], io["ml_conv_w"][0, :, hp * P:(hp + 1) * P].rearrange("j p -> p j")).then_inc(conv_in, 16)
                sp.dma_start(bc[:, :], io["ml_conv_b"].rearrange("l (k p) -> p (l k)", p=P)).then_inc(conv_in, 16)
                sp.wait_ge(pads_zeroed, 1)
                for idx in range(4):
                    w = io["ml_wq"] if idx < 2 else io["ml_wk"]
                    for h2 in range(2):
                        sp.dma_start(bd[h2 * 64:h2 * 64 + 64, idx, h2 * 64:h2 * 64 + 64],
                                     w[0, (idx % 2) * 2 + h2, :, :]).then_inc(conv_in, 16)
                for n, j in enumerate(Q_TILES):
                    sp.wait_ge(qn_ready, n + 1)
                    sp.dma_start(io["qkT"][n * P:(n + 1) * P, :], zin[:, j, :]).then_inc(q_stored, 16)
                sp.wait_ge(um_zeroed, 1)
                sp.dma_start(um[:, :, 3:3 + TT], zT[MU:MU + 2 * P, :].rearrange("(j p) t -> p j t", p=P)).then_inc(conv_in, 16)
                sp.wait_ge(conv_in, 16 * 13)
                for hp in range(HP):
                    sp.dma_start(io["out14"][0, 0, :, hp * P:(hp + 1) * P].rearrange("j p -> p j"), um[:, hp, T:T + 3]).then_inc(out_done, 16)
                sp.dma_start(io["out15"][0, :, 0:2, :], io["state_mlstm_conv"][0, :, 1:3, :]).then_inc(out_done, 16)
                sp.dma_start(io["out15"][0, :, 2, :], io["zS"][:, MU:MU + 256]).then_inc(out_done, 16)
                sp.wait_ge(nA_copied, 9)
                sp.wait_ge(nB_copied, 9)
                sp.dma_start(io["out2"].rearrange("l b (i p) k h d -> p (l b i) (k h d)", p=P), nat[:, 0:TQ, 0:512]).then_inc(out_done, 16)
                sp.dma_start(io["out4"].rearrange("l b (i p) k h d -> p (l b i) (k h d)", p=P), nat[:, 4:TQ, 512:768]).then_inc(out_done, 16)
                sp.dma_start(io["out3"].rearrange("l b t k h d -> (l b t) (k h d)"), nat[0:NS, TQ, 0:512]).then_inc(out_done, 16)
                sp.dma_start(io["out5"][0, :, 511, :, :, :].rearrange("b k h d -> b (k h d)"), nat[0:NS, TQ, 512:768]).then_inc(out_done, 16)
                for s in range(NS):
                    sp.dma_start(io["out5"][0, s, 0:511, :, :, :].rearrange("t k h d -> t (k h d)"),
                                 io["cache_nsa_win"][0, s, 1:512, :, :, :].rearrange("t k h d -> t (k h d)")).then_inc(out_done, 16)
                sp.wait_ge(q_stored, 16 * len(Q_TILES))
                sp.dma_start(pe_nat[:, :], io["cmp_pe"].rearrange("l s r d -> (l s r) d")).then_inc(cmp_in, 16)
                for slot in range(2):
                    for half in range(2):
                        for a in range(2):
                            at = half * 16 + a * 8
                            sp.dma_start(w1c[:, slot, a, :, half, :],
                                         io["cmp_w1"][0, slot, at:at + 8, :, :].rearrange("r d e -> d r e")).then_inc(cmp_in, 16)
                sp.dma_start(w2[:, :, :], io["cmp_w2"].rearrange("l s e d -> e (l s) d")).then_inc(cmp_in, 16)
                sp.dma_start(b1[:, :], io["cmp_b1"].rearrange("l s e -> e (l s)")).then_inc(cmp_in, 16)
                sp.dma_start(b2[:, 0:1], io["cmp_b2"][0, 0:1, :].rearrange("l d -> d l")).then_inc(cmp_in, 16)
                sp.dma_start(b2[0:1, 1:65], io["cmp_b2"][0, 1:2, :]).then_inc(cmp_in, 16)
                for slot in range(2):
                    for h in range(2):
                        at = NQ + (4 + slot) * P + h * 64
                        sp.dma_start(kcv[:, slot, h, :], zT[at:at + 64, 0:T]).then_inc(cmp_in, 16)
                sp.wait_ge(m_ready, 1)
                sp.dma_start(io["out12"].rearrange("l b h -> h (l b)"), mm[:, T:T + 1]).then_inc(out_done, 16)
                sp.wait_ge(out_done, 16 * (4 + 4 + NS + 1))

            @block.tensor
            def _(pe):
                pe.wait_ge(pads_zeroed, 1)
                for n, j in enumerate(Q_TILES):
                    pe.wait_ge(sq_ready, n + 1)
                    if n:
                        pe.wait_ge(rt_ready, 3 * n)
                    for third in range(NT):
                        nc.tensor.matmul(pq[third][:, 0:TC], blk1[:, :], sqt[:, n % 2, third * TC:(third + 1) * TC],
                                         start=True, stop=True).then_inc(ssq_done, 1)
                pe.wait_ge(gla_in, 16 * 5)
                for hp in range(HP):
                    if hp:
                        pe.wait_ge(ls_abs, NT)
                        pe.wait_ge(ls_min, NT)
                    for third in range(NT):
                        nc.tensor.matmul(pl[third][:, 0:TC], aw[:, hp * P:(hp + 1) * P], ga[:, third * TC:(third + 1) * TC],
                                         start=True, stop=True).then_inc(la_done, 1)
                pe.wait_ge(conv_in, 16 * 13)
                for hp in range(HP):
                    nc.tensor.transpose(pn[0][:, hp * 32:hp * 32 + 24], st_nat[:, hp * P:(hp + 1) * P],
                                        ident[0:24, 0:24]).then_inc(st_done, 1)
                pe.wait_ge(ls_abs, 2 * NT)
                pe.wait_ge(ls_min, 2 * NT)
                pe.wait_ge(u_ready, HP)
                for idx in range(4):
                    for third in range(NT):
                        if idx:
                            pe.wait_ge(mqk_copied, (idx - 1) * NT + third + 1)
                        nc.tensor.matmul(pl[third][:, 0:TC], bd[:, idx, :], uact[:, idx % 2, third * TC:(third + 1) * TC],
                                         start=True, stop=True).then_inc(mqk_done, 1)
                pe.wait_ge(qn_ready, len(Q_TILES))
                for j in (4, 5, 7, 9):
                    pe.wait_ge(zin_in[j], 16)
                pe.wait_ge(st_copied, 1)
                for i in range(9):
                    n = P if i < 8 else NS
                    if i:
                        pe.wait_ge(nA_copied, i)
                    for c in range(4):
                        last = nc.tensor.transpose(pn[0][0:n, c * P:(c + 1) * P], zin[:, 4 + c, i * P:i * P + n], ident[:, :])
                    last.then_inc(nA_done, 1)
                    if i:
                        pe.wait_ge(nB_copied, i)
                    for c in range(2):
                        last = nc.tensor.transpose(pn[1][0:n, c * P:(c + 1) * P], zin[:, 8 + c, i * P:i * P + n], ident[:, :])
                    last.then_inc(nB_done, 1)
                pe.wait_ge(rows_ready, 4)
                pe.wait_ge(mqk_copied, 4 * NT)
                for i in range(NCH):
                    pe.wait_ge(nA_copied, 9 + i)
                    for c in range(4):
                        last = nc.tensor.transpose(pn[0][:, c * P:(c + 1) * P], gv[:, c, i * P:(i + 1) * P], ident[:, :])
                    last.then_inc(nA_done, 1)
                    pe.wait_ge(nB_copied, 9 + i)
                    for c in range(2):
                        nc.tensor.transpose(pn[1][:, c * P:(c + 1) * P], mqk[:, 2 + c, i * P:(i + 1) * P], ident[:, :])
                    nc.tensor.transpose(pn[1][:, 256:384], R[:, i * P:(i + 1) * P], ident[:, :]).then_inc(nB_done, 1)
                pe.wait_ge(gates_ready, 1)
                pe.wait_ge(rt_ready, 3 * len(Q_TILES))
                for i in range(9):
                    n = P if i < 8 else NS
                    last = nc.tensor.transpose(pq[0][0:n, i * 24:(i + 1) * 24], ngt[:, i * P:i * P + n], ident[32:56, 32:56])
                last.then_inc(gates_done, 1)
                pe.wait_ge(cmp_in, 16 * 17)
                nc.tensor.transpose(pq[1][0:64, 0:64], pe_nat[:, :], ident[0:64, 0:64]).then_inc(pe_done, 1)
                pe.wait_ge(pe_copied, 1)
                for slot in range(2):
                    for half in range(2):
                        for r in range(16):
                            c = slot * 32 + half * 16 + r
                            last = nc.tensor.matmul(pq[2][0:64, slot:slot + 1], w1c[:, slot, r // 8, r % 8, half, :], peT[:, c:c + 1],
                                                    start=(half == 0 and r == 0), stop=(half == 1 and r == 15))
                last.then_inc(cb_done, 1)
                for slot in range(2):
                    for r in range(16):
                        last = nc.tensor.matmul(pl[slot][:, 0:128], w1c[:, slot, r // 8, r % 8, :, :],
                                                kcv[:, slot, :, :].rearrange("d h (n r) -> d h n r", r=16)[:, :, :, r],
                                                start=(r == 0), stop=(r == 15))
                    last.then_inc(hid_done, 1)
                pe.wait_ge(act_ready, 1)
                nc.tensor.matmul(pl[2][0:64, 0:2 * NB], w2[:, 0, :], hid[:, 0, :, 0:NB], start=True, stop=True).then_inc(kc_done, 1)
                pe.wait_ge(act_ready, 2)
                pe.wait_ge(hi_copied, 2)
                pe.wait_ge(hid_ready, 2)
                for h in range(2):
                    nc.tensor.matmul(pl[0][0:NB, h * 64:h * 64 + 64], hid[:, 1, h, 0:NB], w2[:, 1, :], start=True, stop=False)
                    last = nc.tensor.matmul(pl[0][0:NB, h * 64:h * 64 + 64], ones[0:1, 0:NB], b2[0:1, 1:65], start=False, stop=True)
                last.then_inc(vc_done, 1)
                pe.wait_ge(kc_copied, 2)
                nc.tensor.matmul(pl[1][0:64, 0:2 * NB], blk1[0:64, 0:64], ksq[:, :, 0:NB], start=True, stop=True).then_inc(kss_done, 1)

            @block.scalar
            def _(act):
                act.wait_ge(pads_zeroed, 1)

                def square(n):
                    act.wait_ge(zin_in[Q_TILES[n]], 16)
                    if n >= 2:
                        act.wait_ge(ssq_done, 3 * (n - 1))
                    nc.scalar.activation(sqt[:, n % 2, :], zin[:, Q_TILES[n], :], ACT.Square).then_inc(sq_ready, 1)

                square(0)
                for n in range(len(Q_TILES)):
                    if n + 1 < len(Q_TILES):
                        square(n + 1)
                    if n >= 2:
                        act.wait_ge(qn_ready, n - 1)
                    for third in range(NT):
                        act.wait_ge(ssq_done, 3 * n + third + 1)
                        nc.scalar.activation(rt[:, n % 2, third * TC:(third + 1) * TC], pq[third][:, 0:TC], ACT.Sqrt,
                                             scale=1.0 / HD, bias=eps[:, :]).then_inc(rt_ready, 1)

                for hp in range(HP):
                    if hp:
                        act.wait_ge(scanned, hp)
                    for third in range(NT):
                        act.wait_ge(la_done, hp * NT + third + 1)
                        nc.scalar.activation(t1[:, third * TC:(third + 1) * TC], pl[third][:, 0:TC], ACT.Abs,
                                             bias=ab[:, hp:hp + 1]).then_inc(ls_abs, 1)
                    nc.scalar.drain()
                    nc.scalar.activation(t1[:, :], t1[:, :], ACT.Exp, scale=-1.0)
                    nc.scalar.drain()
                    nc.scalar.activation(t1[:, :], t1[:, :], ACT.Ln, bias=1.0).then_inc(ls_ln, 1)
                act.wait_ge(scanned, HP)
                act.wait_ge(small_in, 16 * 7)
                nc.scalar.activation(t1[0:4, :], gf[:, :], ACT.Abs, bias=gbias[:, 1:2])
                nc.scalar.drain()
                nc.scalar.activation(t1[0:4, :], t1[0:4, :], ACT.Exp, scale=-1.0)
                nc.scalar.drain()
                nc.scalar.activation(t1[0:4, :], t1[0:4, :], ACT.Ln, bias=1.0).then_inc(ls_ln, 1)
                act.wait_ge(em_ready, 1)
                nc.scalar.activation(R[64:68, :], fc[:, :], ACT.Exp).then_inc(rows_ready, 1)
                nc.scalar.activation(R[96:100, :], mm[:, 1:1 + T], ACT.Exp, scale=-1.0).then_inc(rows_ready, 1)
                act.wait_ge(st_done, 2)
                nc.scalar.activation(stT[:, :, :, :], pn[0][:, 0:64].rearrange("p (k c) -> p k c", k=2)[:, :, 0:24]
                                     .rearrange("p k (s j) -> p k s j", j=3), ACT.Copy).then_inc(st_copied, 1)
                for hp in range(HP):
                    act.wait_ge(conv_done, hp + 1)
                    nc.scalar.activation(sqt[:, hp, :], uact[:, hp, :], ACT.Sigmoid).then_inc(sig_done, 1)
                nc.scalar.activation(ngt[:, :], ngt[:, :], ACT.Sigmoid, bias=ngb[:, :]).then_inc(gates_ready, 1)
                for idx in range(4):
                    for third in range(NT):
                        act.wait_ge(mqk_done, idx * NT + third + 1)
                        nc.scalar.activation(mqk[:, idx, third * TC:(third + 1) * TC], pl[third][:, 0:TC], ACT.Copy,
                                             scale=1.0 if idx < 2 else HD ** -0.5).then_inc(mqk_copied, 1)
                nc.scalar.drain()
                nc.scalar.activation(keep["mqk_dec"][:, :, :], mqk[:, :, T:TT], ACT.Copy)
                for i in range(9):
                    n = P if i < 8 else NS
                    act.wait_ge(nB_done, i + 1)
                    nc.scalar.activation(nat[0:n, i, 512:768], pn[1][0:n, 0:256], ACT.Copy).then_inc(nB_copied, 1)
                for i in range(NCH):
                    act.wait_ge(nB_done, 9 + i + 1)
                    nc.scalar.activation(mknat[:, i, :], pn[1][:, 0:256], ACT.Copy)
                    nc.scalar.activation(RN[:, i, :].rearrange("p (k h) -> p k h", h=4),
                                         pn[1][:, 256:384].rearrange("p (k c) -> p k c", k=4)[:, :, 0:4], ACT.Copy).then_inc(nB_copied, 1)
                act.wait_ge(gates_done, 1)
                nc.scalar.activation(gnat[:, 0:8, :], pq[0][:, 0:192].rearrange("p (i c) -> p i c", c=24), ACT.Copy)
                nc.scalar.activation(gnat[0:NS, 8, :], pq[0][0:NS, 192:216], ACT.Copy).then_inc(gates_copied, 1)
                act.wait_ge(pe_done, 1)
                nc.scalar.activation(peT[:, :], pq[1][0:64, 0:64], ACT.Copy).then_inc(pe_copied, 1)
                for slot in range(2):
                    act.wait_ge(hid_done, slot + 1)
                    nc.scalar.activation(hi[:, slot, :, :], pl[slot][64:128, 0:128].rearrange("p (h n) -> p h n", h=2),
                                         ACT.Copy).then_inc(hi_copied, 1)
                act.wait_ge(cb_ready, 1)
                for slot in range(2):
                    act.wait_ge(hid_ready, slot + 1)
                    nc.scalar.activation(sg[:, slot, :, 0:NB], hid[:, slot, :, 0:NB], ACT.Sigmoid,
                                         bias=cbias[:, slot:slot + 1]).then_inc(act_sig, 1)
                act.wait_ge(kc_done, 1)
                kv = pl[2][0:64, 0:2 * NB].rearrange("p (h n) -> p h n", h=2)
                nc.scalar.activation(kcmp[:, :, 0:NB], kv, ACT.Identity, bias=b2[:, 0:1]).then_inc(kc_copied, 1)
                nc.scalar.activation(ksq[:, :, 0:NB], kv, ACT.Square, bias=b2[:, 0:1]).then_inc(kc_copied, 1)
                act.wait_ge(vc_done, 1)
                nc.scalar.activation(vcmp[0:NB, :, :], pl[0][0:NB, 0:128].rearrange("p (h d) -> p h d", h=2), ACT.Copy).then_inc(vc_copied, 1)
                act.wait_ge(kss_done, 1)
                nc.scalar.activation(krt[:, :, 0:NB], pl[1][0:64, 0:2 * NB].rearrange("p (h n) -> p h n", h=2), ACT.Sqrt,
                                     scale=1.0 / HD, bias=eps[0:64, :]).then_inc(krt_ready, 1)

            @block.vector
            def _(dve):
                dve.wait_ge(pads_zeroed, 1)
                dve.wait_ge(small_in, 16 * 7)
                nc.vector.tensor_scalar(g4[:, 0:1], g4[:, 0:1], HD ** -0.5, None, ALU.mult)
                nc.vector.drain()
                for n, j in enumerate(Q_TILES):
                    gain = g4[:, 0:1] if j < 4 else g4[:, 2:3] if j == 6 else g4[:, 3:4]
                    dve.wait_ge(rt_ready, 3 * n + 3)
                    nc.vector.reciprocal(rt[:, n % 2, :], rt[:, n % 2, :])
                    nc.vector.drain()
                    nc.vector.scalar_tensor_tensor(out=zin[:, j, :], in0=zin[:, j, :], scalar=gain, in1=rt[:, n % 2, :],
                                                   op0=ALU.mult, op1=ALU.mult).then_inc(qn_ready, 1)
                dve.wait_ge(gla_in, 16 * 5)
                for hp in range(HP):
                    for third in range(NT):
                        dve.wait_ge(ls_abs, hp * NT + third + 1)
                        nc.vector.tensor_scalar(t2[:, third * TC:(third + 1) * TC], pl[third][:, 0:TC], ab[:, hp:hp + 1], 0.0,
                                                ALU.add, ALU.min).then_inc(ls_min, 1)
                    dve.wait_ge(ls_ln, hp + 1)
                    nc.vector.drain()
                    nc.vector.tensor_tensor(t2[:, :], t2[:, :], t1[:, :], ALU.subtract)
                    nc.vector.drain()
                    nc.vector.tensor_tensor_scan(decay[:, hp, 0:T], resets[:, :, :].rearrange("p i t -> p (i t)"), t2[:, 0:T],
                                                 0.0, ALU.mult, ALU.add)
                    nc.vector.tensor_copy(keep["decay_dec"][:, hp, :], t2[:, T:TT]).then_inc(scanned, 1)
                    nc.vector.drain()
                dve.wait_ge(ls_ln, 3)
                nc.vector.tensor_scalar(gf[:, :], gf[:, :], gbias[:, 1:2], 0.0, ALU.add, ALU.min)
                nc.vector.tensor_scalar(gi[:, :], gi[:, :], gbias[:, 0:1], None, ALU.add)
                nc.vector.drain()
                nc.vector.tensor_tensor(gf[:, :], gf[:, :], t1[0:4, :], ALU.subtract)
                nc.vector.drain()
                nc.vector.tensor_tensor_scan(mm[:, 1:1 + T], gf[:, 0:T], gi[:, 0:T], 0.0, ALU.add, ALU.max).then_inc(m_ready, 1)
                nc.vector.tensor_tensor_scan(fc[:, :], resets[0:4, :, :].rearrange("p i t -> p (i t)"), gf[:, 0:T], 0.0, ALU.mult, ALU.add)
                nc.vector.drain()
                nc.vector.tensor_tensor(R[0:4, :], fc[:, :], mm[:, 1:1 + T], ALU.subtract).then_inc(rows_ready, 1)
                nc.vector.tensor_tensor(R[32:36, :], gi[:, 0:T], fc[:, :], ALU.subtract).then_inc(rows_ready, 1)
                nc.vector.drain()
                nc.vector.tensor_tensor(fc[:, :], fc[:, :], mm[:, 1:1 + T], ALU.subtract)
                nc.vector.drain()
                nc.vector.tensor_tensor(fc[:, :].rearrange("p (i t) -> p i t", t=CH), fc[:, :].rearrange("p (i t) -> p i t", t=CH),
                                        mm[:, 0:T].rearrange("p (i t) -> p i t", t=CH)[:, :, 0:1].broadcast_to([4, NCH, CH]),
                                        ALU.add).then_inc(em_ready, 1)
                dve.wait_ge(conv_in, 16 * 13)
                dve.wait_ge(st_copied, 1)
                dve.wait_ge(ssq_done, 3 * len(Q_TILES))
                for hp in range(HP):
                    nc.vector.tensor_scalar(uact[:, hp, 0:T], um[:, hp, 0:T], wc[:, hp, 0:1], bc[:, hp:hp + 1], ALU.mult, ALU.add)
                    nc.vector.tensor_scalar(uact[:, hp, T:TT], stT[:, hp, :, 0], wc[:, hp, 0:1], bc[:, hp:hp + 1], ALU.mult, ALU.add)
                    nc.vector.drain()
                    for j in range(1, 4):
                        nc.vector.scalar_tensor_tensor(out=uact[:, hp, 0:T], in0=um[:, hp, j:j + T], scalar=wc[:, hp, j:j + 1],
                                                       in1=uact[:, hp, 0:T], op0=ALU.mult, op1=ALU.add)
                        old = stT[:, hp, :, j] if j < 3 else um[:, hp, 3 + T:3 + TT]
                        last = nc.vector.scalar_tensor_tensor(out=uact[:, hp, T:TT], in0=old, scalar=wc[:, hp, j:j + 1],
                                                              in1=uact[:, hp, T:TT], op0=ALU.mult, op1=ALU.add)
                        if j < 3:
                            nc.vector.drain()
                    last.then_inc(conv_done, 1)
                for hp in range(HP):
                    dve.wait_ge(sig_done, hp + 1)
                    nc.vector.tensor_tensor(uact[:, hp, :], uact[:, hp, :], sqt[:, hp, :], ALU.mult).then_inc(u_ready, 1)
                for i in range(9):
                    n = P if i < 8 else NS
                    dve.wait_ge(nA_done, i + 1)
                    nc.vector.tensor_copy(nat[0:n, i, 0:512], pn[0][0:n, :]).then_inc(nA_copied, 1)
                for i in range(NCH):
                    dve.wait_ge(nA_done, 9 + i + 1)
                    nc.vector.tensor_copy(vnat[:, i, :], pn[0][:, :]).then_inc(nA_copied, 1)
                dve.wait_ge(cb_done, 1)
                nc.vector.tensor_tensor(cbias[:, :], pq[2][0:64, 0:2], b1[:, :], ALU.add).then_inc(cb_ready, 1)
                nc.vector.drain()
                for slot in range(2):
                    dve.wait_ge(hi_copied, slot + 1)
                    nc.vector.tensor_tensor(hid[:, slot, :, 0:NB], pl[slot][0:64, 0:128].rearrange("p (h n) -> p h n", h=2)[:, :, 0:NB],
                                            hi[:, slot, :, 1:NB + 1], ALU.add).then_inc(hid_ready, 1)
                nc.vector.drain()
                for slot in range(2):
                    dve.wait_ge(act_sig, slot + 1)
                    nc.vector.scalar_tensor_tensor(out=hid[:, slot, :, 0:NB], in0=hid[:, slot, :, 0:NB], scalar=cbias[:, slot:slot + 1],
                                                   in1=sg[:, slot, :, 0:NB], op0=ALU.add, op1=ALU.mult).then_inc(act_ready, 1)
                dve.wait_ge(krt_ready, 1)
                nc.vector.reciprocal(krt[:, :, 0:NB], krt[:, :, 0:NB])
                nc.vector.drain()
                nc.vector.scalar_tensor_tensor(out=kcmp[:, :, 0:NB], in0=kcmp[:, :, 0:NB], scalar=g4[0:64, 1:2], in1=krt[:, :, 0:NB],
                                               op0=ALU.mult, op1=ALU.mult).then_inc(kn_ready, 1)


BIG = 1e30
FULL, WIN, CMP = 1, 2, 0


def steps_of_head():
    for i in range(TQ):
        yield i, CMP, 0, 1
        yield i, FULL, 0, i + 1
        yield i, WIN, max(0, i - 4), min(i + 1, 5)


STEPS = list(steps_of_head())
NSTEP = len(STEPS)
GROUPS = [-(-s[3] // 4) for s in STEPS]
GAT = [sum(GROUPS[:n]) for n in range(NSTEP + 1)]
NGROUP = GAT[NSTEP]


def attend_prompt(nc, io, keep):
    ident, nat, gnat, kcmp, vcmp, onat = (keep[k] for k in ("ident", "rows_nat", "gates_nat", "kcmpT", "vcmp", "onat"))
    with ExitStack() as ctx:
        sb = lambda n, s, d=F32: ctx.enter_context(nc.sbuf_tensor(n, s, d))
        sem = semaphores(nc, ctx, "attend")
        qS, qraw = sb("qS", [P, 2, T], F32R), sb("qraw", [P, T])
        kHL, kLH = sb("kHL", [P, 4, T], F32R), sb("kLH", [P, 4, T], F32R)
        cHL, cLH, craw = sb("cHL", [P, 2, P], F32R), sb("cLH", [P, 2, P], F32R), sb("craw", [P, 2, P])
        diag, edge = sb("diag", [P, P]), sb("edge", [P, P])
        diag_r, edge_r, ident_r, cmask_r = (sb("diag_r", [P, P], F32R), sb("edge_r", [P, P], F32R), sb("ident_r", [P, P], F32R),
                                            sb("cmask_r", [P, TQ, P], F32R))
        pm = sb("pm", [P, 2, T])
        ptT = sb("ptT", [P, 2, 4 * P])
        cmask = pm[:, 1, :].rearrange("p (i c) -> p i c", i=TQ)
        kraw = [pm[:, 0, :], ptT[:, :, :].rearrange("p a b -> p (a b)")]
        mx, nm, den, rs = sb("mx", [P, 2]), sb("nm", [P, 2]), sb("den", [P, 2]), sb("rs", [P, 2])
        S = [ctx.enter_context(nc.psum_tensor(f"pS{i}", [P, 1024], F32)) for i in range(2)]
        PT = [ctx.enter_context(nc.psum_tensor(f"pT{i}", [P, 512], F32)) for i in range(2)]
        O = [ctx.enter_context(nc.psum_tensor(f"pO{i}", [P, 512], F32)) for i in range(2)]
        q_in, q_high, q_split = sem("q_in"), sem("q_high"), sem("q_split")
        k_in, k_high, k_split = [sem(f"k_in{i}") for i in range(2)], sem("k_high"), sem("k_split")
        c_in, c_high, c_split, masks_r = sem("c_in"), sem("c_high"), sem("c_split"), sem("masks_r")
        masks, s_done, nm_ready, p_ready, pt_done, pt_copied, pv_done, o_used = (
            sem("masks"), sem("s_done"), sem("nm_ready"), sem("p_ready"), sem("pt_done"), sem("pt_copied"), sem("pv_done"),
            sem("o_used"))

        with nc.Block() as block:

            @block.gpsimd
            def _(pool):
                nc.gpsimd.memset(diag[:, :], 0.0)
                nc.gpsimd.memset(edge[:, :], 0.0)
                nc.gpsimd.memset(cmask[:, :, :], 0.0).then_inc(masks, 1)
                pool.wait_ge(masks, 1)
                nc.gpsimd.affine_select(out=diag[:, :], in_=diag[:, :], compare_op=ALU.is_ge, fill=-BIG,
                                        base=0, pattern=[[-1, P]], channel_multiplier=1)
                nc.gpsimd.affine_select(out=edge[:, :], in_=edge[:, :], compare_op=ALU.is_gt, fill=-BIG,
                                        base=0, pattern=[[1, P]], channel_multiplier=-1)
                nc.gpsimd.affine_select(out=cmask[:, :, :], in_=cmask[:, :, :], compare_op=ALU.is_ge, fill=-BIG,
                                        base=-31, pattern=[[P, TQ], [-16, P]], channel_multiplier=1)
                nc.gpsimd.drain()
                nc.gpsimd.memset(cmask[:, :, NB:P], -BIG).then_inc(masks, 1)

            @block.sync
            def _(sp):
                for n in range(4):
                    if n >= 2:
                        sp.wait_ge(k_split, n - 1)
                    for at in (0, 64):
                        sp.dma_start(kraw[n % 2][at:at + 64, :], io["qkT"][4 * P + n * 64:4 * P + n * 64 + 64, 0:T]).then_inc(k_in[n % 2], 16)
                    if n == 1:
                        for at in (0, 64):
                            sp.dma_start(qraw[at:at + 64, :], io["qkT"][0:64, 0:T]).then_inc(q_in, 16)
                with sp.Fori(1, 8) as h:
                    sp.wait_ge(q_split, h)
                    for at in (0, 64):
                        sp.dma_start(qraw[at:at + 64, :], io["qkT"][ds(h * 64, 64), 0:T]).then_inc(q_in, 16)

            @block.tensor
            def _(pe):
                pe.wait_ge(masks_r, 1)
                pe.wait_ge(k_split, 4)
                pe.wait_ge(c_split, 1)
                with pe.Fori(0, 4) as it:
                    for slot in range(2):
                        kv = it // 2
                        s0 = NSTEP * (it * 2 + slot)
                        pe.wait_ge(q_split, it * 2 + slot + 1)

                        def score(n):
                            i, branch, k0, nk = STEPS[n]
                            q = qS[:, slot, i * P:(i + 1) * P]
                            bank = S[n % 2]
                            if n >= 2:
                                pe.wait_ge(p_ready, s0 + n - 1)
                            else:
                                pe.wait_ge(p_ready, s0)
                            if branch == CMP:
                                nc.tensor.matmul(bank[:, 0:P], ident_r[:, :], cmask_r[:, i, :], start=True, stop=False)
                                nc.tensor.matmul(bank[:, 0:P], q, cHL[:, kv, :], start=False, stop=False)
                                nc.tensor.matmul(bank[:, 0:P], q, cLH[:, kv, :], start=False, stop=True).then_inc(s_done, 1)
                                return
                            keys = kv if branch == FULL else kv + 2
                            for b in range(0, nk, 4):
                                m = min(4, nk - b)
                                cut = [(c, mask) for c, mask in ((nk - 1, diag_r), (0 if branch == WIN and i >= 4 else -1, edge_r))
                                       if b <= c < b + m]
                                out, at = bank[:, b * P:(b + m) * P], slice((k0 + b) * P, (k0 + b + m) * P)
                                nc.tensor.matmul(out, q, kHL[:, keys, at], start=True, stop=False)
                                last = nc.tensor.matmul(out, q, kLH[:, keys, at], start=False, stop=not cut)
                                for u, (c, mask) in enumerate(cut):
                                    last = nc.tensor.matmul(bank[:, c * P:(c + 1) * P], ident_r[:, :], mask[:, :],
                                                            start=False, stop=u == len(cut) - 1)
                            last.then_inc(s_done, 1)

                        def transpose_group(n, g):
                            nk = STEPS[n][3]
                            at = GAT[n] + g
                            u = (at + NGROUP * slot) % 2
                            pe.wait_ge(pt_copied, NGROUP * (it * 2 + slot) + at - 1) if at or slot else pe.wait_ge(pt_copied, NGROUP * it * 2)
                            for c in range(4 * g, min(4 * g + 4, nk)):
                                last = nc.tensor.transpose(PT[u][:, (c % 4) * P:(c % 4 + 1) * P], pm[:, n % 2, c * P:(c + 1) * P], ident[:, :])
                            last.then_inc(pt_done, 1)

                        def weigh_group(n, g):
                            i, branch, k0, nk = STEPS[n]
                            at = GAT[n] + g
                            u = (at + NGROUP * slot) % 2
                            pe.wait_ge(pt_copied, NGROUP * (it * 2 + slot) + at + 1)
                            for c in range(4 * g, min(4 * g + 4, nk)):
                                v = (vcmp[:, kv, :] if branch == CMP else
                                     nat[:, k0 + c, ds((384 if branch == FULL else 640) + kv * 64, 64)])
                                last = nc.tensor.matmul(O[n % 2][:, 0:64], ptT[:, u, (c % 4) * P:(c % 4 + 1) * P], v,
                                                        start=(c == 0), stop=(c == nk - 1))
                            last.then_inc(pv_done, 1)

                        score(0)
                        score(1)
                        for n in range(NSTEP):
                            pe.wait_ge(p_ready, s0 + n + 1)
                            ahead = min(2, GROUPS[n])
                            for g in range(ahead):
                                transpose_group(n, g)
                            if n + 2 < NSTEP:
                                score(n + 2)
                            pe.wait_ge(o_used, s0 + n - 1) if n >= 2 else pe.wait_ge(o_used, s0)
                            for g in range(GROUPS[n]):
                                weigh_group(n, g)
                                if g + ahead < GROUPS[n]:
                                    transpose_group(n, g + ahead)

            @block.scalar
            def _(act):
                for n in range(4):
                    act.wait_ge(k_in[n % 2], 32 * (n // 2 + 1))
                    nc.scalar.activation(kHL[:, n, :], kraw[n % 2], ACT.Copy)
                    nc.scalar.activation(kLH[:, n, :], kraw[n % 2], ACT.Copy).then_inc(k_high, 1)
                act.wait_ge(c_in, 1)
                nc.scalar.activation(cHL[:, :, :], craw[:, :, :], ACT.Copy)
                nc.scalar.activation(cLH[:, :, :], craw[:, :, :], ACT.Copy).then_inc(c_high, 1)
                act.wait_ge(masks, 2)
                for mask_r, mask in ((diag_r, diag[:, :]), (edge_r, edge[:, :]), (ident_r, ident[:, :])):
                    nc.scalar.activation(mask_r[:, :], mask, ACT.Copy)
                nc.scalar.activation(cmask_r[:, :, :], cmask, ACT.Copy).then_inc(masks_r, 1)
                act.wait_ge(masks_r, 1)

                def high_query(h, slot):
                    act.wait_ge(q_in, 32 * (h + 1))
                    nc.scalar.activation(qS[:, slot, :], qraw[:, :], ACT.Copy).then_inc(q_high, 1)

                with act.Fori(0, 4) as it:
                    for slot in range(2):
                        s0 = NSTEP * (it * 2 + slot)
                        g0 = NGROUP * (it * 2 + slot)

                        def exponentials(n):
                            w = STEPS[n][3] * P
                            act.wait_ge(nm_ready, s0 + n + 1)
                            if n >= 2:
                                act.wait_ge(pt_done, g0 + GAT[n - 1])
                            else:
                                act.wait_ge(pt_done, g0)
                            nc.scalar.activation(pm[:, n % 2, 0:w], S[n % 2][:, 0:w], ACT.Exp, bias=nm[:, n % 2:n % 2 + 1],
                                                 accum_out=den[:, n % 2:n % 2 + 1]).then_inc(p_ready, 1)

                        if slot == 0:
                            act.wait_ge(s_done, s0)
                            high_query(it * 2, 0)
                        exponentials(0)
                        for n in range(NSTEP):
                            if slot == 0 and n == NSTEP // 2:
                                high_query(it * 2 + 1, 1)
                            nk = STEPS[n][3]
                            if n + 1 < NSTEP:
                                exponentials(n + 1)
                            for g in range(GROUPS[n]):
                                at = GAT[n] + g
                                u = (at + NGROUP * slot) % 2
                                act.wait_ge(pt_done, g0 + at + 1)
                                if slot or at >= 2:
                                    act.wait_ge(pv_done, g0 + at - 1)
                                else:
                                    act.wait_ge(pv_done, g0)
                                cols = min(4, nk - 4 * g) * P
                                nc.scalar.activation(ptT[:, u, 0:cols], PT[u][:, 0:cols], ACT.Copy).then_inc(pt_copied, 1)

            @block.vector
            def _(dve):
                for at in (0, 64):
                    last = nc.vector.tensor_copy(craw[at:at + 64, :, :], kcmp[:, :, :])
                last.then_inc(c_in, 1)
                upper, lower = slice(0, 64), slice(64, P)
                for n in range(4):
                    dve.wait_ge(k_high, n + 1)
                    nc.vector.tensor_tensor(kHL[lower, n, :], kraw[n % 2][lower, :], kHL[lower, n, :].bitcast(F32), ALU.subtract)
                    nc.vector.tensor_tensor(kLH[upper, n, :], kraw[n % 2][upper, :], kLH[upper, n, :].bitcast(F32),
                                            ALU.subtract).then_inc(k_split, 1)
                dve.wait_ge(c_high, 1)
                nc.vector.tensor_tensor(cHL[lower, :, :], craw[lower, :, :], cHL[lower, :, :].bitcast(F32), ALU.subtract)
                nc.vector.tensor_tensor(cLH[upper, :, :], craw[upper, :, :], cLH[upper, :, :].bitcast(F32), ALU.subtract).then_inc(c_split, 1)

                def low_query(h, slot):
                    dve.wait_ge(q_high, h + 1)
                    nc.vector.tensor_tensor(qS[lower, slot, :], qraw[lower, :], qS[lower, slot, :].bitcast(F32),
                                            ALU.subtract).then_inc(q_split, 1)

                with dve.Fori(0, 4) as it:
                    for slot in range(2):
                        h = it * 2 + slot
                        s0 = NSTEP * h
                        g0 = NGROUP * h

                        def row_max(n):
                            i, branch, k0, nk = STEPS[n]
                            w = nk * P
                            dve.wait_ge(s_done, s0 + n + 1)
                            nc.vector.reduce_max(mx[:, n % 2:n % 2 + 1], S[n % 2][:, 0:w], AX.X)
                            nc.vector.drain()
                            nc.vector.tensor_scalar(nm[:, n % 2:n % 2 + 1], mx[:, n % 2:n % 2 + 1], -1e20, -1.0,
                                                    ALU.max, ALU.mult).then_inc(nm_ready, 1)

                        if slot == 0:
                            low_query(h, 0)
                        row_max(0)
                        row_max(1)
                        for n in range(NSTEP):
                            if slot == 0 and n == NSTEP // 2:
                                low_query(h + 1, 1)
                            i, branch, k0, nk = STEPS[n]
                            u = n % 2
                            dve.wait_ge(p_ready, s0 + n + 1)
                            nc.vector.tensor_scalar(rs[:, u:u + 1], den[:, u:u + 1], 1e-30, None, ALU.max)
                            nc.vector.drain()
                            nc.vector.reciprocal(rs[:, u:u + 1], rs[:, u:u + 1])
                            nc.vector.drain()
                            nc.vector.tensor_tensor(rs[:, u:u + 1], rs[:, u:u + 1], gnat[:, i, ds(h * 3 + branch, 1)], ALU.mult)
                            if n + 2 < NSTEP:
                                row_max(n + 2)
                            nc.vector.drain()
                            dve.wait_ge(pv_done, g0 + GAT[n + 1])
                            out = onat[:, i, ds(256 + h * 64, 64)]
                            if branch == CMP:
                                nc.vector.tensor_scalar(out, O[u][:, 0:64], rs[:, u:u + 1], None, ALU.mult).then_inc(o_used, 1)
                            else:
                                nc.vector.scalar_tensor_tensor(out=out, in0=O[u][:, 0:64], scalar=rs[:, u:u + 1], in1=out,
                                                               op0=ALU.mult, op1=ALU.add).then_inc(o_used, 1)


SIDES = 11
NL = 7
KEND, QIN, RAW = 7, 8, 8


def chunk_loop(eng, chunk):
    with eng.Fori(0, NCH // 2 - 1) as it:
        for slot in range(2):
            chunk(it * 2 + slot, slot)
    chunk(NCH - 2, 0)
    chunk(NCH - 1, 1, more=False)


def recur_prompt(nc, io, keep):
    ident, vnat, mqk, mknat, R, RN, decay, onat, hs, ones = (
        keep[k] for k in ("ident", "v_nat", "mqk", "mk_nat", "rows", "rows_cols", "decay", "onat", "hs", "ones"))
    zT = io["zT"]
    with ExitStack() as ctx:
        sb = lambda n, s, d=F32: ctx.enter_context(nc.sbuf_tensor(n, s, d))
        sem = semaphores(nc, ctx, "recur")
        zg = sb("zg", [P, 4, T])
        spare = keep["rows_nat"][:, :, :].rearrange("p i c -> p (i c)")
        odd = [spare[:, n * HP * 9 * P:(n + 1) * HP * 9 * P].rearrange("p (k l t) -> p k l t", k=HP, l=9) for n in range(3)]
        dd, qd, kd = [sb("dd", [P, HP, 9, P]), odd[0]], [sb("qd", [P, HP, 9, P]), odd[1]], [sb("kd", [P, HP, 9, P]), odd[2]]
        lvl = sb("lvl", [P, 8, P], U32)
        pT = sb("pTg", [P, 4, P])
        kn = sb("kn", [P, HP, P])
        G = sb("Gst", [P, HP, 64])
        sel4 = sb("sel4", [4, 4, P])
        sel127 = sb("sel127", [P, P])
        maskT = sb("maskT", [P, 4, P])
        kst, qst = [sb(f"kst{i}", [P, HP, P]) for i in range(2)], [sb(f"qst{i}", [P, HP, P]) for i in range(2)]
        wT = sb("wTm", [P, 4, P])
        pTm = sb("pTm", [P, 4, P])
        vaug = sb("vaug", [P, NCH, 4, 65])
        kw = sb("kw", [P, 4, 64])
        C = sb("Cst", [P, HP, 65])
        wcb = sb("wcb", [P, NCH, 16])
        bs = sb("bs", [P, 4, 65])
        carry = sb("carry", [1, 1])
        ps = [ctx.enter_context(nc.psum_tensor(f"pr{i}", [P, 512], F32)) for i in range(8)]
        sc = ps[0:2]
        og, kt, dl, pw, pb, pd = ps[2], ps[3], ps[3], ps[4], ps[6], ps[7]
        pa = ps[5]

        g_in, setup, setup2, lv_ready, diffs, factors, keyed, queried, raws = (
            sem("g_in2"), sem("setup"), sem("setup2"), sem("lv_ready"), sem("diffs"), sem("factors"), sem("keyed"),
            sem("queried"), sem("raws"))
        sc_done, sc_used, og_done, og_copied, kt_done, kt_copied, dl_done, g_updated = (
            sem("sc_done"), sem("sc_used"), sem("og_done"), sem("og_copied"), sem("kt_done"), sem("kt_copied"),
            sem("dl_done"), sem("g_updated"))
        side_done = sem("side_done")
        pw_done, w_ready, st_done, p_ready, num_done, h_ready, kw_ready, pd_done, c_updated, wc_done, wc_ready, states_out = (
            sem("pw_done"), sem("w_ready"), sem("st_done2"), sem("p_ready2"), sem("num_done"), sem("h_ready"),
            sem("kw_ready"), sem("pd_done"), sem("c_updated"), sem("wc_done"), sem("wc_ready"), sem("states_out"))

        with nc.Block() as block:

            @block.sync
            def _(sp):
                sp.dma_start(zg[:, :, :], zT[GQ:GQ + 4 * P, 0:T].rearrange("(j p) t -> p j t", p=P)).then_inc(g_in, 16)
                sp.wait_ge(g_updated, NCH)
                sp.wait_ge(c_updated, NCH)
                for h in range(4):
                    at = slice((h % 2) * 64, (h % 2) * 64 + 64)
                    sp.dma_start(io["out6"][0, 0, h, :, :], G[at, h // 2, :]).then_inc(states_out, 16)
                    sp.dma_start(io["out8"][0, 0, h, :, :], C[at, h // 2, 0:64]).then_inc(states_out, 16)
                    sp.dma_start(io["out10"][0, 0, h, :].rearrange("(d a) -> d a", a=1), C[at, h // 2, 64:65]).then_inc(states_out, 16)
                sp.wait_ge(states_out, 16 * 12)

            @block.gpsimd
            def _(pool):
                nc.gpsimd.memset(lvl[:, :, :].bitcast(I32), 1)
                nc.gpsimd.memset(pT[:, :, :], 0.0)
                nc.gpsimd.memset(G[:, :, :], 0.0)
                nc.gpsimd.memset(C[:, :, :], 0.0)
                nc.gpsimd.memset(vaug[:, :, :, :], 1.0)
                nc.gpsimd.memset(maskT[:, :, :], 0.0)
                nc.gpsimd.memset(sel127[:, :], 0.0)
                nc.gpsimd.memset(sel4[:, :, :], 0.0).then_inc(setup, 1)
                pool.wait_ge(setup, 1)
                nc.gpsimd.affine_select(out=maskT[:, :, :], in_=maskT[:, :, :], compare_op=ALU.is_ge, fill=-BIG,
                                        base=0, pattern=[[0, 4], [1, P]], channel_multiplier=-1)
                nc.gpsimd.affine_select(out=sel127[:, :], in_=sel127[:, :], compare_op=ALU.not_equal, fill=1.0,
                                        base=-(P - 1), pattern=[[0, P]], channel_multiplier=1)
                nc.gpsimd.affine_select(out=lvl[:, 7, :].bitcast(I32), in_=lvl[:, 7, :].bitcast(I32), compare_op=ALU.is_equal, fill=0,
                                        base=0, pattern=[[1, P]], channel_multiplier=-1)
                for l in range(NL):
                    half = 1 << l
                    v = lvl[:, l, :].bitcast(I32).rearrange("p (b h c) -> p b h c", h=2, c=half)
                    nc.gpsimd.memset(v[:, :, 0, :], 0)
                nc.gpsimd.drain()
                for l in range(NL):
                    half = 1 << l
                    v = lvl[:, l, :].bitcast(I32).rearrange("p (b h c) -> p b h c", h=2, c=half)[:, :, 1, :]
                    nb = P // (2 * half)
                    nc.gpsimd.affine_select(out=v, in_=v, compare_op=ALU.is_gt, fill=0,
                                            base=half, pattern=[[2 * half, nb], [0, half]], channel_multiplier=-1)
                nc.gpsimd.drain()
                for l in range(NL):
                    half = 1 << l
                    v = lvl[:, l, :].bitcast(I32).rearrange("p (b h c) -> p b h c", h=2, c=half)[:, :, 1, :]
                    nb = P // (2 * half)
                    nc.gpsimd.affine_select(out=v, in_=v, compare_op=ALU.is_ge, fill=0,
                                            base=0, pattern=[[-2 * half, nb], [0, half]], channel_multiplier=1)
                nc.gpsimd.affine_select(out=sel4[:, :, :], in_=sel4[:, :, :], compare_op=ALU.not_equal, fill=1.0,
                                        base=0, pattern=[[-1, 4], [0, P]], channel_multiplier=1)
                nc.gpsimd.tensor_copy(vaug[:, :, :, 0:64], vnat[:, :, 256:512].rearrange("p i (h e) -> p i h e", h=4)).then_inc(setup, 1)
                pool.wait_ge(g_in, 16)

                def keys(c, slot, first=False):
                    pool.wait_ge(factors, c + 1)
                    if not first:
                        pool.wait_ge(og_done, c - 1)
                        pool.wait_ge(kt_done, c - 1)
                    nc.gpsimd.tensor_tensor(kd[slot][:, :, 0:8, :],
                                            zg[:, 2:4, ds(c * P, P)].unsqueeze(2).broadcast_to([P, HP, 8, P]),
                                            dd[slot][:, :, 0:8, :], ALU.mult).then_inc(keyed, 1)

                keys(0, 0, first=True)
                keys(1, 1, first=True)
                with pool.Fori(1, NCH // 2) as it:
                    for slot in range(2):
                        keys(it * 2 + slot, slot)

            @block.scalar
            def _(act):
                act.wait_ge(setup, 2)
                act.wait_ge(wc_done, 1)
                nc.scalar.activation(wcb[:, :, :], ps[7][:, 0:P].rearrange("p (i k) -> p i k", i=NCH), ACT.Copy).then_inc(wc_ready, 1)
                act.wait_ge(lv_ready, 1)

                def factors_of(c, slot, first=False):
                    if not first:
                        act.wait_ge(og_done, c - 1)
                        act.wait_ge(num_done, c - 1)
                    for dst, src in ((qd[slot][:, :, RAW, :], zg[:, 0:2, :]), (kd[slot][:, :, RAW, :], zg[:, 2:4, :]),
                                     (qst[slot][:, :, :], mqk[:, 0:2, :]), (kst[slot][:, :, :], mqk[:, 2:4, :])):
                        last = nc.scalar.activation(dst, src[:, :, ds(c * P, P)], ACT.Copy)
                    last.then_inc(raws, 1)
                    act.wait_ge(diffs, c + 1)
                    nc.scalar.activation(dd[slot][:, :, :, :], dd[slot][:, :, :, :], ACT.Abs)
                    nc.scalar.drain()
                    nc.scalar.activation(dd[slot][:, :, :, :], dd[slot][:, :, :, :], ACT.Exp, scale=-1.0 / 16.0).then_inc(factors, 1)

                def chunk(c, slot, more=True):
                    act.wait_ge(pw_done, c + 1)
                    for h in range(4):
                        last = nc.scalar.activation(wT[:, h, :], pw[:, h * P:(h + 1) * P], ACT.Exp, bias=RN[:, c, 4 + h:5 + h])
                    last.then_inc(w_ready, 1)
                    if more:
                        factors_of(c + 1, 1 - slot)
                    act.wait_ge(kt_done, c + 1)
                    nc.scalar.activation(kn[:, :, :], kt[:, 0:2 * P].rearrange("p (k c) -> p k c", k=2), ACT.Copy).then_inc(kt_copied, 1)
                    act.wait_ge(og_done, c + 1)
                    nc.scalar.activation(onat[:, c, 0:256], og[:, 0:256], ACT.Copy).then_inc(og_copied, 1)

                factors_of(0, 0, first=True)
                chunk_loop(act, chunk)

            @block.tensor
            def _(pe):
                pe.wait_ge(setup, 2)
                nc.tensor.matmul(ps[7][:, 0:P], sel127[:, :], RN[:, :, :].rearrange("p i k -> p (i k)"), start=True, stop=True).then_inc(wc_done, 1)
                pe.wait_ge(wc_ready, 1)
                def chunk(c, slot, more=True):
                    sides = [0]

                    def by_side(product):
                        for h in (0, 2):
                            last = product(h, slice(0, 64))
                        last.then_inc(side_done, 1)
                        sides[0] += 1
                        pe.wait_ge(side_done, SIDES * c + sides[0])
                        for h in (1, 3):
                            last = product(h, slice(64, 128))
                        return last

                    pe.wait_ge(w_ready, c)
                    nc.tensor.matmul(pw[:, :], ident[:, :], maskT[:, :, :].rearrange("p h t -> p (h t)"), start=True, stop=False)
                    for h in range(4):
                        last = nc.tensor.matmul(pw[:, h * P:(h + 1) * P], sel4[:, h, :], R[0:4, ds(c * P, P)], start=False, stop=h == 3)
                    last.then_inc(pw_done, 1)
                    pe.wait_ge(raws, c + 1)
                    pe.wait_ge(h_ready, c)
                    by_side(lambda h, at: nc.tensor.matmul(pb[:, h * P:(h + 1) * P], kst[slot][at, h // 2, :], qst[slot][at, h // 2, :],
                                                           start=True, stop=True)).then_inc(st_done, 1)
                    pe.wait_ge(keyed, c + 1)
                    pe.wait_ge(queried, c + 1)
                    for l in range(NL + 1):
                        pe.wait_ge(sc_used, 8 * c + l - 1) if l >= 2 else pe.wait_ge(sc_used, 8 * c)
                        ql = RAW if l == NL else l
                        by_side(lambda h, at: nc.tensor.matmul(sc[l % 2][:, h * P:(h + 1) * P], kd[slot][at, h // 2, ql, :],
                                                               qd[slot][at, h // 2, ql, :], start=True, stop=True)).then_inc(sc_done, 1)
                    pe.wait_ge(g_updated, c)
                    for hp in range(HP):
                        last = nc.tensor.transpose(kt[:, hp * P:(hp + 1) * P], kd[slot][:, hp, KEND, :], ident[:, :])
                    last.then_inc(kt_done, 1)
                    pe.wait_ge(p_ready, c + 1)
                    for h in range(4):
                        nc.tensor.matmul(pa[:, h * 65:(h + 1) * 65], pTm[:, h, :], vaug[:, c, h, :], start=True, stop=True)
                    pe.wait_ge(c_updated, c)
                    by_side(lambda h, at: nc.tensor.matmul(pb[:, h * 65:(h + 1) * 65], qst[slot][at, h // 2, :], C[at, h // 2, :],
                                                           start=True, stop=True)).then_inc(num_done, 1)
                    pe.wait_ge(kw_ready, c + 1)
                    for hp in range(HP):
                        last = nc.tensor.matmul(pd[:, hp * 130:(hp + 1) * 130], kw[:, 2 * hp:2 * hp + 2, :].rearrange("p h d -> p (h d)"),
                                                vaug[:, c, 2 * hp:2 * hp + 2, :].rearrange("p h d -> p (h d)"), start=True, stop=True)
                    last.then_inc(pd_done, 1)
                    pe.wait_ge(sc_used, 8 * c + 8)
                    pe.wait_ge(og_copied, c)
                    for h in range(4):
                        nc.tensor.matmul(og[:, h * 64:(h + 1) * 64], pT[:, h, :], vnat[:, c, h * 64:(h + 1) * 64], start=(h == 0), stop=False)
                    by_side(lambda h, at: nc.tensor.matmul(og[:, h * 64:(h + 1) * 64], qd[slot][at, h // 2, KEND, :], G[at, h // 2, :],
                                                           start=False, stop=(h == 3))).then_inc(og_done, 1)
                    pe.wait_ge(kt_copied, c + 1)
                    for hp in range(HP):
                        last = nc.tensor.matmul(dl[:, 256 + hp * P:256 + (hp + 1) * P], kn[:, hp, :], vnat[:, c, hp * P:(hp + 1) * P],
                                                start=True, stop=True)
                    last.then_inc(dl_done, 1)

                chunk_loop(pe, chunk)

            @block.vector
            def _(dve):
                dve.wait_ge(g_in, 16)
                dve.wait_ge(setup, 2)
                dve.wait_ge(wc_ready, 1)
                nc.vector.tensor_scalar(zg[:, 0:2, :], zg[:, 0:2, :], HD ** -0.5, None, ALU.mult).then_inc(lv_ready, 1)
                nc.vector.drain()

                def differences(c, slot, first=False):
                    b = decay[:, :, ds(c * P, P)]
                    nc.vector.drain()
                    if not first:
                        dve.wait_ge(keyed, c - 1)
                    for l in range(NL):
                        half = 1 << l
                        nb = P // (2 * half)
                        blocks = b.rearrange("p k (b w) -> p k b w", w=2 * half)
                        nc.vector.tensor_tensor(dd[slot][:, :, l, :].rearrange("p k (b w) -> p k b w", w=2 * half), blocks,
                                                blocks[:, :, :, half - 1:half].broadcast_to([P, HP, nb, 2 * half]), ALU.subtract)
                    nc.vector.tensor_tensor(dd[slot][:, :, KEND, :], b, b[:, :, P - 1:P].broadcast_to([P, HP, P]), ALU.subtract)
                    nc.vector.tensor_copy(dd[slot][:, :, QIN, :], b).then_inc(diffs, 1)

                def queries(c, slot, first=False):
                    dve.wait_ge(factors, c + 1)
                    if not first:
                        dve.wait_ge(og_done, c - 1)
                    q = zg[:, 0:2, ds(c * P, P)]
                    nc.vector.tensor_tensor(qd[slot][:, :, 0:NL, :], q.unsqueeze(2).broadcast_to([P, HP, NL, P]), dd[slot][:, :, 0:NL, :],
                                            ALU.mult)
                    nc.vector.tensor_tensor(qd[slot][:, :, KEND, :], q, dd[slot][:, :, QIN, :], ALU.mult).then_inc(queried, 1)

                def merge(c, l):
                    nc.vector.drain()
                    if l == 0:
                        dve.wait_ge(og_done, c)
                    dve.wait_ge(sc_done, 8 * c + l + 1)
                    nc.vector.tensor_copy(carry[0:1, 0:1], wcb[0:1, 0, 0:1])
                    nc.vector.copy_predicated(pT[:, :, :], lvl[:, l, :].unsqueeze(1).broadcast_to([P, 4, P]),
                                              sc[l % 2][:, :].rearrange("p (h t) -> p h t", h=4)).then_inc(sc_used, 1)

                def chunk(c, slot, more=True):
                    if more:
                        differences(c + 1, 1 - slot)
                    for l in range(4):
                        merge(c, l)
                    dve.wait_ge(w_ready, c + 1)
                    dve.wait_ge(st_done, c + 1)
                    dve.wait_ge(pd_done, c)
                    nc.vector.tensor_tensor(pTm[:, :, :], pb[:, :].rearrange("p (h t) -> p h t", h=4), wT[:, :, :], ALU.mult).then_inc(p_ready, 1)
                    nc.vector.tensor_tensor(kw[:, :, :], mknat[:, c, :].rearrange("p (h d) -> p h d", h=4),
                                            wT[:, :, P - 1:P].broadcast_to([P, 4, 64]), ALU.mult).then_inc(kw_ready, 1)
                    for l in range(4, NL + 1):
                        merge(c, l)
                    if more:
                        queries(c + 1, 1 - slot)
                    dve.wait_ge(num_done, c + 1)
                    nc.vector.tensor_tensor(bs[:, :, :], pb[:, 0:260].rearrange("p (h e) -> p h e", h=4),
                                            RN[:, c, 8:12].unsqueeze(2).broadcast_to([P, 4, 65]), ALU.mult)
                    nc.vector.drain()
                    nc.vector.tensor_tensor(hs[:, c, :, :], pa[:, 0:260].rearrange("p (h e) -> p h e", h=4), bs[:, :, :], ALU.add).then_inc(h_ready, 1)
                    dve.wait_ge(pd_done, c + 1)
                    for h in range(4):
                        at = slice((h % 2) * 64, (h % 2) * 64 + 64)
                        off = (h // 2) * 130 + (h % 2) * 65
                        last = nc.vector.scalar_tensor_tensor(out=C[at, h // 2, :], in0=C[at, h // 2, :], scalar=wcb[at, c, 8 + h:9 + h],
                                                              in1=pd[at, off:off + 65], op0=ALU.mult, op1=ALU.add)
                    last.then_inc(c_updated, 1)
                    dve.wait_ge(dl_done, c + 1)
                    for h in range(4):
                        at = slice((h % 2) * 64, (h % 2) * 64 + 64)
                        off = 256 + (h // 2) * P + (h % 2) * 64
                        last = nc.vector.scalar_tensor_tensor(out=G[at, h // 2, :], in0=G[at, h // 2, :], scalar=dd[slot][at, h // 2, QIN, P - 1:P],
                                                              in1=dl[at, off:off + 64], op0=ALU.mult, op1=ALU.add)
                    last.then_inc(g_updated, 1)

                differences(0, 0, first=True)
                queries(0, 0, first=True)
                chunk_loop(dve, chunk)


NR = 8 * NS
L = 2048
NG16 = L // 16
NBD = NG16 - 1
WIN_ROWS = 512


def decode_recurrences(nc, io, keep):
    ident, eps, ones, mixS, mqd, dcd = (keep[k] for k in ("ident", "eps", "ones", "mixS", "mqk_dec", "decay_dec"))
    zT, zS = io["zT"], io["zS"]
    with ExitStack() as ctx:
        sb = lambda n, s, d=F32: ctx.enter_context(nc.sbuf_tensor(n, s, d))
        sem = semaphores(nc, ctx, "step")
        qk = sb("qkd", [P, 4, NS])
        vb, kv, Gs = sb("vb", [P, HP, NS, 65]), sb("kvd", [P, HP, NS, 65]), sb("Gs", [P, HP, NS, 64])
        vm, Cs = sb("vm", [P, HP, NS, 65]), sb("Cs", [P, HP, NS, 65])
        m0, gi, gf = sb("m0", [P, HP, NS]), sb("gid", [P, HP, NS]), sb("gfd", [P, HP, NS])
        gb = sb("gbd", [P, 2, HP])
        lf, mt, wc, wl, em = (sb(n, [P, HP, NS]) for n in ("lf", "mt", "wcd", "wld", "emd"))
        qbd, qbm = sb("qbd", [P, HP, NS, 2]), sb("qbm", [P, HP, NS, 2])
        qn, blk = sb("qn", [P, HP, NS]), sb("blkd", [P, P])
        o, sqo, em64, dn, nd = (sb(n, [64, 2, HP, NS]) for n in ("od", "sqo", "em64", "dnd", "ndd"))
        ps = [ctx.enter_context(nc.psum_tensor(f"pdr{i}", [P, 512], F32)) for i in range(6)]
        loads, zeroed, stored = sem("d_loads"), sem("d_zeroed"), sem("d_stored")
        G_FACT, G_STATE, G_OUT, G_SQ, G_SUM, G_RT, G_NORM = (
            sem(f"gla_{n}") for n in ("factor", "state", "out", "squares", "sum", "root", "norm"))
        F_ABS, M_T, M_EXP, C_STATE, M_DEN, M_DIV, M_SQ, M_SUM, M_RT = (
            sem(f"mlstm_{n}") for n in ("abs", "m", "exp", "state", "denominator", "div", "squares", "sum", "root"))

        with nc.Block() as block:

            @block.gpsimd
            def _(pool):
                nc.gpsimd.memset(vm[:, :, :, 64:65], 1.0)
                nc.gpsimd.memset(qbd[:, :, :, :], 0.0)
                nc.gpsimd.memset(qbm[:, :, :, :], 0.0)
                nc.gpsimd.memset(blk[:, :], 0.0)
                nc.gpsimd.drain()
                nc.gpsimd.memset(blk[0:64, 0:64], 1.0)
                nc.gpsimd.drain()
                nc.gpsimd.memset(blk[64:128, 64:128], 1.0).then_inc(zeroed, 1)

            @block.sync
            def _(sp):
                def load(dst, src):
                    sp.dma_start(dst, src).then_inc(loads, 16)

                load(qk[:, :, :], zT[GQ:GQ + 4 * P, T:TT].rearrange("(j p) s -> p j s", p=P))
                for h in range(4):
                    at, hp = slice((h % 2) * 64, (h % 2) * 64 + 64), h // 2
                    load(vb[at, hp, :, 0:64], zS[:, GV + h * 64:GV + h * 64 + 64].unsqueeze(0).broadcast_to([64, NS, 64]))
                    load(Gs[at, hp, :, :], io["state_gla"][0, :, h, :, :].rearrange("s d e -> d s e"))
                    load(vm[at, hp, :, 0:64], zS[:, MV + h * 64:MV + h * 64 + 64].unsqueeze(0).broadcast_to([64, NS, 64]))
                    load(Cs[at, hp, :, 0:64], io["state_mlstm_c"][0, :, h, :, :].rearrange("s d e -> d s e"))
                    load(Cs[at, hp, :, 64:65], io["state_mlstm_n"][0, :, h, :].rearrange("s (d a) -> d s a", a=1))
                    load(m0[at, hp, :], io["state_mlstm_m"][0, :, h:h + 1].rearrange("s a -> a s").broadcast_to([64, NS]))
                    load(gi[at, hp, :], zT[MI + h:MI + h + 1, T:TT].broadcast_to([64, NS]))
                    load(gf[at, hp, :], zT[MF + h:MF + h + 1, T:TT].broadcast_to([64, NS]))
                for h2 in range(2):
                    load(gb[h2 * 64:h2 * 64 + 64, :, :],
                         io["ml_gate_b"][0:1, :, :].rearrange("l k (a b) -> l k a b", b=2)[:, :, :, h2].broadcast_to([64, 2, HP]))
                sp.wait_ge(G_STATE, 1)
                sp.wait_ge(C_STATE, 1)
                for h in range(4):
                    at, hp = slice((h % 2) * 64, (h % 2) * 64 + 64), h // 2
                    sp.dma_start(io["out7"][0, :, h, :, :].rearrange("s d e -> d s e"), Gs[at, hp, :, :]).then_inc(stored, 16)
                    sp.dma_start(io["out9"][0, :, h, :, :].rearrange("s d e -> d s e"), Cs[at, hp, :, 0:64]).then_inc(stored, 16)
                    sp.dma_start(io["out11"][0, :, h, :].rearrange("s (d a) -> d s a", a=1), Cs[at, hp, :, 64:65]).then_inc(stored, 16)
                    sp.dma_start(io["out13"][0, :, h:h + 1].rearrange("s a -> a s"), mt[(h % 2) * 64:(h % 2) * 64 + 1, hp, :]).then_inc(stored, 16)
                sp.wait_ge(stored, 16 * 16)

            @block.scalar
            def _(act):
                act.wait_ge(loads, 16 * (1 + 4 * 8 + 2))
                nc.scalar.activation(dcd[:, :, :], dcd[:, :, :], ACT.Exp, scale=1.0 / 16.0).then_inc(G_FACT, 1)
                for hp in range(HP):
                    last = nc.scalar.activation(lf[:, hp, :], gf[:, hp, :], ACT.Abs, bias=gb[:, 1, hp:hp + 1])
                nc.scalar.drain()
                nc.scalar.activation(lf[:, :, :], lf[:, :, :], ACT.Exp, scale=-1.0)
                nc.scalar.drain()
                nc.scalar.activation(lf[:, :, :], lf[:, :, :], ACT.Ln, bias=1.0).then_inc(F_ABS, 1)
                act.wait_ge(M_T, 1)
                nc.scalar.activation(wc[:, :, :], wc[:, :, :], ACT.Exp)
                nc.scalar.activation(wl[:, :, :], wl[:, :, :], ACT.Exp)
                nc.scalar.activation(em[:, :, :], mt[:, :, :], ACT.Exp, scale=-1.0)
                nc.scalar.drain()
                for h2 in range(2):
                    last = nc.scalar.activation(em64[:, h2, :, :], em[h2 * 64:h2 * 64 + 64, :, :], ACT.Copy)
                last.then_inc(M_EXP, 1)
                act.wait_ge(G_OUT, 1)
                nc.scalar.activation(o[:, :, :, :], ps[0][0:64, 0:32].rearrange("p (a k s) -> p a k s", a=2, k=2), ACT.Copy)
                nc.scalar.activation(sqo[:, :, :, :], ps[0][0:64, 0:32].rearrange("p (a k s) -> p a k s", a=2, k=2), ACT.Square).then_inc(G_SQ, 1)
                act.wait_ge(G_SUM, 1)
                nc.scalar.activation(sqo[:, :, :, :], ps[1][0:64, 0:32].rearrange("p (a k s) -> p a k s", a=2, k=2), ACT.Sqrt,
                                     scale=1.0 / HD, bias=eps[0:64, :]).then_inc(G_RT, 1)
                act.wait_ge(M_DIV, 1)
                act.wait_ge(G_NORM, 1)
                nc.scalar.activation(sqo[:, :, :, :], o[:, :, :, :], ACT.Square).then_inc(M_SQ, 1)
                act.wait_ge(M_SUM, 1)
                nc.scalar.activation(sqo[:, :, :, :], ps[4][0:64, 0:32].rearrange("p (a k s) -> p a k s", a=2, k=2), ACT.Sqrt,
                                     scale=1.0 / HD, bias=eps[0:64, :]).then_inc(M_RT, 1)

            @block.vector
            def _(dve):
                dve.wait_ge(loads, 16 * (1 + 4 * 8 + 2))
                dve.wait_ge(zeroed, 1)
                dve.wait_ge(G_FACT, 1)
                bc = lambda a, n: a.unsqueeze(3).broadcast_to([P, HP, NS, n])
                for h2 in range(2):
                    at = slice(h2 * 64, h2 * 64 + 64)
                    nc.vector.tensor_scalar(qbd[at, :, :, h2], qk[at, 0:2, :], HD ** -0.5, None, ALU.mult)
                    nc.vector.tensor_copy(qbm[at, :, :, h2], mqd[at, 0:2, :])
                nc.vector.tensor_tensor(Gs[:, :, :, :], Gs[:, :, :, :], bc(dcd[:, :, :], 64), ALU.mult)
                nc.vector.tensor_tensor(kv[:, :, :, 0:64], vb[:, :, :, 0:64], bc(qk[:, 2:4, :], 64), ALU.mult)
                nc.vector.drain()
                nc.vector.tensor_tensor(Gs[:, :, :, :], Gs[:, :, :, :], kv[:, :, :, 0:64], ALU.add).then_inc(G_STATE, 1)
                nc.vector.drain()
                dve.wait_ge(F_ABS, 1)
                for hp in range(HP):
                    nc.vector.tensor_scalar(gf[:, hp, :], gf[:, hp, :], gb[:, 1, hp:hp + 1], 0.0, ALU.add, ALU.min)
                    nc.vector.tensor_scalar(gi[:, hp, :], gi[:, hp, :], gb[:, 0, hp:hp + 1], None, ALU.add)
                nc.vector.drain()
                nc.vector.tensor_tensor(lf[:, :, :], gf[:, :, :], lf[:, :, :], ALU.subtract)
                nc.vector.drain()
                nc.vector.tensor_tensor(lf[:, :, :], lf[:, :, :], m0[:, :, :], ALU.add)
                nc.vector.drain()
                nc.vector.tensor_tensor(mt[:, :, :], lf[:, :, :], gi[:, :, :], ALU.max)
                nc.vector.drain()
                nc.vector.tensor_tensor(wc[:, :, :], lf[:, :, :], mt[:, :, :], ALU.subtract)
                nc.vector.tensor_tensor(wl[:, :, :], gi[:, :, :], mt[:, :, :], ALU.subtract).then_inc(M_T, 1)
                dve.wait_ge(M_EXP, 1)
                nc.vector.tensor_tensor(wl[:, :, :], wl[:, :, :], mqd[:, 2:4, :], ALU.mult)
                nc.vector.tensor_tensor(Cs[:, :, :, :], Cs[:, :, :, :], bc(wc[:, :, :], 65), ALU.mult)
                nc.vector.drain()
                nc.vector.tensor_tensor(kv[:, :, :, :], vm[:, :, :, :], bc(wl[:, :, :], 65), ALU.mult)
                nc.vector.drain()
                nc.vector.tensor_tensor(Cs[:, :, :, :], Cs[:, :, :, :], kv[:, :, :, :], ALU.add)
                nc.vector.drain()
                nc.vector.tensor_tensor(qn[:, :, :], mqd[:, 0:2, :], Cs[:, :, :, 64], ALU.mult).then_inc(C_STATE, 1)
                dve.wait_ge(G_RT, 1)
                nc.vector.reciprocal(sqo[:, :, :, :], sqo[:, :, :, :])
                nc.vector.drain()
                for h2 in range(2):
                    last = nc.vector.tensor_tensor(mixS[h2 * 64:h2 * 64 + 64, 0:2, :], o[:, h2, :, :], sqo[:, h2, :, :], ALU.mult)
                last.then_inc(G_NORM, 1)
                dve.wait_ge(M_DEN, 1)
                den = ps[3][0:64, 0:32].rearrange("p (a k s) -> p a k s", a=2, k=2)
                nc.vector.tensor_copy(dn[:, :, :, :], den)
                nc.vector.tensor_scalar(nd[:, :, :, :], den, -1.0, None, ALU.mult)
                nc.vector.drain()
                nc.vector.tensor_tensor(nd[:, :, :, :], nd[:, :, :, :], dn[:, :, :, :], ALU.max)
                nc.vector.drain()
                nc.vector.tensor_tensor(nd[:, :, :, :], nd[:, :, :, :], em64[:, :, :, :], ALU.max)
                nc.vector.drain()
                nc.vector.reciprocal(nd[:, :, :, :], nd[:, :, :, :])
                nc.vector.drain()
                nc.vector.tensor_tensor(o[:, :, :, :], ps[2][0:64, 0:32].rearrange("p (a k s) -> p a k s", a=2, k=2), nd[:, :, :, :],
                                        ALU.mult).then_inc(M_DIV, 1)
                dve.wait_ge(M_RT, 1)
                nc.vector.reciprocal(sqo[:, :, :, :], sqo[:, :, :, :])
                nc.vector.drain()
                for h2 in range(2):
                    nc.vector.tensor_tensor(mixS[h2 * 64:h2 * 64 + 64, 6:8, :], o[:, h2, :, :], sqo[:, h2, :, :], ALU.mult)

            @block.tensor
            def _(pe):
                out = lambda bank: bank[0:64, 0:32].rearrange("p (a k s) -> p k s a", a=2, k=2)
                pe.wait_ge(G_STATE, 1)
                for hp in range(HP):
                    for s in range(NS):
                        last = nc.tensor.matmul(out(ps[0])[:, hp, s, :], Gs[:, hp, s, :], qbd[:, hp, s, :], start=True, stop=True)
                last.then_inc(G_OUT, 1)
                pe.wait_ge(G_SQ, 1)
                nc.tensor.matmul(ps[1][0:64, 0:32], ones[0:64, 0:64], sqo[:, :, :, :].rearrange("p a k s -> p (a k s)"),
                                 start=True, stop=True).then_inc(G_SUM, 1)
                pe.wait_ge(C_STATE, 1)
                for hp in range(HP):
                    for s in range(NS):
                        nc.tensor.matmul(out(ps[2])[:, hp, s, :], Cs[:, hp, s, 0:64], qbm[:, hp, s, :], start=True, stop=True)
                for h2 in range(2):
                    last = nc.tensor.matmul(ps[3][0:64, h2 * 16:h2 * 16 + 16], blk[:, h2 * 64:h2 * 64 + 64],
                                            qn[:, :, :].rearrange("p k s -> p (k s)"), start=True, stop=True)
                last.then_inc(M_DEN, 1)
                pe.wait_ge(M_SQ, 1)
                nc.tensor.matmul(ps[4][0:64, 0:32], ones[0:64, 0:64], sqo[:, :, :, :].rearrange("p a k s -> p (a k s)"),
                                 start=True, stop=True).then_inc(M_SUM, 1)



def decode_queries(nc, io, keep, at):
    with ExitStack() as ctx:
        sb = lambda n, s, d=F32: ctx.enter_context(nc.sbuf_tensor(n, s, d))
        sem = semaphores(nc, ctx, "queries")
        q2, gbias = sb("q2", [P, 4, NS]), sb("gbias2", [NR, 3])
        loads, zeroed, gated = sem("q_loads"), sem("q_zeroed"), sem("q_gated")
        qbd, q64, gates, rows_of, of_rows, kwn, ksn, v_new = (
            at[k] for k in ("qbd", "q64", "gates", "rows_of", "of_rows", "kwn", "ksn", "v_new"))
        with nc.Block() as block:

            @block.sync
            def _(sp):
                def load(dst, src):
                    sp.dma_start(dst, src).then_inc(loads, 16)

                for h in range(2):
                    rows = slice(h * 64, h * 64 + 64)
                    load(q2[rows, :, :], io["qkT"][h * 256:h * 256 + 256, T:TT].rearrange("(g d) s -> d g s", d=64))
                    load(ksn[:, :, h], io["qkT"][4 * P + h * 64:4 * P + h * 64 + 64, T:TT])
                    load(kwn[:, :, h], io["qkT"][5 * P + h * 64:5 * P + h * 64 + 64, T:TT])
                for slot, tile in ((0, 7), (1, 9)):
                    for s in range(NS):
                        load(v_new[2 * s:2 * s + 2, slot, :],
                             io["zS"][s, NQ + tile * P:NQ + (tile + 1) * P].rearrange("(h d) -> h d", h=2))
                for s in range(NS):
                    load(gates[8 * s:8 * s + 8, :], io["zS"][s, NG:NG + 24].rearrange("(r b) -> r b", b=3))
                    load(gbias[8 * s:8 * s + 8, :], io["nsa_gate_b"][0, :].rearrange("(r b) -> r b", b=3))

            @block.gpsimd
            def _(pool):
                nc.gpsimd.memset(qbd[:, :, :], 0.0)
                nc.gpsimd.memset(rows_of[:, :], 1.0)
                nc.gpsimd.memset(of_rows[:, :], 1.0).then_inc(zeroed, 1)
                pool.wait_ge(zeroed, 1)
                nc.gpsimd.affine_select(out=rows_of[:, :], in_=rows_of[:, :], compare_op=ALU.is_ge, fill=0.0,
                                        base=0, pattern=[[-4, 16]], channel_multiplier=1)
                nc.gpsimd.affine_select(out=of_rows[:, :], in_=of_rows[:, :], compare_op=ALU.is_ge, fill=0.0,
                                        base=0, pattern=[[1, NR]], channel_multiplier=-4)
                nc.gpsimd.drain()
                nc.gpsimd.affine_select(out=rows_of[:, :], in_=rows_of[:, :], compare_op=ALU.is_ge, fill=0.0,
                                        base=3, pattern=[[4, 16]], channel_multiplier=-1)
                nc.gpsimd.affine_select(out=of_rows[:, :], in_=of_rows[:, :], compare_op=ALU.is_ge, fill=0.0,
                                        base=3, pattern=[[-1, NR]], channel_multiplier=4).then_inc(zeroed, 1)

            @block.vector
            def _(dve):
                dve.wait_ge(loads, 16 * (6 + 4 * NS))
                dve.wait_ge(zeroed, 2)
                for h in range(2):
                    rows = slice(h * 64, h * 64 + 64)
                    nc.vector.tensor_copy(qbd[rows, :, h * 4:h * 4 + 4], q2[rows, :, :].rearrange("p g s -> p s g"))
                    nc.vector.tensor_copy(q64[:, :].rearrange("p (s h g) -> p s h g", h=2, g=4)[:, :, h, :],
                                          q2[rows, :, :].rearrange("p g s -> p s g"))
                nc.vector.tensor_tensor(gates[:, :], gates[:, :], gbias[:, :], ALU.add).then_inc(gated, 1)

            @block.scalar
            def _(act):
                act.wait_ge(gated, 1)
                nc.scalar.activation(gates[:, :], gates[:, :], ACT.Sigmoid)


def decode_window(nc, io, keep, at):
    ident = keep["ident"]
    qbd, q64, gates, rows_of, kwn, v_new, oT = (at[k] for k in ("qbd", "q64", "gates", "rows_of", "kwn", "v_new", "oT"))
    with ExitStack() as ctx:
        sb = lambda n, s, d=F32: ctx.enter_context(nc.sbuf_tensor(n, s, d))
        sem = semaphores(nc, ctx, "window")
        win = sb("win_rows", [P, NS, 4, 256])
        kT = sb("kTw", [P, 2, 4 * P])
        sT = sb("sTw", [P, 4, NR])
        S = sb("Sw", [NR, WIN_ROWS + 1])
        pT = sb("pTw", [P, 4, NR])
        t16, nw = sb("t16", [NR, 16]), sb("nw", [NR, 1])
        den, mx = sb("denw", [NR, 1]), sb("mxw", [NR, 1])
        pg, pgT = sb("pg", [NR, 16]), sb("pgT", [16, NR])
        ps = [ctx.enter_context(nc.psum_tensor(f"pw{i}", [P, 512], F32)) for i in range(8)]
        win_in, kt_done, kt_copied, sc_done, st_copied, s_done, new_done, mx_ready, p_ready, scaled, pt_done, pt_copied, o_done = (
            sem(n) for n in ("win_in", "kt_done", "kt_copied", "wsc_done", "wst_copied", "ws_done", "new_done", "mx_ready", "wp_ready",
                             "scaled", "wpt_done", "wpt_copied", "wo_done"))

        with nc.Block() as block:

            @block.sync
            def _(sp):
                sp.dma_start(win[:, :, :, :].rearrange("p s c x -> p s (c x)"),
                             io["cache_nsa_win"].rearrange("l s (p c) k h d -> p (l s) (c k h d)", c=4)).then_inc(win_in, 16)

            @block.tensor
            def _(pe):
                pe.wait_ge(win_in, 16)
                for s in range(NS):
                    if s >= 2:
                        pe.wait_ge(kt_copied, s - 1)
                    for c in range(4):
                        last = nc.tensor.transpose(ps[s % 2][:, c * P:(c + 1) * P], win[:, s, c, 0:P], ident[:, :])
                    last.then_inc(kt_done, 1)
                    if s:
                        pe.wait_ge(kt_copied, s)
                        for c in range(4):
                            nc.tensor.matmul(ps[2][:, c * NR + (s - 1) * 8:c * NR + s * 8], kT[:, (s - 1) % 2, c * P:(c + 1) * P],
                                             qbd[:, s - 1, :], start=True, stop=True).then_inc(sc_done, 1)
                pe.wait_ge(kt_copied, NS)
                for c in range(4):
                    nc.tensor.matmul(ps[2][:, c * NR + (NS - 1) * 8:c * NR + NS * 8], kT[:, (NS - 1) % 2, c * P:(c + 1) * P],
                                     qbd[:, NS - 1, :], start=True, stop=True).then_inc(sc_done, 1)
                nc.tensor.matmul(ps[3][0:NR, 0:16], q64[:, :], kwn[:, :, :].rearrange("p s h -> p (s h)"), start=True, stop=True).then_inc(new_done, 1)
                pe.wait_ge(st_copied, 1)
                for c in range(4):
                    last = nc.tensor.transpose(ps[4][0:NR, c * P:(c + 1) * P], sT[:, c, :], ident[:, :])
                last.then_inc(s_done, 1)
                pe.wait_ge(scaled, 1)
                for c in range(4):
                    last = nc.tensor.transpose(ps[5][:, c * NR:(c + 1) * NR], S[:, c * P:(c + 1) * P], ident[0:NR, 0:NR])
                last.then_inc(pt_done, 1)
                nc.tensor.transpose(ps[6][0:16, 0:NR], pg[:, :], ident[0:NR, 0:NR]).then_inc(pt_done, 1)
                pe.wait_ge(pt_copied, 2)
                for s in range(NS):
                    for c in range(4):
                        nc.tensor.matmul(ps[7][:, s * 8:s * 8 + 8], win[:, s, c, P:2 * P], pT[:, c, s * 8:s * 8 + 8],
                                         start=(c == 0), stop=(c == 3))
                nc.tensor.matmul(ps[0][0:64, 0:NR], v_new[:, 1, :], pgT[:, :], start=True, stop=True).then_inc(o_done, 1)

            @block.scalar
            def _(act):
                for s in range(NS):
                    act.wait_ge(kt_done, s + 1)
                    if s >= 2:
                        act.wait_ge(sc_done, 4 * (s - 1))
                    nc.scalar.activation(kT[:, s % 2, :], ps[s % 2][:, :], ACT.Copy).then_inc(kt_copied, 1)
                act.wait_ge(sc_done, 4 * NS)
                nc.scalar.activation(sT[:, :, :], ps[2][:, 0:4 * NR].rearrange("p (c r) -> p c r", c=4), ACT.Copy).then_inc(st_copied, 1)
                act.wait_ge(mx_ready, 1)
                nc.scalar.activation(S[:, :], S[:, :], ACT.Exp, bias=mx[:, :], accum_out=den[:, :]).then_inc(p_ready, 1)
                act.wait_ge(pt_done, 2)
                nc.scalar.activation(pT[:, :, :], ps[5][:, 0:4 * NR].rearrange("p (c r) -> p c r", c=4), ACT.Copy).then_inc(pt_copied, 1)
                nc.scalar.activation(pgT[:, :], ps[6][0:16, 0:NR], ACT.Copy).then_inc(pt_copied, 1)

            @block.vector
            def _(dve):
                dve.wait_ge(new_done, 1)
                nc.vector.tensor_tensor(t16[:, :], ps[3][0:NR, 0:16], rows_of[:, :], ALU.mult)
                nc.vector.drain()
                nc.vector.reduce_sum(S[:, WIN_ROWS:WIN_ROWS + 1], t16[:, :], AX.X)
                dve.wait_ge(s_done, 1)
                nc.vector.tensor_copy(S[:, 0:WIN_ROWS], ps[4][0:NR, :])
                nc.vector.drain()
                nc.vector.memset(S[:, 0:1], -BIG)
                nc.vector.drain()
                nc.vector.reduce_max(mx[:, :], S[:, :], AX.X)
                nc.vector.drain()
                nc.vector.tensor_scalar(mx[:, :], mx[:, :], -1.0, None, ALU.mult).then_inc(mx_ready, 1)
                dve.wait_ge(p_ready, 1)
                nc.vector.tensor_scalar(den[:, :], den[:, :], 1e-30, None, ALU.max)
                nc.vector.drain()
                nc.vector.reciprocal(den[:, :], den[:, :])
                nc.vector.drain()
                nc.vector.tensor_tensor(den[:, :], den[:, :], gates[:, WIN:WIN + 1], ALU.mult)
                nc.vector.drain()
                nc.vector.tensor_scalar(S[:, :], S[:, :], den[:, :], None, ALU.mult)
                nc.vector.drain()
                nc.vector.tensor_scalar(pg[:, :], rows_of[:, :], S[:, WIN_ROWS:WIN_ROWS + 1], None, ALU.mult).then_inc(scaled, 1)
                dve.wait_ge(o_done, 1)
                for h in range(2):
                    rows = lambda a: a.rearrange("p (s h g) -> p s h g", h=2, g=4)[:, :, h, :]
                    nc.vector.tensor_copy(rows(oT[:, :]), rows(ps[7][h * 64:h * 64 + 64, 0:NR]))
                nc.vector.drain()
                nc.vector.tensor_tensor(oT[:, :], ps[0][0:64, 0:NR], oT[:, :], ALU.add)


def decode_blocks(nc, io, keep, at):
    ident, eps, ones, g4, cbias, w2, b2, mixS = (keep[k] for k in ("ident", "eps", "ones", "g4", "cbias", "w2", "b2", "mixS"))
    qbd, q64, gates, rows_of, of_rows, ksn, v_new, oT = (
        at[k] for k in ("qbd", "q64", "gates", "rows_of", "of_rows", "ksn", "v_new", "oT"))
    cache = io["cache_nsa_kv"].rearrange("l n (g r) k h d -> (l n g) (r k h d)", r=8)
    NPAGE = L // 128
    with ExitStack() as ctx:
        sb = lambda n, s, d=F32: ctx.enter_context(nc.sbuf_tensor(n, s, d))
        sem = semaphores(nc, ctx, "blocks")
        rows = sb("page_rows", [P, 2, 8 * 512])
        kv = [rows[:, half, :].rearrange("p (r k h d) -> p r k h d", r=8, k=4, h=2) for half in range(2)]
        vall = sb("vall", [P, NS, 16, P])
        w1 = sb("w1_diag", [P, 2, 16, 2, P])
        w2d = sb("w2_diag", [P, 2, P])
        ones_diag = sb("ones_diag", [P, P])
        cb, b2k, b2v = sb("cb", [P, 2]), sb("b2k", [P, 1]), sb("b2v", [1, 2, 64])
        tr = sb("tr", [P, 4, 512])
        sTa = sb("sTa", [P, 16, NR])
        hid = sb("hid_all", [P, 2, NS, P])
        scC = sb("scC", [P, NR])
        after = [rows[:, half, :] for half in range(2)]
        sg = tr[:, :, :].rearrange("p a b -> p (a b)").rearrange("p (j s n) -> p j s n", j=2, s=NS)
        kc = after[1][:, 0:NS * P].rearrange("p (s n) -> p s n", s=NS)
        krt = after[1][:, NS * P:2 * NS * P].rearrange("p (s n) -> p s n", s=NS)
        S = after[0][0:NR, 0:L + 1]
        vcall = after[1][:, 3 * NS * P:4 * NS * P].rearrange("p (s d) -> p s d", s=NS)
        pT = after[1][:, 2 * NS * P:2 * NS * P + 16 * NR].rearrange("p (r c) -> p r c", r=16)
        pc = sb("pc", [NR, P])
        pcT = sb("pcT", [P, NR])
        pages, off, idx = sb("pages", [P, NS], I32), sb("off", [P, 1], I32), sb("idx", [P, 2, NS], I32)
        grp, cand, rank, pick, pen = (
            sb("grp", [16, 130]), sb("cand", [16, 32]), sb("rank", [16, 30]), sb("pick", [16, 32]), sb("pen", [NR, 32]))
        pairs = tr[0:16, :, :].rearrange("p a b -> p (a b)")
        better, tie = (pairs[:, n * 900:(n + 1) * 900].rearrange("p (a b) -> p a b", b=30) for n in range(2))
        earlier = after[0][0:16, 4 * P * 5:4 * P * 5 + 900].rearrange("p (a b) -> p a b", b=30)
        t16, mx, den, mc, dc = sb("t16d", [NR, 16]), sb("mxd", [NR, 1]), sb("dend", [NR, 1]), sb("mxc", [NR, 1]), sb("denc", [NR, 1])
        pg, pgT = sb("pgd", [NR, 16]), sb("pgTd", [16, NR])
        ps = [ctx.enter_context(nc.psum_tensor(f"pb{i}", [P, 512], F32)) for i in range(8)]
        TP, HIDP, SCP, MA, MB = ps[0:3], ps[3:5], ps[5], ps[6], ps[7]
        HID = HIDP[0][:, :].rearrange("p (j w g) -> p j w g", j=2, w=2)
        NFILL = 12

        pages_in, idx_ready, w_in, gathered = sem("pages_in"), sem("idx_ready"), sem("bw_in"), [sem(f"gathered{i}") for i in range(2)]
        f_done, f_copied, f_used, v_kept = sem("f_done"), sem("f_copied"), sem("f_used"), sem("v_kept")
        sc_copied, first_copied, hid_ready, sg_ready, act_ready, zeroed, small_ready = (
            sem("bsc_copied"), sem("bfirst_copied"), sem("bhid_ready"), sem("bsg_ready"), sem("bact_ready"), sem("zeroed"),
            sem("small_ready"))
        kc_done, kc_copied, kss_done, krt_ready, kn_ready, scc_done, vc_done, vc_copied = (
            sem(n) for n in ("bkc_done", "bkc_copied", "bkss_done", "bkrt_ready", "bkn_ready", "bscc_done", "bvc_done", "bvc_copied"))
        c_nat, c_max, c_exp, c_norm, grp_done, pick_ready, pen_done, pen_ready = (
            sem(n) for n in ("c_nat", "c_max", "c_exp", "c_norm", "grp_done", "pick_ready", "pen_done", "pen_ready"))
        s_nat, s_out, new_done, s_max, s_exp, s_norm, pc_done, pc_copied, pt_done, pt_copied, o_done, earl = (
            sem(n) for n in ("s_nat", "s_out", "bnew_done", "s_max", "s_exp", "s_norm", "pc_done", "pc_copied", "bpt_done", "bpt_copied",
                             "bo_done", "earl"))

        with nc.Block() as block:

            @block.sync
            def _(sp):
                for p in range(NPAGE):
                    sp.dma_start(pages[p * 8:p * 8 + 8, :], io["page_table"][:, p:p + 1].rearrange("s a -> a s").broadcast_to([8, NS])).then_inc(pages_in, 16)
                for j in range(2):
                    for h in range(2):
                        for half in range(2):
                            sp.dma_start(w1[h * 64:h * 64 + 64, j, :, half, h * 64:h * 64 + 64],
                                         io["cmp_w1"][0, j, half * 16:half * 16 + 16, :, :].rearrange("r d e -> d r e")).then_inc(w_in, 16)

            @block.gpsimd
            def _(pool):
                nc.gpsimd.iota(off[:, :], pattern=[[0, 1]], base=0, channel_multiplier=1).then_inc(earl, 1)
                nc.gpsimd.memset(w1[0:64, :, :, :, 64:P], 0.0).then_inc(zeroed, 1)
                pool.wait_ge(idx_ready, 1)
                for s in range(NS):
                    for half in range(2):
                        n = 2 * s + half
                        if s:
                            pool.wait_ge(f_done, 6 * (n - 1))
                        nc.gpsimd.indirect_dma_start(out=rows[:, half, :], out_offset=None, in_=cache,
                                                     in_offset=bass.IndirectOffsetOnAxis(ap=idx[:, half, s:s + 1].bitcast(U32), axis=0)
                                                     ).then_inc(gathered[half], 16)
                        if n:
                            m = n - 1
                            pool.wait_ge(gathered[m % 2], 16 * (m // 2 + 1))
                            nc.gpsimd.tensor_copy(vall[:, m // 2, (m % 2) * 8:(m % 2) * 8 + 8, :].rearrange("p r (h d) -> p r h d", h=2),
                                                  kv[m % 2][:, :, 3, :, :]).then_inc(v_kept, 1)
                            pool.wait_ge(v_kept, n)
                pool.wait_ge(gathered[1], 16 * NS)
                nc.gpsimd.tensor_copy(vall[:, NS - 1, 8:16, :].rearrange("p r (h d) -> p r h d", h=2), kv[1][:, :, 3, :, :]).then_inc(v_kept, 1)
                pool.wait_ge(f_done, NFILL * NS)
                nc.gpsimd.memset(earlier[:, :, :], 1.0)
                nc.gpsimd.drain()
                nc.gpsimd.affine_select(out=earlier[:, :, :], in_=earlier[:, :, :], compare_op=ALU.is_gt, fill=0.0,
                                        base=0, pattern=[[1, 30], [-1, 30]], channel_multiplier=0).then_inc(earl, 1)

            @block.tensor
            def _(pe):
                pe.wait_ge(w_in, 16 * 8)
                pe.wait_ge(zeroed, 2)
                with pe.Fori(0, NS) as s:
                    f0 = NFILL * s

                    def fill(half, f):
                        n = half * 6 + f
                        src = kv[half]
                        pe.wait_ge(f_copied, f0 + n - 2) if n >= 3 else pe.wait_ge(f_copied, f0)
                        for u in range(4):
                            token = src[:, (f % 2) * 4 + u, f // 2, :, :].rearrange("p h d -> p (h d)")
                            last = nc.tensor.transpose(TP[n % 3][:, u * P:(u + 1) * P], token, ident[:, :])
                        last.then_inc(f_done, 1)

                    def use(half, f):
                        n = half * 6 + f
                        pe.wait_ge(f_copied, f0 + n + 1)
                        if f < 4:
                            j = f // 2
                            if n == 0:
                                pe.wait_ge(hid_ready, s)
                            for u in range(4):
                                r = half * 8 + (f % 2) * 4 + u
                                for w in range(2):
                                    last = nc.tensor.matmul(HID[:, j, w, :], w1[:, j, r, w, :], tr[:, n % 4, u * P:(u + 1) * P],
                                                            start=(j == 0 and r == 0 and w == 0), stop=(j == 1 and r == 15 and w == 1))
                        else:
                            if n == 4:
                                pe.wait_ge(sc_copied, s)
                            for u in range(4):
                                r = half * 8 + (f - 4) * 4 + u
                                last = nc.tensor.matmul(SCP[:, r * 8:r * 8 + 8], tr[:, n % 4, u * P:(u + 1) * P],
                                                        qbd[:, ds(s, 1), :].rearrange("p a c -> p (a c)"), start=True, stop=True)
                        last.then_inc(f_used, 1)

                    for half in range(2):
                        pe.wait_ge(gathered[half], 16 * (s + 1))
                        for f in range(6):
                            fill(half, f)
                            if f:
                                use(half, f - 1)
                        use(half, 5)
                pe.wait_ge(small_ready, 1)
                pe.wait_ge(act_ready, 1)
                for four in range(2):
                    nc.tensor.matmul([MA, MB][four][:, :], w2d[:, 0, :], hid[:, 0, four * 4:four * 4 + 4, :].rearrange("p s n -> p (s n)"),
                                     start=True, stop=True).then_inc(kc_done, 1)
                pe.wait_ge(act_ready, 2)
                for s in range(NS):
                    out = TP[s // 4][0:NBD, (s % 4) * P:(s % 4 + 1) * P]
                    nc.tensor.matmul(out, hid[:, 1, s, 0:NBD], w2d[:, 1, :], start=(s % 4 == 0), stop=False)
                    last = nc.tensor.matmul(out, ones[0:1, 0:NBD], b2v[:, :, :].rearrange("p h d -> p (h d)"), start=False, stop=(s % 4 == 3))
                    if s % 4 == 3:
                        last.then_inc(vc_done, 1)
                for four in range(2):
                    pe.wait_ge(kc_copied, 2 * four + 2)
                    nc.tensor.matmul([MA, MB][four][:, :], ones_diag[:, :], krt[:, four * 4:four * 4 + 4, :].rearrange("p s n -> p (s n)"),
                                     start=True, stop=True).then_inc(kss_done, 1)
                pe.wait_ge(kn_ready, 1)
                for s in range(NS):
                    last = nc.tensor.matmul(TP[2][0:NBD, s * 8:s * 8 + 8], kc[:, s, 0:NBD], qbd[:, s, :], start=True, stop=True)
                last.then_inc(scc_done, 1)
                pe.wait_ge(vc_copied, 2)

                pe.wait_ge(c_nat, 1)
                nc.tensor.transpose(MA[0:NR, 0:NBD], scC[0:NBD, :], ident[0:NBD, 0:NBD]).then_inc(c_nat, 1)
                nc.tensor.matmul(MB[0:NR, 0:16], q64[:, :], ksn[:, :, :].rearrange("p s h -> p (s h)"), start=True, stop=True).then_inc(new_done, 1)
                pe.wait_ge(sc_copied, NS)

                def selected(b):
                    for u in range(4):
                        last = nc.tensor.transpose(TP[b % 3][0:NR, u * P:(u + 1) * P], sTa[:, b * 4 + u, :], ident[:, :])
                    last.then_inc(s_nat, 1)

                for b in range(3):
                    selected(b)
                pe.wait_ge(c_norm, 1)
                nc.tensor.matmul(HIDP[0][0:16, 0:NBD], rows_of[:, :], pc[:, 0:NBD], start=True, stop=True).then_inc(grp_done, 1)
                pe.wait_ge(pick_ready, 1)
                nc.tensor.matmul(HIDP[1][0:NR, 0:32], of_rows[:, :], pick[:, :], start=True, stop=True).then_inc(pen_done, 1)
                pe.wait_ge(s_out, 1)
                selected(3)
                pe.wait_ge(c_norm, 2)
                nc.tensor.transpose(MA[0:NBD, 0:NR], pc[:, 0:NBD], ident[0:NR, 0:NR]).then_inc(pc_done, 1)
                pe.wait_ge(s_norm, 1)
                pe.wait_ge(s_out, 4)
                for b in range(4):
                    if b >= 3:
                        pe.wait_ge(pt_copied, 1)
                    for u in range(4):
                        r = b * 4 + u
                        last = nc.tensor.transpose(TP[b % 3][:, u * NR:(u + 1) * NR], S[:, r * P:(r + 1) * P], ident[0:NR, 0:NR])
                    last.then_inc(pt_done, 1)
                nc.tensor.transpose(MB[0:16, 0:NR], pg[:, :], ident[0:NR, 0:NR]).then_inc(pt_done, 1)
                pe.wait_ge(pc_copied, 1)
                pe.wait_ge(pt_copied, 5)
                pe.wait_ge(v_kept, 2 * NS)
                for s in range(NS):
                    cols = slice(s * 8, s * 8 + 8)
                    nc.tensor.matmul(SCP[:, cols], vcall[0:NBD, s, :], pcT[0:NBD, cols], start=True, stop=False)
                    for r in range(16):
                        nc.tensor.matmul(SCP[:, cols], vall[:, s, r, :], pT[:, r, cols], start=False, stop=(r == 15))
                nc.tensor.matmul(HIDP[0][0:64, 0:NR], v_new[:, 0, :], pgT[:, :], start=True, stop=True).then_inc(o_done, 1)

            @block.scalar
            def _(act):
                with act.Fori(0, NS) as s:
                    f0 = NFILL * s
                    for n in range(0, NFILL, 2):
                        act.wait_ge(f_done, f0 + n + 1)
                        if n >= 4:
                            act.wait_ge(f_used, f0 + n - 3)
                        else:
                            act.wait_ge(f_used, f0)
                        act.wait_ge(f_copied, f0 + n)
                        nc.scalar.activation(tr[:, n % 4, :], TP[n % 3][:, :], ACT.Copy).then_inc(f_copied, 1)
                    act.wait_ge(f_used, f0 + 10)
                    act.wait_ge(f_copied, f0 + NFILL)
                    nc.scalar.activation(hid[:, :, ds(s, 1), :], HID[:, :, 0, :].unsqueeze(2), ACT.Copy).then_inc(first_copied, 1)
                    act.wait_ge(f_used, f0 + NFILL)
                    nc.scalar.activation(sTa[:, :, ds(s * 8, 8)], SCP[:, 0:P].rearrange("p (r c) -> p r c", r=16), ACT.Copy).then_inc(sc_copied, 1)
                act.wait_ge(hid_ready, NS)
                act.wait_ge(small_ready, 1)
                act.wait_ge(v_kept, 2 * NS)
                act.wait_ge(f_done, NFILL * NS)
                for j in range(2):
                    nc.scalar.activation(sg[:, j, :, :], hid[:, j, :, :], ACT.Sigmoid, bias=cb[:, j:j + 1]).then_inc(sg_ready, 1)
                for four in range(2):
                    act.wait_ge(kc_done, four + 1)
                    at = slice(four * 4, four * 4 + 4)
                    v = [MA, MB][four][:, :].rearrange("p (s n) -> p s n", s=4)
                    nc.scalar.activation(kc[:, at, :], v, ACT.Identity, bias=b2k[:, :]).then_inc(kc_copied, 1)
                    nc.scalar.activation(krt[:, at, :], v, ACT.Square, bias=b2k[:, :]).then_inc(kc_copied, 1)
                for four in range(2):
                    act.wait_ge(vc_done, four + 1)
                    nc.scalar.activation(vcall[0:NBD, four * 4:four * 4 + 4, :],
                                         TP[four][0:NBD, :].rearrange("p (s d) -> p s d", s=4), ACT.Copy).then_inc(vc_copied, 1)
                for four in range(2):
                    act.wait_ge(kss_done, four + 1)
                    nc.scalar.activation(krt[:, four * 4:four * 4 + 4, :], [MA, MB][four][:, :].rearrange("p (s n) -> p s n", s=4),
                                         ACT.Sqrt, scale=1.0 / HD, bias=eps[:, :]).then_inc(krt_ready, 1)
                act.wait_ge(scc_done, 1)
                nc.scalar.activation(scC[0:NBD, :], TP[2][0:NBD, 0:NR], ACT.Copy)
                nc.scalar.drain()
                nc.scalar.activation(mc[:, :], gates[:, 0:1], ACT.Copy).then_inc(c_nat, 1)
                act.wait_ge(c_max, 1)
                nc.scalar.activation(pc[:, 0:NBD], pc[:, 0:NBD], ACT.Exp, bias=mc[:, :], accum_out=dc[:, :]).then_inc(c_exp, 1)
                act.wait_ge(s_max, 1)
                nc.scalar.activation(S[:, :], S[:, :], ACT.Exp, bias=mx[:, :], accum_out=den[:, :]).then_inc(s_exp, 1)
                act.wait_ge(pc_done, 1)
                nc.scalar.activation(pcT[0:NBD, :], MA[0:NBD, 0:NR], ACT.Copy).then_inc(pc_copied, 1)
                for b in range(4):
                    act.wait_ge(pt_done, b + 1)
                    nc.scalar.activation(pT[:, b * 4:b * 4 + 4, :], TP[b % 3][:, 0:4 * NR].rearrange("p (u r) -> p u r", u=4),
                                         ACT.Copy).then_inc(pt_copied, 1)
                act.wait_ge(pt_done, 5)
                nc.scalar.activation(pgT[:, :], MB[0:16, 0:NR], ACT.Copy).then_inc(pt_copied, 1)

            @block.vector
            def _(dve):
                dve.wait_ge(pages_in, 16 * NPAGE)
                dve.wait_ge(earl, 1)
                nc.vector.tensor_scalar(off[:, :], off[:, :], 7, 1, ALU.bitwise_and, ALU.logical_shift_left)
                nc.vector.tensor_scalar(pages[:, :], pages[:, :], 4, None, ALU.logical_shift_left)
                nc.vector.drain()
                nc.vector.tensor_tensor(idx[:, 0, :], pages[:, :], off[:, :].broadcast_to([P, NS]), ALU.bitwise_or)
                nc.vector.drain()
                nc.vector.tensor_scalar(idx[:, 1, :], idx[:, 0, :], 1, None, ALU.bitwise_or).then_inc(idx_ready, 1)
                nc.vector.memset(w1[64:P, :, :, :, 0:64], 0.0).then_inc(zeroed, 1)
                nc.vector.memset(w2d[:, :, :], 0.0)
                nc.vector.memset(ones_diag[:, :], 0.0)
                nc.vector.drain()
                for h in range(2):
                    at = slice(h * 64, h * 64 + 64)
                    nc.vector.tensor_copy(w2d[at, :, at], w2[:, :, :])
                    nc.vector.memset(ones_diag[at, at], 1.0)
                    nc.vector.tensor_copy(cb[at, :], cbias[:, :])
                    nc.vector.tensor_copy(b2k[at, :], b2[:, 0:1])
                    nc.vector.tensor_copy(b2v[:, h, :], b2[0:1, 1:65])
                nc.vector.engine_nop().then_inc(small_ready, 1)
                with dve.Fori(0, NS) as s:
                    f0 = NFILL * s
                    for n in range(1, NFILL, 2):
                        dve.wait_ge(f_done, f0 + n + 1)
                        if n >= 4:
                            dve.wait_ge(f_used, f0 + n - 3)
                        else:
                            dve.wait_ge(f_used, f0)
                        dve.wait_ge(f_copied, f0 + n)
                        nc.vector.tensor_copy(tr[:, n % 4, :], TP[n % 3][:, :]).then_inc(f_copied, 1)
                    dve.wait_ge(first_copied, s + 1)
                    own = hid[:, :, ds(s, 1), 0:NBD]
                    nc.vector.tensor_tensor(own, HID[:, :, 1, 1:P].unsqueeze(2), own, ALU.add).then_inc(hid_ready, 1)
                for j in range(2):
                    dve.wait_ge(sg_ready, j + 1)
                    nc.vector.scalar_tensor_tensor(out=hid[:, j, :, :], in0=hid[:, j, :, :], scalar=cb[:, j:j + 1],
                                                   in1=sg[:, j, :, :], op0=ALU.add, op1=ALU.mult).then_inc(act_ready, 1)
                for four in range(2):
                    at = slice(four * 4, four * 4 + 4)
                    dve.wait_ge(krt_ready, four + 1)
                    nc.vector.reciprocal(krt[:, at, :], krt[:, at, :])
                    nc.vector.drain()
                    nc.vector.scalar_tensor_tensor(out=kc[:, at, :], in0=kc[:, at, :], scalar=g4[:, 1:2], in1=krt[:, at, :],
                                                   op0=ALU.mult, op1=ALU.mult)
                nc.vector.engine_nop().then_inc(kn_ready, 1)
                dve.wait_ge(c_nat, 2)
                nc.vector.tensor_copy(pc[:, 0:NBD], MA[0:NR, 0:NBD])
                nc.vector.drain()
                nc.vector.reduce_max(mc[:, :], pc[:, 0:NBD], AX.X)
                nc.vector.drain()
                nc.vector.tensor_scalar(mc[:, :], mc[:, :], -1.0, None, ALU.mult).then_inc(c_max, 1)
                dve.wait_ge(c_exp, 1)
                nc.vector.tensor_scalar(dc[:, :], dc[:, :], 1e-30, None, ALU.max)
                nc.vector.drain()
                nc.vector.reciprocal(dc[:, :], dc[:, :])
                nc.vector.drain()
                nc.vector.tensor_scalar(pc[:, 0:NBD], pc[:, 0:NBD], dc[:, :], None, ALU.mult).then_inc(c_norm, 1)
                nc.vector.memset(grp[:, :], 0.0)
                nc.vector.drain()
                dve.wait_ge(grp_done, 1)
                nc.vector.tensor_copy(grp[:, 1:1 + NBD], HIDP[0][0:16, 0:NBD])
                nc.vector.drain()
                nc.vector.tensor_scalar(pc[:, 0:NBD], pc[:, 0:NBD], gates[:, CMP:CMP + 1], None, ALU.mult).then_inc(c_norm, 1)
                nc.vector.tensor_tensor(tie[:, 0:5, :].rearrange("p a b -> p (a b)")[:, 0:P], grp[:, 1:1 + P], grp[:, 0:P], ALU.add)
                nc.vector.drain()
                nc.vector.reduce_sum(cand[:, :], tie[:, 0:5, :].rearrange("p a b -> p (a b)")[:, 0:P].rearrange("p (j r) -> p j r", r=4), AX.X)
                nc.vector.drain()
                own = cand[:, 1:31].unsqueeze(2).broadcast_to([16, 30, 30])
                other = cand[:, 1:31].unsqueeze(1).broadcast_to([16, 30, 30])
                nc.vector.tensor_tensor(better[:, :, :], other, own, ALU.is_gt)
                nc.vector.tensor_tensor(tie[:, :, :], other, own, ALU.is_equal)
                nc.vector.drain()
                dve.wait_ge(earl, 2)
                nc.vector.tensor_tensor(tie[:, :, :], tie[:, :, :], earlier[:, :, :], ALU.mult)
                nc.vector.drain()
                nc.vector.tensor_tensor(better[:, :, :], better[:, :, :], tie[:, :, :], ALU.add)
                nc.vector.drain()
                nc.vector.reduce_sum(rank[:, :], better[:, :, :], AX.X)
                nc.vector.memset(pick[:, :], 1.0)
                nc.vector.drain()
                nc.vector.tensor_scalar(pick[:, 1:31], rank[:, :], 12.5, None, ALU.is_lt).then_inc(pick_ready, 1)
                dve.wait_ge(pen_done, 1)
                nc.vector.tensor_scalar(pen[:, :], HIDP[1][0:NR, 0:32], -1.0, BIG, ALU.add, ALU.mult)
                nc.vector.drain()
                for b in range(4):
                    dve.wait_ge(s_nat, b + 1)
                    nc.vector.tensor_tensor(S[:, b * 512:(b + 1) * 512].rearrange("p (u j w) -> p u j w", u=4, w=4),
                                            TP[b % 3][0:NR, :].rearrange("p (u j w) -> p u j w", u=4, w=4),
                                            pen[:, :].unsqueeze(1).unsqueeze(3).broadcast_to([NR, 4, 32, 4]), ALU.add).then_inc(s_out, 1)
                dve.wait_ge(new_done, 1)
                nc.vector.tensor_tensor(t16[:, :], MB[0:NR, 0:16], rows_of[:, :], ALU.mult)
                nc.vector.drain()
                nc.vector.reduce_sum(S[:, L:L + 1], t16[:, :], AX.X)
                nc.vector.drain()
                nc.vector.reduce_max(mx[:, :], S[:, :], AX.X)
                nc.vector.drain()
                nc.vector.tensor_scalar(mx[:, :], mx[:, :], -1.0, None, ALU.mult).then_inc(s_max, 1)
                dve.wait_ge(s_exp, 1)
                nc.vector.tensor_scalar(den[:, :], den[:, :], 1e-30, None, ALU.max)
                nc.vector.drain()
                nc.vector.reciprocal(den[:, :], den[:, :])
                nc.vector.drain()
                nc.vector.tensor_tensor(den[:, :], den[:, :], gates[:, FULL:FULL + 1], ALU.mult)
                nc.vector.drain()
                nc.vector.tensor_scalar(S[:, :], S[:, :], den[:, :], None, ALU.mult)
                nc.vector.drain()
                nc.vector.tensor_scalar(pg[:, :], rows_of[:, :], S[:, L:L + 1], None, ALU.mult).then_inc(s_norm, 1)
                dve.wait_ge(o_done, 1)
                nc.vector.tensor_tensor(oT[:, :], HIDP[0][0:64, 0:NR], oT[:, :], ALU.add)
                nc.vector.drain()
                for h in range(2):
                    rws = lambda a: a.rearrange("p (s h g) -> p s h g", h=2, g=4)[:, :, h, :]
                    nc.vector.tensor_tensor(rws(oT[:, :]), rws(SCP[h * 64:h * 64 + 64, 0:NR]), rws(oT[:, :]), ALU.add)
                nc.vector.drain()
                for g2 in range(2):
                    for h in range(2):
                        nc.vector.tensor_copy(mixS[g2 * 64:g2 * 64 + 64, 2 + 2 * h:4 + 2 * h, :],
                                              oT[:, :].rearrange("p (s h g a) -> p h a g s", h=2, g=2, a=2)[:, h, g2, :, :])


def decode(nc, io, keep):
    decode_recurrences(nc, io, keep)
    with ExitStack() as ctx:
        sb = lambda n, s, d=F32: ctx.enter_context(nc.sbuf_tensor(n, s, d))
        at = {
            "qbd": sb("qbd_n", [P, NS, 8]), "q64": sb("q64", [64, NR]), "gates": sb("gates_dec", [NR, 3]),
            "rows_of": sb("rows_of", [NR, 16]), "of_rows": sb("of_rows", [16, NR]),
            "kwn": sb("kwn", [64, NS, 2]), "ksn": sb("ksn", [64, NS, 2]), "v_new": sb("v_new", [16, 2, 64]),
            "oT": sb("oT", [64, NR]),
        }
        decode_queries(nc, io, keep, at)
        decode_window(nc, io, keep, at)
        decode_blocks(nc, io, keep, at)


def mix_and_project(nc, io, keep, x2T, hH, hL):
    ident, eps, ones, uact, onat, hs, RN, mixS = (keep[k] for k in ("ident", "eps", "ones", "uact", "onat", "hs", "rows_cols", "mixS"))
    zT = io["zT"]
    w_out = io["w_out"].rearrange("l (k p) n -> p (l k) n", p=P)
    with ExitStack() as ctx:
        sb = lambda n, s, d=F32: ctx.enter_context(nc.sbuf_tensor(n, s, d))
        sem = semaphores(nc, ctx, "mix")
        mixH, mixL = hH, hL
        wo, woH, woL = sb("wo", [P, KD, P]), sb("woH", [P, KD, P], F32R), sb("woL", [P, KD, P], F32R)
        mixc = sb("mixc", [P, KD, P])
        gr, mo, sig = sb("gr", [P, HP, TT]), sb("mo", [P, HP, TT]), sb("sig", [P, HP, TT])
        ss = sb("ssh", [P, 2, NCH * 4])
        nd = sb("nd", [P, NCH, 4])
        tmp = sb("tmpm", [P, HP, P])
        gains = sb("gains", [P, 2])
        skip, g2 = sb("skip", [P, HP]), sb("g2", [P, KD])
        sqx = sb("sqx", [P, 2, TT])
        sq = sqx[:, :, :].rearrange("p a t -> p (a t)")[:, 0:NCH * 4 * 64].rearrange("p (n e) -> p n e", e=64)
        rn = sb("rn", [P, TT])
        ps = [ctx.enter_context(nc.psum_tensor(f"pg{i}", [P, 512], F32)) for i in range(8)]
        gates_in, x_in, sig_done, div_done, sq_done, ss_done, rt_done, normed, gated = (
            sem("gates_in"), [sem(f"x_in{i}") for i in range(2)], sem("sig_done3"), sem("div_done"), sem("sq_done"), sem("ssum_done"), sem("rt_done"),
            sem("normed"), sem("gated"))
        t_done, t_used = sem("t_done"), sem("t_used")
        wo_in, woH_ready, woL_ready = sem("wo_in"), sem("woH_ready"), sem("woL_ready")
        mixc_ready, mixH_ready, mixL_ready = sem("mixc_ready"), sem("mixH_ready"), sem("mixL_ready")
        hc_ready, hH_ready, hL_ready = sem("hc_ready"), sem("hH_ready"), sem("hL_ready")
        y_done, y_added, sqx_done, sum_done, rn_done = (
            sem("y_done"), sem("y_added"), sem("sqx_done"), sem("sum_done"), sem("rn_done"))
        heads = lambda at: onat[:, :, at:at + 256].rearrange("p i (h e) -> p i h e", h=4)

        with nc.Block() as block:

            @block.sync
            def _(sp):
                sp.dma_start(gr[:, :, :], zT[GR:GR + 256, :].rearrange("(j p) t -> p j t", p=P)).then_inc(gates_in, 16)
                sp.dma_start(mo[:, :, :], zT[MO:MO + 256, :].rearrange("(j p) t -> p j t", p=P)).then_inc(gates_in, 16)
                for half in range(2):
                    at = slice(half * 64, half * 64 + 64)
                    sp.dma_start(gains[at, 0:1], io["gla_norm_g"].rearrange("l d -> d l")).then_inc(gates_in, 16)
                    sp.dma_start(gains[at, 1:2], io["ml_norm_g"].rearrange("l d -> d l")).then_inc(gates_in, 16)
                sp.dma_start(skip[:, :], io["ml_skip"].rearrange("l (k p) -> p (l k)", p=P)).then_inc(gates_in, 16)
                sp.dma_start(g2[:, :], io["norm2_g"].rearrange("l (k p) -> p (l k)", p=P)).then_inc(gates_in, 16)
                sp.dma_start(wo[:, :, :], w_out[:, :, 0:P]).then_inc(wo_in, 16)
                sp.wait_ge(t_done, TQ)
                for half in range(2):
                    at = slice(half * KD // 2, (half + 1) * KD // 2)
                    sp.dma_start(x2T[:, at, :], io["xT"].rearrange("(k p) t -> p k t", p=P)[:, at, :]).then_inc(x_in[half], 16)
                with sp.Fori(1, KD) as m:
                    sp.wait_ge(woL_ready, m)
                    sp.dma_start(wo[:, :, :], w_out[:, :, ds(m * P, P)]).then_inc(wo_in, 16)

            @block.scalar
            def _(act):
                act.wait_ge(gates_in, 16 * 8)
                nc.scalar.activation(sig[:, :, :], gr[:, :, :], ACT.Sigmoid).then_inc(sig_done, 1)
                nc.scalar.activation(mo[:, :, :], mo[:, :, :], ACT.Sigmoid).then_inc(sig_done, 1)
                for n, at in enumerate((0, 768)):
                    if n:
                        act.wait_ge(div_done, 1)
                        act.wait_ge(ss_done, 1)
                    nc.scalar.activation(sq[:, :, :].rearrange("p (i h) e -> p i h e", h=4), heads(at), ACT.Square).then_inc(sq_done, 1)
                    act.wait_ge(ss_done, n + 1)
                    nc.scalar.activation(ss[:, n, :], ss[:, n, :], ACT.Sqrt, scale=1.0 / HD, bias=eps[:, :]).then_inc(rt_done, 1)
                for i in range(TQ + 1):
                    n = P if i < TQ else NS
                    act.wait_ge(mixc_ready, i + 1)
                    nc.scalar.activation(mixH[:, :, i * P:i * P + n], mixc[:, :, 0:n], ACT.Copy).then_inc(mixH_ready, 1)
                act.wait_ge(wo_in, 16)
                nc.scalar.activation(woH[:, :, :], wo[:, :, :], ACT.Copy).then_inc(woH_ready, 1)
                for m in range(1, KD):
                    act.wait_ge(wo_in, 16 * (m + 1))
                    act.wait_ge(y_done, NT * m)
                    nc.scalar.activation(woH[:, :, :], wo[:, :, :], ACT.Copy).then_inc(woH_ready, 1)
                for k in range(KD):
                    act.wait_ge(y_added, NT * (k + 1))
                    if k >= 2:
                        act.wait_ge(sum_done, k - 1)
                    nc.scalar.activation(sqx[:, k % 2, :], x2T[:, k, :], ACT.Square).then_inc(sqx_done, 1)
                act.wait_ge(sum_done, KD)
                for third in range(NT):
                    last = nc.scalar.activation(rn[:, third * TC:(third + 1) * TC], ps[third][:, 0:TC], ACT.Sqrt, scale=1.0 / D, bias=eps[:, :])
                last.then_inc(rn_done, 1)
                for k in range(KD):
                    act.wait_ge(hc_ready, k + 1)
                    nc.scalar.activation(hH[:, k, :], sqx[:, k % 2, :], ACT.Copy).then_inc(hH_ready, 1)

            @block.vector
            def _(dve):
                den = hs[:, :, :, 64]
                nc.vector.tensor_scalar(nd[:, :, :], den, -1.0, None, ALU.mult)
                nc.vector.drain()
                nc.vector.tensor_tensor(nd[:, :, :], nd[:, :, :], den, ALU.max)
                nc.vector.drain()
                nc.vector.tensor_tensor(nd[:, :, :], nd[:, :, :], RN[:, :, 12:16], ALU.max)
                nc.vector.drain()
                nc.vector.reciprocal(nd[:, :, :], nd[:, :, :])
                nc.vector.drain()
                nc.vector.tensor_tensor(heads(768), hs[:, :, :, 0:64], nd[:, :, :].unsqueeze(3).broadcast_to([P, NCH, 4, 64]),
                                        ALU.mult).then_inc(div_done, 1)
                dve.wait_ge(gates_in, 16 * 8)
                dve.wait_ge(sig_done, 2)
                for hp in range(HP):
                    nc.vector.scalar_tensor_tensor(out=gr[:, hp, :], in0=gr[:, hp, :], scalar=gains[:, 0:1], in1=sig[:, hp, :],
                                                   op0=ALU.mult, op1=ALU.mult)
                    nc.vector.scalar_tensor_tensor(out=uact[:, hp, :], in0=uact[:, hp, :], scalar=skip[:, hp:hp + 1], in1=mo[:, hp, :],
                                                   op0=ALU.mult, op1=ALU.mult)
                nc.vector.drain()
                nc.vector.tensor_scalar(mo[:, :, :], mo[:, :, :], gains[:, 1:2], None, ALU.mult)
                for n, at in enumerate((0, 768)):
                    dve.wait_ge(sq_done, n + 1)
                    nc.vector.reduce_sum(ss[:, n, :], sq[:, :, :], AX.X).then_inc(ss_done, 1)
                    dve.wait_ge(rt_done, n + 1)
                    nc.vector.reciprocal(ss[:, n, :], ss[:, n, :])
                    nc.vector.drain()
                    nc.vector.tensor_tensor(heads(at), heads(at),
                                            ss[:, n, :].rearrange("p (i h) -> p i h", h=4).unsqueeze(3).broadcast_to([P, NCH, 4, 64]),
                                            ALU.mult).then_inc(normed, 1)
                nc.vector.drain()
                def split_mix(i, n):
                    dve.wait_ge(mixH_ready, i + 1)
                    nc.vector.tensor_tensor(mixL[:, :, i * P:i * P + n], mixc[:, :, 0:n], mixH[:, :, i * P:i * P + n].bitcast(F32),
                                            ALU.subtract).then_inc(mixL_ready, 1)

                for i in range(TQ):
                    at = slice(i * P, (i + 1) * P)
                    a, b = ps[2 * (i % 2)], ps[2 * (i % 2) + 1]
                    pair = lambda bank, lo: bank[:, lo * P:(lo + 2) * P].rearrange("p (k t) -> p k t", k=2)
                    dve.wait_ge(t_done, i + 1)
                    nc.vector.tensor_tensor(mixc[:, 0:2, :], pair(a, 0), gr[:, :, at], ALU.mult)
                    nc.vector.tensor_copy(mixc[:, 2:4, :], pair(a, 2))
                    nc.vector.tensor_copy(mixc[:, 4:6, :], pair(b, 0))
                    nc.vector.tensor_tensor(tmp[:, :, :], pair(b, 2), mo[:, :, at], ALU.mult).then_inc(t_used, 1)
                    nc.vector.drain()
                    nc.vector.tensor_tensor(mixc[:, 6:8, :], tmp[:, :, :], uact[:, :, at], ALU.add).then_inc(mixc_ready, 1)
                    split_mix(i, P)
                    nc.vector.drain()
                at = slice(T, TT)
                nc.vector.tensor_tensor(mixc[:, 0:2, 0:NS], mixS[:, 0:2, :], gr[:, :, at], ALU.mult)
                nc.vector.tensor_copy(mixc[:, 2:6, 0:NS], mixS[:, 2:6, :])
                nc.vector.tensor_tensor(tmp[:, :, 0:NS], mixS[:, 6:8, :], mo[:, :, at], ALU.mult)
                nc.vector.drain()
                nc.vector.tensor_tensor(mixc[:, 6:8, 0:NS], tmp[:, :, 0:NS], uact[:, :, at], ALU.add).then_inc(mixc_ready, 1)
                split_mix(TQ, NS)
                def low_weights(m):
                    dve.wait_ge(woH_ready, m + 1)
                    nc.vector.tensor_tensor(woL[:, :, :], wo[:, :, :], woH[:, :, :].bitcast(F32), ALU.subtract).then_inc(woL_ready, 1)

                low_weights(0)
                for m in range(KD):
                    dve.wait_ge(x_in[m // (KD // 2)], 16)
                    for third in range(NT):
                        cols = slice(third * TC, (third + 1) * TC)
                        dve.wait_ge(y_done, NT * m + third + 1)
                        if third == NT - 1 and m + 1 < KD:
                            low_weights(m + 1)
                        nc.vector.tensor_tensor(x2T[:, m, cols], ps[2 + (m % 2) * 3 + third][:, 0:TC], x2T[:, m, cols],
                                                ALU.add).then_inc(y_added, 1)
                dve.wait_ge(rn_done, 1)
                nc.vector.reciprocal(rn[:, :], rn[:, :])
                nc.vector.drain()
                def scaled(k):
                    if k >= 2:
                        nc.vector.drain()
                    nc.vector.scalar_tensor_tensor(out=sqx[:, k % 2, :], in0=x2T[:, k, :], scalar=g2[:, k:k + 1], in1=rn[:, :],
                                                   op0=ALU.mult, op1=ALU.mult).then_inc(hc_ready, 1)

                scaled(0)
                for k in range(KD):
                    if k + 1 < KD:
                        scaled(k + 1)
                    dve.wait_ge(hH_ready, k + 1)
                    nc.vector.tensor_tensor(hL[:, k, :], sqx[:, k % 2, :], hH[:, k, :].bitcast(F32), ALU.subtract).then_inc(hL_ready, 1)

            @block.tensor
            def _(pe):
                pe.wait_ge(normed, 2)
                for i in range(TQ):
                    if i >= 2:
                        pe.wait_ge(t_used, i - 1)
                    for k in range(KD):
                        last = nc.tensor.transpose(ps[2 * (i % 2) + k // 4][:, (k % 4) * P:(k % 4 + 1) * P],
                                                   onat[:, i, k * P:(k + 1) * P], ident[:, :])
                    last.then_inc(t_done, 1)
                pe.wait_ge(mixH_ready, TQ + 1)
                pe.wait_ge(mixL_ready, TQ + 1)
                for m in range(KD):
                    pe.wait_ge(woH_ready, m + 1)
                    pe.wait_ge(woL_ready, m + 1)
                    if m >= 2:
                        pe.wait_ge(y_added, NT * (m - 1))
                    for third in range(NT):
                        split_product(nc, ps[2 + (m % 2) * 3 + third][:, 0:TC], [(woH[:, k, :], woL[:, k, :]) for k in range(KD)],
                                      [(mixH[:, k, third * TC:(third + 1) * TC], mixL[:, k, third * TC:(third + 1) * TC])
                                       for k in range(KD)]).then_inc(y_done, 1)
                pe.wait_ge(y_added, NT * KD)
                for k in range(KD):
                    pe.wait_ge(sqx_done, k + 1)
                    for third in range(NT):
                        last = nc.tensor.matmul(ps[third][:, 0:TC], ones[:, :], sqx[:, k % 2, third * TC:(third + 1) * TC],
                                                start=(k == 0), stop=(k == KD - 1))
                    last.then_inc(sum_done, 1)


FG = 2
NFG = 4 * D // P // FG


def channel_mixer(nc, io, keep, x2T, hH, hL):
    ident = keep["ident"]
    w_up = io["w_up"].rearrange("l (k p) n -> p (l k) n", p=P)
    w_down = io["w_down"].rearrange("l (f p) n -> p (l f) n", p=P)
    y_p, y_s = io["out0"].rearrange("b t d -> (b t) d"), io["out1"].rearrange("b t d -> (b t) d")
    with ExitStack() as ctx:
        sb = lambda n, s, d=F32: ctx.enter_context(nc.sbuf_tensor(n, s, d))
        sem = semaphores(nc, ctx, "channel")
        wu = keep["uact"][:, :, :].rearrange("p a t -> p (a t)")[:, 0:KD * FG * P].rearrange("p (k n) -> p k n", k=KD)
        wd = keep["hs"][:, :, :, :].rearrange("p i h e -> p (i h e)")[:, 0:FG * D].rearrange("p (f n) -> p f n", f=FG)
        wuH, wuL = sb("wuH", [P, FG, KD, P], F32R), sb("wuL", [P, FG, KD, P], F32R)
        wdH, wdL = sb("wdH", [P, FG, D], F32R), sb("wdL", [P, FG, D], F32R)
        act2 = sb("act2", [P, FG, TT])
        hidH, hidL = sb("hidH", [P, 2, FG, TT], F32R), sb("hidL", [P, 2, FG, TT], F32R)
        ynat = act2[:, :, 0:D]
        ps = [ctx.enter_context(nc.psum_tensor(f"ph{i}", [P, 512], F32)) for i in range(8)]
        wu_in, wuH_ready, wuL_ready = sem("wu_in"), sem("wuH_ready"), sem("wuL_ready")
        wd_in, wdH_ready, wdL_ready = sem("wd_in"), sem("wdH_ready"), sem("wdL_ready")
        up_done, relu_done, hidH_ready, hidL_ready, down_done, added = (
            sem("up_done"), sem("relu_done"), sem("hidH_ready"), sem("hidL_ready"), sem("down_done"), sem("added"))
        out_t, out_a, out_b = sem("out_t"), sem("out_a"), sem("out_b")
        stored = [sem(f"y_stored{i}") for i in range(2)]
        NUP, NDN = FG * NT, KD * NT

        with nc.Block() as block:

            @block.sync
            def _(sp):
                sp.dma_start(wu[:, :, :], w_up[:, :, 0:FG * P]).then_inc(wu_in, 16)
                sp.dma_start(wd[:, :, :], w_down[:, 0:FG, :]).then_inc(wd_in, 16)
                with sp.Fori(1, NFG) as g:
                    sp.wait_ge(wuL_ready, FG * g)
                    sp.dma_start(wu[:, :, :], w_up[:, :, ds(g * FG * P, FG * P)]).then_inc(wu_in, 16)
                    sp.wait_ge(wdL_ready, g)
                    sp.dma_start(wd[:, :, :], w_down[:, ds(g * FG, FG), :]).then_inc(wd_in, 16)
                for i in range(9):
                    n, dst = (P, y_p[i * P:(i + 1) * P, :]) if i < 8 else (NS, y_s)
                    sp.wait_ge(out_a, i + 1)
                    sp.wait_ge(out_b, i + 1)
                    sp.dma_start(dst, ynat[0:n, i % 2, :]).then_inc(stored[i % 2], 16)
                sp.wait_ge(stored[0], 16 * 5)
                sp.wait_ge(stored[1], 16 * 4)

            @block.tensor
            def _(pe):
                def up(g, first=False):
                    for f in range(FG):
                        pe.wait_ge(wuH_ready, FG * g + f + 1)
                        pe.wait_ge(wuL_ready, FG * g + f + 1)
                        for third in range(NT):
                            n = f * NT + third
                            cols = slice(third * TC, (third + 1) * TC)
                            if not first or n >= 3:
                                pe.wait_ge(relu_done, NUP * g + n - 2)
                            split_product(nc, ps[n % 3][:, 0:TC], [(wuH[:, f, k, :], wuL[:, f, k, :]) for k in range(KD)],
                                          [(hH[:, k, cols], hL[:, k, cols]) for k in range(KD)]).then_inc(up_done, 1)

                def down(g, slot):
                    pe.wait_ge(wdH_ready, g + 1)
                    pe.wait_ge(wdL_ready, g + 1)
                    pe.wait_ge(hidH_ready, FG * g + FG)
                    pe.wait_ge(hidL_ready, FG * g + FG)
                    for m in range(KD):
                        out = slice(m * P, (m + 1) * P)
                        for third in range(NT):
                            n = m * NT + third
                            cols = slice(third * TC, (third + 1) * TC)
                            if n >= 4:
                                pe.wait_ge(added, NDN * g + n - 3)
                            else:
                                pe.wait_ge(added, NDN * g)
                            split_product(nc, ps[4 + n % 4][:, 0:TC], [(wdH[:, f, out], wdL[:, f, out]) for f in range(FG)],
                                          [(hidH[:, slot, f, cols], hidL[:, slot, f, cols]) for f in range(FG)]).then_inc(down_done, 1)

                up(0, first=True)
                with pe.Fori(0, NFG // 2 - 1) as it:
                    for slot in range(2):
                        up(2 * it + slot + 1)
                        down(2 * it + slot, slot)
                up(NFG - 1)
                down(NFG - 2, 0)
                down(NFG - 1, 1)
                pe.wait_ge(added, NDN * NFG)
                for i in range(9):
                    n = P if i < 8 else NS
                    if i >= 2:
                        pe.wait_ge(out_a, i - 1)
                        pe.wait_ge(out_b, i - 1)
                    for k in range(KD):
                        last = nc.tensor.transpose(ps[2 * (i % 2) + k // 4][0:n, (k % 4) * P:(k % 4 + 1) * P],
                                                   x2T[:, k, i * P:i * P + n], ident[:, :])
                    last.then_inc(out_t, 1)

            @block.scalar
            def _(act):
                def high_up(g, f, fresh=False):
                    act.wait_ge(wu_in, 16 * (g + 1))
                    if not fresh:
                        act.wait_ge(up_done, NUP * (g - 1) + NT * (f + 1))
                    nc.scalar.activation(wuH[:, f, :, :], wu[:, :, f * P:(f + 1) * P], ACT.Copy).then_inc(wuH_ready, 1)

                def high_down(g, fresh=False):
                    act.wait_ge(wd_in, 16 * (g + 1))
                    if not fresh:
                        act.wait_ge(down_done, NDN * g)
                    nc.scalar.activation(wdH[:, :, :], wd[:, :, :], ACT.Copy).then_inc(wdH_ready, 1)

                def hidden(g, slot, f, fresh=False):
                    if not fresh:
                        act.wait_ge(hidL_ready, FG * (g - 1) + f + 1)
                    for third in range(NT):
                        act.wait_ge(up_done, NUP * g + NT * f + third + 1)
                        nc.scalar.activation(act2[:, f, third * TC:(third + 1) * TC], ps[third][:, 0:TC], ACT.Relu).then_inc(relu_done, 1)
                    nc.scalar.drain()
                    nc.scalar.activation(act2[:, f, :], act2[:, f, :], ACT.Square)
                    nc.scalar.drain()
                    nc.scalar.activation(hidH[:, slot, f, :], act2[:, f, :], ACT.Copy).then_inc(hidH_ready, 1)

                for f in range(FG):
                    high_up(0, f, fresh=True)
                high_down(0, fresh=True)
                for f in range(FG):
                    hidden(0, 0, f, fresh=True)
                    high_up(1, f)
                with act.Fori(0, NFG // 2 - 1) as it:
                    for slot in range(2):
                        g = 2 * it + slot
                        for f in range(FG):
                            hidden(g + 1, 1 - slot, f)
                            high_up(g + 2, f)
                        high_down(g + 1)
                for f in range(FG):
                    hidden(NFG - 1, 1, f)
                high_down(NFG - 1)
                act.wait_ge(hidL_ready, FG * NFG)
                for i in range(9):
                    n = P if i < 8 else NS
                    act.wait_ge(out_t, i + 1)
                    if i >= 2:
                        act.wait_ge(stored[i % 2], 16 * (i // 2))
                    nc.scalar.activation(ynat[0:n, i % 2, 0:512], ps[2 * (i % 2)][0:n, :], ACT.Copy).then_inc(out_a, 1)

            @block.vector
            def _(dve):
                def low_up(g, f):
                    dve.wait_ge(wuH_ready, FG * g + f + 1)
                    nc.vector.tensor_tensor(wuL[:, f, :, :], wu[:, :, f * P:(f + 1) * P], wuH[:, f, :, :].bitcast(F32),
                                            ALU.subtract).then_inc(wuL_ready, 1)

                def low_down(g):
                    dve.wait_ge(wdH_ready, g + 1)
                    nc.vector.tensor_tensor(wdL[:, :, :], wd[:, :, :], wdH[:, :, :].bitcast(F32), ALU.subtract).then_inc(wdL_ready, 1)

                def low_hidden(g, slot, f):
                    dve.wait_ge(hidH_ready, FG * g + f + 1)
                    nc.vector.tensor_tensor(hidL[:, slot, f, :], act2[:, f, :], hidH[:, slot, f, :].bitcast(F32),
                                            ALU.subtract).then_inc(hidL_ready, 1)

                def add_down(g):
                    for m in range(KD):
                        for third in range(NT):
                            n = m * NT + third
                            y = x2T[:, m, third * TC:(third + 1) * TC]
                            dve.wait_ge(down_done, NDN * g + n + 1)
                            nc.vector.tensor_tensor(y, ps[4 + n % 4][:, 0:TC], y, ALU.add).then_inc(added, 1)

                for f in range(FG):
                    low_up(0, f)
                low_down(0)
                for f in range(FG):
                    low_hidden(0, 0, f)
                    low_up(1, f)
                with dve.Fori(0, NFG // 2 - 1) as it:
                    for slot in range(2):
                        g = 2 * it + slot
                        for f in range(FG):
                            low_hidden(g + 1, 1 - slot, f)
                            low_up(g + 2, f)
                        add_down(g)
                        low_down(g + 1)
                for f in range(FG):
                    low_hidden(NFG - 1, 1, f)
                add_down(NFG - 2)
                low_down(NFG - 1)
                add_down(NFG - 1)
                for i in range(9):
                    n = P if i < 8 else NS
                    dve.wait_ge(out_t, i + 1)
                    if i >= 2:
                        dve.wait_ge(stored[i % 2], 16 * (i // 2))
                    nc.vector.tensor_copy(ynat[0:n, i % 2, 512:1024], ps[2 * (i % 2) + 1][0:n, :]).then_inc(out_b, 1)


_OUTS = [((1, 1024, 1024), 'float32'), ((8, 1, 1024), 'float32'), ((1, 1, 1024, 4, 2, 64), 'float32'),
         ((1, 8, 1, 4, 2, 64), 'float32'), ((1, 1, 512, 2, 2, 64), 'float32'), ((1, 8, 512, 2, 2, 64), 'float32'),
         ((1, 1, 4, 64, 64), 'float32'), ((1, 8, 4, 64, 64), 'float32'),
         ((1, 1, 4, 64, 64), 'float32'), ((1, 8, 4, 64, 64), 'float32'),
         ((1, 1, 4, 64), 'float32'), ((1, 8, 4, 64), 'float32'), ((1, 1, 4), 'float32'), ((1, 8, 4), 'float32'),
         ((1, 1, 3, 256), 'float32'), ((1, 8, 3, 256), 'float32')]


def program(nc, io):
    scratch = lambda n, s: nc.dram_tensor(f"{n}_scratch", s, F32, kind="Internal").ap()
    io["zT"] = scratch("zT", [IN_W, TT])
    io["zS"] = scratch("zS", [NS, IN_W])
    io["xT"] = scratch("xT", [D, TT])
    io["qkT"] = scratch("qkT", [6 * P, TT])
    with ExitStack() as ctx:
        sb = lambda n, s, d=F32: ctx.enter_context(nc.sbuf_tensor(n, s, d))
        keep = {"ident": sb("ident", [P, P]), "eps": sb("eps", [P, 1]), "ones": sb("ones", [P, P])}
        norm_and_project(nc, io, keep)
        keep.update({
            "g4": sb("g4", [P, 4]), "cbias": sb("cbias", [64, 2]), "w2": sb("w2", [64, 2, HD]), "b2": sb("b2", [64, 65]),
            "uact": sb("uact", [P, HP, TT]), "rows_cols": sb("rows_cols", [P, NCH, 16]),
            "hs": sb("hs", [P, NCH, 4, 65]),
            "mqk_dec": sb("mqk_dec", [P, 4, NS]), "decay_dec": sb("decay_dec", [P, HP, NS]),
            "mixS": sb("mixS", [P, KD, NS]),
        })
        keep["onat_flat"] = sb("onat", [P, KD * TT])
        keep["onat"] = keep["onat_flat"][:, 0:TQ * D].rearrange("p (i d) -> p i d", i=TQ)
        with ExitStack() as inner:
            sbi = lambda n, s, d=F32: inner.enter_context(nc.sbuf_tensor(n, s, d))
            keep.update({
                "decay": sbi("decay", [P, HP, T]), "mqk": sbi("mqk", [P, 4, TT]),
                "rows_nat": sbi("rows_nat", [P, 9, 768]), "gates_nat": sbi("gates_nat", [P, 9, 24]),
                "kcmpT": sbi("kcmpT", [64, 2, P]), "vcmp": sbi("vcmp", [P, 2, 64]),
                "v_nat": sbi("v_nat", [P, NCH, 512]), "mk_nat": sbi("mk_nat", [P, NCH, 256]), "rows": sbi("rows", [P, T]),
            })
            prepare_prompt(nc, io, keep)
            attend_prompt(nc, io, keep)
            recur_prompt(nc, io, keep)
        decode(nc, io, keep)
        x2T = keep["onat_flat"][:, :].rearrange("p (k t) -> p k t", k=KD)
        hH, hL = sb("hH", [P, KD, TT], F32R), sb("hL", [P, KD, TT], F32R)
        mix_and_project(nc, io, keep, x2T, hH, hL)
        channel_mixer(nc, io, keep, x2T, hH, hL)


def kernel(**inputs):
    import numpy as _np
    import concourse.bacc as _bacc
    from concourse import mybir as _mybir
    from concourse.bass_utils import run_bass_kernel_spmd as _run

    nc = _bacc.Bacc("TRN2", target_bir_lowering=False, num_devices=1)
    arrays, io = {}, {}
    for name in inputs:
        a = _np.ascontiguousarray(inputs[name])
        arrays[f"in_{name}_dram"] = a
        io[name] = nc.dram_tensor(f"in_{name}_dram", a.shape, _mybir.dt.from_np(a.dtype), kind="ExternalInput").ap()
    for i, (shape, dtype) in enumerate(_OUTS):
        dt = _mybir.dt.from_np(_np.dtype(dtype))
        io[f"out{i}"] = nc.dram_tensor(f"out_{i}_dram", shape, dt, kind="ExternalOutput").ap()
    with nc.allow_non_contiguous_dma(reason="short vectors and columns"):
        program(nc, io)
    r = _run(nc, [arrays], core_ids=[0])
    return tuple(r.results[0][f"out_{i}_dram"] for i in range(len(_OUTS)))
```
